# Optimizing a Trainium2 kernel written in Bass

```python
import jax, jax.numpy as jnp
from jax import lax
import numpy as np

D_MODEL = 1024
BATCH = 1
SEQ = 512
DEPTH = 1

GDN_HEADS = 4
GDN_HEAD_DIM = 128
GDN_WIDTH = GDN_HEADS * GDN_HEAD_DIM
GDN_CONV = 4
GDN_CHUNK = 64
SC_GROUPS = 4
SC_WIDTH = 512
SC_CONV = 3
FOX_HEADS = 4
FOX_HEAD_DIM = 128
FOX_WIDTH = FOX_HEADS * FOX_HEAD_DIM
FOX_BLOCK = 128
N_BRANCH = 3
D_FF = 2816
FFN_CONV = 3
EPS = 1e-6

SPLIT_SIZES = (3 * GDN_WIDTH, GDN_WIDTH, GDN_HEADS, GDN_HEADS,
               3 * SC_WIDTH, 3 * FOX_WIDTH, FOX_HEADS, N_BRANCH * D_MODEL)
PROJ_WIDTH = 3 * GDN_WIDTH + GDN_WIDTH + 2 * GDN_HEADS + 3 * SC_WIDTH + 3 * FOX_WIDTH + FOX_HEADS + N_BRANCH * D_MODEL

kernel_name = "hybrid_gdn_shortconv_fox_convffn"

def rmsnorm(x, g):
    xf = x.astype(jnp.float32)
    y = xf * lax.rsqrt(jnp.mean(xf * xf, axis=-1, keepdims=True) + EPS)
    return (y * g.astype(jnp.float32)).astype(x.dtype)

def l2norm(x):
    xf = x.astype(jnp.float32)
    return xf * lax.rsqrt(jnp.sum(xf * xf, axis=-1, keepdims=True) + EPS)

def causal_dwconv(x, w):
    K, C = w.shape
    return lax.conv_general_dilated(
        x, w[:, None, :].astype(x.dtype), window_strides=(1,), padding=[(K - 1, 0)],
        dimension_numbers=('NWC', 'WIO', 'NWC'), feature_group_count=C)

def split_cols(p):
    pts, acc = [], 0
    for s in SPLIT_SIZES[:-1]:
        acc += s
        pts.append(acc)
    return jnp.split(p, pts, axis=-1)

def gated_delta_rule(q, k, v, g, beta):
    out_dtype = v.dtype
    B, T, H, dk = q.shape
    dv = v.shape[-1]
    C = GDN_CHUNK
    N = T // C
    f32 = jnp.float32

    def chunks(t):
        return t.astype(f32).reshape(B, N, C, H, -1).transpose(0, 3, 1, 2, 4)

    q = chunks(q) * (dk ** -0.5)
    k = chunks(k)
    v = chunks(v)
    beta_c = beta.astype(f32).reshape(B, N, C, H).transpose(0, 3, 1, 2)[..., None]
    gc = jnp.cumsum(g.astype(f32).reshape(B, N, C, H).transpose(0, 3, 1, 2), axis=-1)
    kb = k * beta_c
    vb = v * beta_c

    tril = jnp.tril(jnp.ones((C, C), dtype=bool))
    strict = jnp.tril(jnp.ones((C, C), dtype=bool), -1)
    decay = jnp.exp(jnp.where(tril, gc[..., :, None] - gc[..., None, :], -jnp.inf))

    L = jnp.where(strict, jnp.einsum('bhncd,bhnsd->bhncs', kb, k) * decay, 0.0)
    eye = jnp.eye(C, dtype=f32)
    Tm = lax.linalg.triangular_solve(eye + L, jnp.broadcast_to(eye, L.shape),
                                     left_side=True, lower=True)
    u = jnp.einsum('bhncs,bhnse->bhnce', Tm, vb)
    w = jnp.einsum('bhncs,bhnsd->bhncd', Tm, kb * jnp.exp(gc)[..., None])
    attn = jnp.einsum('bhncd,bhnsd->bhncs', q, k) * decay

    def step(S, xs):
        q_i, k_i, u_i, w_i, g_i, a_i = xs
        v_new = u_i - jnp.einsum('bhcd,bhde->bhce', w_i, S)
        o_i = (jnp.einsum('bhcd,bhde->bhce', q_i * jnp.exp(g_i)[..., None], S)
               + jnp.einsum('bhcs,bhse->bhce', a_i, v_new))
        g_last = g_i[..., -1]
        S = (S * jnp.exp(g_last)[..., None, None]
             + jnp.einsum('bhcd,bhce->bhde', k_i * jnp.exp(g_last[..., None] - g_i)[..., None], v_new))
        return S, o_i

    mv = lambda t: jnp.moveaxis(t, 2, 0)
    S0 = jnp.zeros((B, H, dk, dv), f32)
    _, o = lax.scan(step, S0, (mv(q), mv(k), mv(u), mv(w), mv(gc), mv(attn)))
    return o.transpose(1, 0, 3, 2, 4).reshape(B, T, H, dv).astype(out_dtype)

def forgetting_attention(q, k, v, logf):
    B, T, H, d = q.shape
    scale = d ** -0.5
    c = jnp.cumsum(logf.astype(jnp.float32), axis=1).transpose(0, 2, 1)
    outs = []
    for i in range(T // FOX_BLOCK):
        s0, e = i * FOX_BLOCK, (i + 1) * FOX_BLOCK
        logits = jnp.einsum('bqhd,bkhd->bhqk', q[:, s0:e], k[:, :e]).astype(jnp.float32) * scale
        logits = logits + c[:, :, s0:e, None] - c[:, :, None, :e]
        causal = (s0 + jnp.arange(FOX_BLOCK))[:, None] >= jnp.arange(e)[None, :]
        p = jax.nn.softmax(jnp.where(causal, logits, -jnp.inf), axis=-1)
        outs.append(jnp.einsum('bhqk,bkhd->bqhd', p.astype(v.dtype), v[:, :e]))
    return jnp.concatenate(outs, axis=1)

def hybrid_mixer(xn, w_in, conv_qkv, a_log, dt_bias, gdn_norm, w_br_a,
                 conv_sc, w_br_b, fox_bias, w_br_c, w_o):
    B, T, _ = xn.shape
    proj = xn @ w_in
    qkv_a, z_a, beta_logit, a_logit, bch, qkv_c, f_logit, gate_logits = split_cols(proj)

    qkv_a = jax.nn.silu(causal_dwconv(qkv_a, conv_qkv))
    qa, ka, va = jnp.split(qkv_a, 3, axis=-1)
    hd = (B, T, GDN_HEADS, GDN_HEAD_DIM)
    qa, ka, va = l2norm(qa.reshape(hd)), l2norm(ka.reshape(hd)), va.reshape(hd)
    beta = jax.nn.sigmoid(beta_logit.astype(jnp.float32))
    g = -jnp.exp(a_log.astype(jnp.float32)) * jax.nn.softplus(
        a_logit.astype(jnp.float32) + dt_bias.astype(jnp.float32))
    oa = gated_delta_rule(qa, ka, va, g, beta)
    oa = rmsnorm(oa, gdn_norm) * jax.nn.silu(z_a.reshape(hd))
    ya = oa.reshape(B, T, GDN_WIDTH) @ w_br_a

    b_gate, c_gate, h = jnp.split(bch, 3, axis=-1)
    yb = (b_gate * causal_dwconv(c_gate * h, conv_sc)) @ w_br_b

    qc, kc, vc = jnp.split(qkv_c, 3, axis=-1)
    fd = (B, T, FOX_HEADS, FOX_HEAD_DIM)
    logf = jax.nn.log_sigmoid(f_logit.astype(jnp.float32) + fox_bias.astype(jnp.float32))
    oc = forgetting_attention(qc.reshape(fd), kc.reshape(fd), vc.reshape(fd), logf)
    yc = oc.reshape(B, T, FOX_WIDTH) @ w_br_c

    ga, gb, gcg = jnp.split(jax.nn.sigmoid(gate_logits), 3, axis=-1)
    return (ga * ya + gb * yb + gcg * yc) @ w_o

def conv_glu_ffn(xn, w_up, conv_ffn, w_down):
    h = causal_dwconv(xn @ w_up, conv_ffn)
    gate, up = jnp.split(h, 2, axis=-1)
    return (jax.nn.silu(gate) * up) @ w_down

def setup_inputs(seed: int = 0) -> dict:
    key = jax.random.key(seed)
    ks = jax.random.split(key, 20)
    L, D = DEPTH, D_MODEL
    nrm = lambda k, shape, fan: jax.random.normal(k, shape, jnp.float32) * (fan ** -0.5)
    gain = lambda k, shape: 1.0 + 0.02 * jax.random.normal(k, shape, jnp.float32)
    dt = jnp.exp(jax.random.uniform(ks[4], (L, GDN_HEADS), jnp.float32,
                                    float(np.log(1e-3)), float(np.log(1e-1))))
    return {
        "x": jax.random.normal(ks[0], (BATCH, SEQ, D), jnp.float32),
        "norm1_g": gain(ks[1], (L, D)),
        "w_in": nrm(ks[2], (L, D, PROJ_WIDTH), D),
        "conv_qkv": nrm(ks[3], (L, GDN_CONV, 3 * GDN_WIDTH), GDN_CONV),
        "a_log": jnp.log(jax.random.uniform(ks[5], (L, GDN_HEADS), jnp.float32, 1.0, 16.0)),
        "dt_bias": dt + jnp.log(-jnp.expm1(-dt)),
        "gdn_norm": gain(ks[6], (L, GDN_HEAD_DIM)),
        "w_br_a": nrm(ks[7], (L, GDN_WIDTH, D), GDN_WIDTH),
        "conv_sc": nrm(ks[8], (L, SC_CONV, SC_WIDTH), SC_CONV),
        "w_br_b": nrm(ks[9], (L, SC_WIDTH, D), SC_WIDTH),
        "fox_bias": 2.0 + 0.1 * jax.random.normal(ks[10], (L, FOX_HEADS), jnp.float32),
        "w_br_c": nrm(ks[11], (L, FOX_WIDTH, D), FOX_WIDTH),
        "w_o": nrm(ks[12], (L, D, D), D),
        "norm2_g": gain(ks[13], (L, D)),
        "w_up": nrm(ks[14], (L, D, 2 * D_FF), D),
        "conv_ffn": nrm(ks[15], (L, FFN_CONV, 2 * D_FF), FFN_CONV),
        "w_down": nrm(ks[16], (L, D_FF, D), D_FF),
        "norm_f": gain(ks[17], (D,)),
    }

def reference(x, norm1_g, w_in, conv_qkv, a_log, dt_bias, gdn_norm, w_br_a,
              conv_sc, w_br_b, fox_bias, w_br_c, w_o, norm2_g, w_up, conv_ffn,
              w_down, norm_f):
    h = x
    for l in range(DEPTH):
        h = h + hybrid_mixer(rmsnorm(h, norm1_g[l]), w_in[l], conv_qkv[l], a_log[l], dt_bias[l],
                             gdn_norm[l], w_br_a[l], conv_sc[l], w_br_b[l], fox_bias[l],
                             w_br_c[l], w_o[l])
        h = h + conv_glu_ffn(rmsnorm(h, norm2_g[l]), w_up[l], conv_ffn[l], w_down[l])
    return rmsnorm(h, norm_f)


_drawn_inputs = setup_inputs


def setup_inputs(seed=0):
    import zlib

    import numpy as np

    out = dict(_drawn_inputs(seed))
    spreads = {}
    factors = {'a_log': 2.762, 'gdn_norm': 8.0, 'fox_bias': 49.48, 'norm2_g': 4.096, 'norm_f': 8.217}
    for name, (base, spread) in spreads.items():
        noise = np.random.default_rng([zlib.crc32(name.encode()), seed]).standard_normal(out[name].shape)
        drawn = base * np.exp(spread * noise) if base else spread * noise
        out[name] = __import__('jax').numpy.asarray(drawn.astype(out[name].dtype))
    for name, factor in factors.items():
        out[name] = (out[name] * factor).astype(out[name].dtype)
    return out
```

```python
from contextlib import ExitStack

import numpy as np

import concourse.bass as bass
from concourse import mybir

ALU = mybir.AluOpType
ACT = mybir.ActivationFunctionType
F32 = mybir.dt.float32
F32R = mybir.dt.float32r
I32 = mybir.dt.int32
AX_X = mybir.AxisListType.X

P = 128
D = 1024
T = 512
KT = D // P
NT = T // P
H = 4
HD = 128
FF = 2816
KF = FF // P
EPS = 1e-6
NLEV = 7
NEG = -1.0e30

U_QK = 0
U_V = U_QK + 2 * H
U_MIX = U_V + H
U_Z = U_MIX + 6 * H
U_BR = U_Z + H
U_O = U_BR + 6 * KT
U_UP = U_O + KT
U_DN = U_UP + 2 * KF
KDN = (8, 8, KF - 16)

C_ID, C_ONE, C_TRI, C_NEGT, C_CAUSAL, C_LEV = 0, 1, 2, 3, 4, 5
NCONST = C_LEV + NLEV

PRM = {}
_at = 0
for _n, _w in (("g1", KT), ("g2", KT), ("gf", KT), ("conv_qkv", 3 * H * 4), ("conv_sc", H * 3),
               ("conv_ffn", KF * 2 * 3), ("gdn_norm", 1), ("a_log", H), ("dt_bias", H), ("fox_bias", H)):
    PRM[_n] = slice(_at, _at + _w)
    _at += _w
NPRM = _at

Q_G, Q_BRK, Q_RQ, Q_RK, Q_GC, Q_NBE, Q_HB = range(7)


def build(nc, xT, consts, params, w_small, w_qkv, w_mix, w_z, w_gate, w_br, w_o, w_up, w_dn, outT):
    ctx = ExitStack()
    with ctx:
        def sb(name, shape, dt=F32, scope=ctx):
            return scope.enter_context(nc.sbuf_tensor(name, shape, dt))

        def bank(name):
            return ctx.enter_context(nc.psum_tensor(name, [P, 512], F32))

        def sem(name):
            return ctx.enter_context(nc.semaphore(name))

        cst = sb("cst", [P, NCONST, P])
        prm = sb("prm", [P, NPRM])
        raw = [sb(f"raw{s}", [P, KT * P]) for s in range(2)]
        w_h = [sb(f"w_h{s}", [P, KT * P], F32R) for s in range(2)]
        w_l = [sb(f"w_l{s}", [P, KT * P], F32R) for s in range(2)]
        xn_h = sb("xn_h", [P, KT, T], F32R)
        xn_l = sb("xn_l", [P, KT, T], F32R)
        ws_raw = sb("ws_raw", [P, KT * 12])
        ws_h = sb("ws_h", [P, KT * 12], F32R)
        ws_l = sb("ws_l", [P, KT * 12], F32R)
        col = sb("col", [P, 8, NT])
        diag = sb("diag", [P, NT, P])
        sqsum = sb("sqsum", [P, T])
        sq2 = sb("sq2", [P, T])
        ident = cst[:, C_ID, :]
        ones = cst[:, C_ONE, :]

        s_br = ExitStack()
        ogd = sb("ogd", [P, H, T], F32, s_br)
        sc_h = sb("sc_h", [P, H, T], F32R, s_br)
        sc_l = sb("sc_l", [P, H, T], F32R, s_br)
        fx_h = sb("fx_h", [P, H, T], F32R, s_br)
        fx_l = sb("fx_l", [P, H, T], F32R, s_br)

        s_x = ExitStack()
        x_in = sb("x_in", [P, KT, T], F32, s_x)
        x_sq = sb("x_sq", [P, KT, T], F32, s_x)
        s_x.close()

        s_mix = ExitStack()
        qkv = sb("qkv", [P, 3 * H, T], F32, s_mix)
        lg = sb("lg", [P, NT, 12], F32, s_mix)
        spu = sb("spu", [P, 8, NT, 2 * H], F32, s_mix)
        ea = sb("ea", [P, H], F32, s_mix)
        bet = sb("bet", [P, 3, NT, H], F32, s_mix)
        g16 = sb("g16", [P, NT, H], F32, s_mix)
        ec16 = sb("ec16", [P, NT, H], F32, s_mix)
        nrm = sb("nrm", [P, 3, 2, NT, H], F32, s_mix)
        gcols = sb("gcols", [P, NT, 7, H], F32, s_mix)
        fcols = sb("fcols", [P, H, 8], F32, s_mix)
        s_qkv = ExitStack()
        sq = sb("sq", [P, 2 * H, T], F32, s_qkv)
        cy = [sb(f"cy{s}", [P, T], F32, s_qkv) for s in range(2)]
        th = [sb(f"th{s}", [P, T], F32, s_qkv) for s in range(2)]
        tap4 = sb("tap4", [P, H, 4], F32, s_qkv)
        s_qkv.close()
        gcs = sb("gcs", [P, 7, H], F32, s_mix)
        kd = sb("kd", [P, 3, H], F32, s_mix)
        stg = sb("stg", [P, 3 * H, P], F32, s_mix)
        kb = sb("kb", [P, H, P], F32, s_mix)
        qh = sb("qh", [P, H, P], F32, s_mix)
        erow = sb("erow", [P, H, P], F32, s_mix)
        dec = sb("dec", [P, H, P], F32, s_mix)
        lt = sb("lt", [P, H, P], F32, s_mix)
        at = sb("at", [P, H, P], F32, s_mix)
        olev = [sb(f"olev{s}", [P, H, P], F32, s_mix) for s in range(2)]
        xi = sb("xi", [P, H, P], F32, s_mix)
        xt = sb("xt", [P, H, P], F32, s_mix)
        zlev = [None] + [sb(f"zlev{s}", [P, H, P], F32, s_mix) for s in range(1, NLEV)]
        ktok = sb("ktok", [P, H, P], F32, s_mix)
        vb = sb("vb", [P, H, P], F32, s_mix)
        vn = sb("vn", [P, H, P], F32, s_mix)
        state = sb("state", [P, H, P], F32, s_mix)
        fq = sb("fq", [P, T], F32, s_mix)
        fk = sb("fk", [P, T], F32, s_mix)
        fv = sb("fv", [P, T], F32, s_mix)
        fvt = sb("fvt", [P, NT, P], F32, s_mix)
        fcs = sb("fcs", [P, 8], F32, s_mix)
        fcum = sb("fcum", [P, NT, P], F32, s_mix)
        pr = [sb(f"pr{s}", [P, T], F32, s_mix) for s in range(2)]
        pt = sb("pt", [P, NT, P], F32, s_mix)
        fst = sb("fst", [P, 4, NT], F32, s_mix)
        cs = sb("cs", [P, T], F32, s_mix)
        us = sb("us", [P, T], F32, s_mix)
        tap3 = sb("tap3", [P, 3], F32, s_mix)
        s_mix.close()

        s_bp = ExitStack()
        zg = sb("zg", [P, H, T], F32, s_bp)
        oa_h = sb("oa_h", [P, H, T], F32R, s_bp)
        oa_l = sb("oa_l", [P, H, T], F32R, s_bp)
        osq = sb("osq", [P, H, T], F32, s_bp)
        gn_half = sb("gn_half", [P, 1], F32, s_bp)
        onrm = sb("onrm", [P, 4, H, NT], F32, s_bp)
        zt = [sb(f"zt{s}", [P, T], F32, s_bp) for s in range(2)]
        tg = sb("tg", [P, T], F32, s_bp)
        mg = sb("mg", [P, T], F32, s_bp)
        mg2 = sb("mg2", [P, T], F32, s_bp)
        mg_h = sb("mg_h", [P, KT, T], F32R, s_bp)
        mg_l = sb("mg_l", [P, KT, T], F32R, s_bp)
        x_res = sb("x_res", [P, KT, T], F32, s_bp)
        s_bp.close()
        s_br.close()

        res = sb("res", [P, KT, T])
        ff_h = sb("ff_h", [P, KF, T], F32R)
        ff_l = sb("ff_l", [P, KF, T], F32R)
        yc = [sb(f"yc{s}", [P, T]) for s in range(4)]
        yt = [sb(f"yt{s}", [P, T]) for s in range(2)]
        hv = [sb(f"hv{s}", [P, T]) for s in range(2)]
        tapf = sb("tapf", [P, 4, 3])

        acc = [bank(f"acc{s}") for s in range(2)]
        gb = [bank(f"gb{s}") for s in range(3)]
        fb = [bank(f"fb{s}") for s in range(3)]

        raw_in = [sem(f"raw_in{s}") for s in range(2)]
        hi_done = sem("hi_done")
        lo_done = sem("lo_done")
        unit_done = sem("unit_done")
        acc_free = [sem(f"acc_free{b}") for b in range(2)]
        sig = {n: sem(n) for n in """
            abs_ok at_ok colu_ok colx cst_in cum_done cum_mm dec_ok diag_ok ds_mm ea_ok eb_done erow_ok exp_ok
            f_h f_hv f_l f_sg f_tap fc1_ok fc_ok fth_ok fvt_mm fvt_ok fxh_ok fxl_ok fy_tap gc_mm gcc_ok gcols_ok
            kb_ok kd0_ok kd1_ok kdx_ok kk_mm ks_mm ktok_ok kvt_mm lgt_ok lt_ok m2_ok mgh_ok mgl_ok msk_ok mx_ok
            nf_done nh_done nl_done nmx_ok o_mm o_ok oa1_ok oa2_ok oah_ok oal_ok odiag_ok olev_ok orow_mm osq_ok
            ostat_mm ot0_ok out_ok out_st pn_ok prep_ok prm_in pt_mm pt_ok pv_mm q_done qc_ok qe_ok qh_ok
            qt_done qth_ok qy_tap r_ok ri_ok rown_mm rows_mm rsq_ok rss_ok rstat_mm s_mm scc_ok sch_ok scl_ok
            sct_ok small_mm sq_done st_ok stage_ok stat_mm v_chain vb_ok vn_mm vn_ok ws_in wsh_done wsl_done
            xi0_ok xi_ok xres_in xsq_done xstat_mm xt0_ok xt_ok xtr_mm xz_mm z_mm z_ok zer_ok zth_ok""".split()}
        xin = [sem(f"xin{c}") for c in range(4)]


        block = ctx.enter_context(nc.Block())

        def heads(ap):
            return ap.unsqueeze(2).broadcast_to([P, ap.shape[1], P])

        def tiles(ap, n=H):
            return ap.unsqueeze(1).broadcast_to([P, n, P])

        def four(b):
            return b[:, :].rearrange("p (h c) -> p h c", h=H)

        def half(ap, lev, up):
            v = ap.rearrange("p h (g two b) -> p (h g) two b", two=2, b=1 << lev)
            return v[:, :, up, :]

        def half1(ap, lev, up):
            v = ap.rearrange("p (g two b) -> p g two b", two=2, b=1 << lev)
            return v[:, :, up, :]

        def packed(b, lev):
            return b[:, 0:H * 64].rearrange("p (g b) -> p g b", b=1 << lev)

        def evacuated(eng, base, per, i, p):
            eng.wait_ge(acc_free[p % 2], per // 2 * i + ((base + p) // 2 + 2))

        @block.sync
        def _(sp):
            def fetch(slot, src, kt):
                sp.dma_start(raw[slot][:, 0:kt * P], src).then_inc(raw_in[slot], 16)

            xv = xT.rearrange("(c k p) t -> c p k t", c=4, p=P)
            for c in range(4):
                sp.dma_start(x_in[:, 2 * c:2 * c + 2, :], xv[c]).then_inc(xin[c], 16)
            sp.dma_start(cst[:, :, :], consts.rearrange("p (n c) -> p n c", c=P)).then_inc(sig["cst_in"], 16)
            sp.dma_start(prm[:, :], params).then_inc(sig["prm_in"], 16)
            sp.dma_start(ws_raw[:, :], w_small).then_inc(sig["ws_in"], 16)
            for u in range(2):
                fetch(u, w_qkv[u], KT)
            with sp.Fori(1, 6) as i:
                for p in range(2):
                    sp.wait_ge(lo_done, 2 * i + p - 1)
                    fetch(p, w_qkv[2 * i + p], KT)
            with sp.Fori(0, 12) as i:
                for p in range(2):
                    sp.wait_ge(lo_done, 2 * i + (U_MIX + p - 1))
                    fetch(p, w_mix[2 * i + p], KT)
            for i in range(H):
                sp.wait_ge(lo_done, U_Z + i - 1)
                fetch(i % 2, w_z[i], KT)
            sp.wait_ge(sig["fxl_ok"], H + 1)
            sp.wait_ge(sig["scl_ok"], H)
            sp.wait_ge(sig["st_ok"], H + 1)
            sp.dma_start(x_res[:, :, :], xT.rearrange("(k p) t -> p k t", p=P)).then_inc(sig["xres_in"], 16)
            with sp.Fori(0, KT) as i:
                for p in range(3):
                    sp.wait_ge(lo_done, 6 * i + (U_BR + 2 * p - 1))
                    fetch(0, w_gate[3 * i + p], KT)
                    sp.wait_ge(lo_done, 6 * i + (U_BR + 2 * p))
                    fetch(1, w_br[3 * i + p], H)
            with sp.Fori(0, KT // 2) as i:
                for p in range(2):
                    sp.wait_ge(lo_done, 2 * i + (U_O + p - 1))
                    fetch(p, w_o[2 * i + p], KT)
            with sp.Fori(0, KF) as i:
                for p in range(2):
                    sp.wait_ge(lo_done, 2 * i + (U_UP + p - 1))
                    fetch(p, w_up[2 * i + p], KT)
            with sp.Fori(0, KT // 2) as i:
                for p in range(6):
                    k0 = 8 * (p % 3)
                    sp.wait_ge(lo_done, 6 * i + (U_DN + p - 1))
                    fetch(p % 2, w_dn[2 * i + p // 3][:, k0 * P:(k0 + KDN[p % 3]) * P], KDN[p % 3])
            for k in range(KT):
                sp.wait_ge(sig["out_ok"], k + 1)
                sp.dma_start(outT[k * P:(k + 1) * P, :], res[:, k, :]).then_inc(sig["out_st"], 16)
            sp.wait_ge(sig["out_st"], 16 * KT)

        @block.tensor
        def _(pe):
            def passes(out, wh, wl, xh, xl, start, stop):
                pe.matmul(out, wh, xh, start=start, stop=False)
                pe.matmul(out, wh, xl, start=False, stop=False)
                return pe.matmul(out, wl, xh, start=False, stop=stop)

            def unit(base, per, i, p, xh, xl, kt, k0=0, bnk=None, start=True, stop=True, gaps=None, k_wait=None):
                slot, u = p % 2, per * i + (base + p)
                out = acc[slot if bnk is None else bnk][:, :]
                for k in range(kt):
                    if gaps and k % 2 == 0:
                        gaps(k // 2)
                    if k == 0:
                        pe.wait_ge(lo_done, u + 1)
                        if start and bnk is None:
                            pe.wait_ge(acc_free[slot], per // 2 * i + ((base + p) // 2 + 1))
                    if k_wait:
                        k_wait(k)
                    wk = slice(k * P, (k + 1) * P)
                    mm = passes(out, w_h[slot][:, wk], w_l[slot][:, wk], xh[:, k0 + k, :], xl[:, k0 + k, :],
                                start and k == 0, stop and k == kt - 1)
                mm.then_inc(unit_done, 1)

            def column_sums(out, sqt, n):
                for j in range(n):
                    mm = pe.matmul(out[:, j:j + 1], sqt(j), ones[:, 0:1], start=True, stop=True)
                return mm

            pe.wait_ge(sig["cst_in"], 16)
            for k in range(KT):
                if k % 2 == 0:
                    pe.wait_ge(sig["xsq_done"], k // 2 + 1)
                for t in range(NT):
                    mm = pe.matmul(fb[0][:, t:t + 1], x_sq[:, k, t * P:(t + 1) * P], ones[:, 0:1],
                                   start=(k == 0 and t == 0), stop=(k == KT - 1), skip_group_check=True)
            mm.then_inc(sig["xstat_mm"], 1)
            pe.wait_ge(sig["diag_ok"], 1)
            pe.matmul(fb[1][:, :], ones, diag[:, :, :], start=True, stop=True).then_inc(sig["rown_mm"], 1)

            def xn_ready(k):
                pe.wait_ge(sig["nl_done"], k + 1)

            with pe.Fori(0, 2) as i:
                for p in range(H):
                    unit(U_QK, 4, i, p, xn_h, xn_l, KT, k_wait=xn_ready if p == 0 else None)
            pe.wait_ge(sig["wsl_done"], 1)
            for t in range(NT):
                for k in range(KT):
                    ts, ws = slice(t * P, (t + 1) * P), slice(12 * k, 12 * k + 12)
                    o = fb[2][:, 12 * t:12 * t + 12]
                    pe.matmul(o, xn_h[:, k, ts], ws_h[:, ws], start=(k == 0), stop=False)
                    pe.matmul(o, xn_h[:, k, ts], ws_l[:, ws], start=False, stop=False)
                    mm = pe.matmul(o, xn_l[:, k, ts], ws_h[:, ws], start=False, stop=(k == KT - 1))
            mm.then_inc(sig["small_mm"], 1)

            def v_gap(p):
                def gap(q):
                    if p == 0 and q == 3:
                        pe.wait_ge(sig["sq_done"], 2 * H)
                        column_sums(fb[0][:, 0:32],
                                    lambda j: sq[:, 4 * (j // 16) + j % 4, P * (j // 4 % 4):P * (j // 4 % 4) + P],
                                    32).then_inc(sig["stat_mm"], 1)
                    if p == 3 and q == 3:
                        pe.wait_ge(sig["colx"], 1)
                        pe.matmul(fb[1][:, 0:16], cst[:, C_TRI, :], g16[:, :, :], start=True, stop=True)\
                          .then_inc(sig["gc_mm"], 1)
                return gap

            for p in range(H):
                unit(U_V, 4, 0, p, xn_h, xn_l, KT, gaps=v_gap(p))

            def rows(i):
                pe.wait_ge(sig["prep_ok"], i + 1)
                pe.wait_ge(sig["st_ok"], i + 1)
                pe.wait_ge(sig["o_ok"], i + 1)
                pe.matmul(gb[0][:, :], ones, dec[:, :, :], start=True, stop=True)
                pe.matmul(gb[1][:, :], ones, kb[:, :, :], start=True, stop=True)
                pe.matmul(gb[2][:, :], ones, qh[:, :, :], start=True, stop=True).then_inc(sig["rows_mm"], 1)

            def kv_turn(i):
                for h in range(H):
                    pe.transpose(fb[0][:, h * P:(h + 1) * P], stg[:, H + h, :], ident)
                for h in range(H):
                    mm = pe.transpose(fb[1][:, h * P:(h + 1) * P], stg[:, 2 * H + h, :], ident)
                mm.then_inc(sig["kvt_mm"], 1)

            def cum_row(i):
                pe.wait_ge(sig["fxl_ok"], i + 1)
                pe.matmul(fb[2][:, :], ones, fcum[:, :, :], start=True, stop=True).then_inc(sig["cum_mm"], 1)

            def kk(i):
                pe.wait_ge(sig["kb_ok"], i + 1)
                pe.wait_ge(sig["qh_ok"], i + 1)
                for h in range(H):
                    pe.matmul(gb[1][:, h * P:(h + 1) * P], stg[:, H + h, :], kb[:, h, :], start=True, stop=True)
                for h in range(H):
                    mm = pe.matmul(gb[2][:, h * P:(h + 1) * P], stg[:, H + h, :], qh[:, h, :], start=True, stop=True)
                mm.then_inc(sig["kk_mm"], 1)

            def k_state(i):
                pe.wait_ge(sig["cum_done"], i + 1)
                for h in range(H):
                    mm = pe.matmul(fb[2][:, h * P:(h + 1) * P], stg[:, H + h, :], state[:, h, :], start=True, stop=True)
                mm.then_inc(sig["ks_mm"], 1)

            def x_turn(i):
                pe.wait_ge(sig["xt0_ok"], i + 1)
                pe.wait_ge(sig["erow_ok"], i + 1)
                for h in range(H):
                    mm = pe.transpose(gb[0][:, h * P:(h + 1) * P], xt[:, h, :], ident)
                mm.then_inc(sig["xtr_mm"], 1)

            def lev_z(lev):
                def go(i):
                    pe.wait_ge(sig["olev_ok"], 6 * i + lev)
                    if lev == 1:
                        pe.wait_ge(sig["xi0_ok"], i + 1)
                    else:
                        pe.wait_ge(sig["xi_ok"], 5 * i + lev - 1)
                    for h in range(H):
                        mm = pe.matmul(gb[0][:, 64 * h:64 * h + 64], olev[lev % 2][:, h, :], half1(xi[:, h, :], lev, 0),
                                       start=True, stop=True)
                    mm.then_inc(sig["z_mm"], 1)
                return go

            def lev_xz(lev):
                def go(i):
                    pe.wait_ge(sig["z_ok"], 6 * i + lev)
                    if lev == 1:
                        pe.wait_ge(sig["at_ok"], i + 1)
                    else:
                        pe.wait_ge(sig["xt_ok"], 6 * i + lev - 1)
                    if lev < NLEV - 1:
                        for h in range(H):
                            pe.matmul(gb[1][:, 64 * h:64 * h + 64], xt[:, h, :], half1(zlev[lev][:, h, :], lev, 0),
                                      start=True, stop=True)
                    for h in range(H):
                        mm = pe.matmul(gb[2][:, 64 * h:64 * h + 64], zlev[lev][:, h, :], half1(xt[:, h, :], lev, 1),
                                       start=True, stop=True)
                    mm.then_inc(sig["xz_mm"], 1)
                return go

            def v_new(i):
                pe.wait_ge(sig["xt_ok"], 6 * i + 6)
                pe.wait_ge(sig["r_ok"], i + 1)
                for h in range(H):
                    mm = pe.matmul(gb[1][:, h * P:(h + 1) * P], xt[:, h, :], vb[:, h, :], start=True, stop=True)
                mm.then_inc(sig["vn_mm"], 1)

            def out_state(i):
                pe.wait_ge(sig["vn_ok"], i + 1)
                pe.wait_ge(sig["qe_ok"], i + 1)
                pe.wait_ge(sig["ktok_ok"], i + 1)
                for h in range(H):
                    o = gb[2][:, h * P:(h + 1) * P]
                    pe.matmul(o, state[:, h, :], erow[:, h, :], start=True, stop=False)
                    mm = pe.matmul(o, vn[:, h, :], at[:, h, :], start=False, stop=True)
                mm.then_inc(sig["o_mm"], 1)
                for h in range(H):
                    mm = pe.matmul(gb[0][:, h * P:(h + 1) * P], ktok[:, h, :], vn[:, h, :], start=True, stop=True)
                mm.then_inc(sig["ds_mm"], 1)

            def fv_turn(i):
                evacuated(pe, U_MIX, 6, i, 2)
                pe.wait_ge(sig["vb_ok"], i + 1)
                for t in range(NT):
                    mm = pe.transpose(fb[1][:, t * P:(t + 1) * P], fv[:, t * P:(t + 1) * P], ident)
                mm.then_inc(sig["fvt_mm"], 1)

            def scores(t):
                def go(i):
                    if t == 0:
                        evacuated(pe, U_MIX, 6, i, 1)
                        evacuated(pe, U_MIX, 6, i, 0)
                        pe.wait_ge(sig["ktok_ok"], i + 1)
                    else:
                        pe.wait_ge(sig["lgt_ok"], 4 * i + t)
                    pe.matmul(fb[0][:, 0:(t + 1) * P], fq[:, t * P:(t + 1) * P], fk[:, 0:(t + 1) * P],
                              start=True, stop=True).then_inc(sig["s_mm"], 1)
                return go

            def p_turn(t):
                def go(i):
                    pe.wait_ge(sig["pn_ok"], 4 * i + t + 1)
                    if t == 0:
                        pe.wait_ge(sig["fvt_ok"], i + 1)
                    else:
                        pe.wait_ge(sig["pt_ok"], 4 * i + t)
                    for j in range(t + 1):
                        mm = pe.transpose(fb[1][:, j * P:(j + 1) * P], pr[t % 2][:, j * P:(j + 1) * P], ident)
                    mm.then_inc(sig["pt_mm"], 1)
                return go

            def p_v(t):
                def go(i):
                    pe.wait_ge(sig["pt_ok"], 4 * i + t + 1)
                    if t == 0:
                        pe.wait_ge(sig["r_ok"], i + 1)
                    for j in range(t + 1):
                        mm = pe.matmul(fb[2][:, t * P:(t + 1) * P], fvt[:, j, :], pt[:, j, :],
                                       start=(j == 0), stop=(j == t))
                    mm.then_inc(sig["pv_mm"], 1)
                return go

            mixer = {
                0: [rows], 1: [kv_turn], 2: [cum_row], 3: [kk], 4: [k_state], 5: [x_turn],
                13: [scores(0)], 14: [fv_turn], 15: [scores(1)], 16: [p_turn(0)], 17: [scores(2), p_v(0)],
                18: [p_turn(1), v_new], 19: [scores(3), p_v(1)], 20: [p_turn(2), out_state], 21: [p_v(2)],
                22: [p_turn(3)], 23: [p_v(3)],
            }
            for lev in range(1, NLEV):
                mixer.setdefault(4 + 2 * lev, []).append(lev_z(lev))
                mixer.setdefault(5 + 2 * lev, []).append(lev_xz(lev))

            with pe.Fori(0, H) as i:
                for p in range(6):
                    def gap(q, p=p):
                        for step in mixer.get(4 * p + q, ()):
                            step(i)
                    unit(U_MIX, 6, i, p, xn_h, xn_l, KT, gaps=gap)

            def z_gap(p):
                def gap(q):
                    if p == 1 and q == 0:
                        pe.wait_ge(sig["osq_ok"], H)
                        column_sums(fb[0][:, 0:16], lambda j: osq[:, j // 4, P * (j % 4):P * (j % 4) + P], 16)\
                            .then_inc(sig["ostat_mm"], 1)
                    if p >= 2 and q % 2 == 1:
                        h = 2 * (p - 2) + q // 2
                        pe.wait_ge(sig["odiag_ok"], h + 1)
                        if h >= 2:
                            pe.wait_ge(sig["oa1_ok"], h - 1)
                        pe.matmul(gb[h % 2][:, :], ones, osq[:, h, :], start=True, stop=True).then_inc(sig["orow_mm"], 1)
                return gap

            for p in range(H):
                unit(U_Z, 4, 0, p, xn_h, xn_l, KT, gaps=z_gap(p))

            with pe.Fori(0, KT) as i:
                for p, (bh, bl) in enumerate(((oa_h, oa_l), (sc_h, sc_l), (fx_h, fx_l))):
                    unit(U_BR, 6, i, 2 * p, xn_h, xn_l, KT)
                    if p == 0:
                        pe.wait_ge(sig["oal_ok"], H)
                    unit(U_BR, 6, i, 2 * p + 1, bh, bl, H)
            with pe.Fori(0, KT // 2) as i:
                for p in range(2):
                    if p == 0:
                        pe.wait_ge(sig["mgl_ok"], KT + 1)
                    unit(U_O, 2, i, p, mg_h, mg_l, KT)

            def sums_and_row(n):
                pe.wait_ge(sig["rss_ok"], (KT + 1) * n)
                column_sums(fb[0][:, 0:NT], lambda j: sqsum[:, P * j:P * j + P], NT).then_inc(sig["rstat_mm"], 1)
                pe.wait_ge(sig["diag_ok"], n + 1)
                pe.matmul(fb[1][:, :], ones, diag[:, :, :], start=True, stop=True).then_inc(sig["rown_mm"], 1)

            sums_and_row(1)

            def xn2_ready(k):
                pe.wait_ge(sig["nl_done"], KT + k + 1)

            with pe.Fori(0, KF // 2) as i:
                for p in range(4):
                    unit(U_UP, 4, i, p, xn_h, xn_l, KT, k_wait=xn2_ready if p == 0 else None)
            with pe.Fori(0, KT // 2) as i:
                for p in range(6):
                    if p == 0:
                        pe.wait_ge(sig["f_l"], KF + 2)
                    if p % 3 == 0:
                        pe.wait_ge(acc_free[p // 3], i + (U_DN // 2 + 1))
                    unit(U_DN, 6, i, p, ff_h, ff_l, KDN[p % 3], k0=8 * (p % 3), bnk=p // 3,
                         start=p % 3 == 0, stop=p % 3 == 2)
            sums_and_row(2)

        @block.scalar
        def _(act):
            def hi(base, per, i, p, kt):
                slot = p % 2
                act.wait_ge(raw_in[slot], 8 * per * i + (8 * (base + p - slot) + 16))
                if base + p >= 2:
                    act.wait_ge(unit_done, per * i + (base + p - 1))
                act.copy(w_h[slot][:, 0:kt * P], raw[slot][:, 0:kt * P]).then_inc(hi_done, 1)

            def done(base, per, i, p):
                act.wait_ge(unit_done, per * i + (base + p + 1))

            for c in range(4):
                act.wait_ge(xin[c], 16)
                act.activation(x_sq[:, 2 * c:2 * c + 2, :], x_in[:, 2 * c:2 * c + 2, :], ACT.Square)\
                   .then_inc(sig["xsq_done"], 1)
            hi(0, 2, 0, 0, KT)
            hi(0, 2, 0, 1, KT)
            for k in range(KT):
                act.wait_ge(sig["nf_done"], k + 1)
                act.copy(xn_h[:, k, :], (sq2 if k % 2 else sqsum)[:, :]).then_inc(sig["nh_done"], 1)
            act.wait_ge(sig["ws_in"], 16)
            act.copy(ws_h[:, :], ws_raw[:, :]).then_inc(sig["wsh_done"], 1)
            act.wait_ge(sig["prm_in"], 16)
            act.activation(ea[:, :], prm[:, PRM["a_log"]], ACT.Exp).then_inc(sig["ea_ok"], 1)

            def conv_silu(i, p, base, square):
                b = p % 2
                if p == 0:
                    act.wait_ge(acc_free[1], 2 * i + (base // 2 + 1))
                    t0 = PRM["conv_qkv"].start
                    k = i if square else 2
                    act.copy(tap4[:, :, :], prm[:, bass.ds(t0 + 4 * H * k, 4 * H)].rearrange("p (h j) -> p h j", j=4))\
                       .then_inc(sig["qt_done"], 1)
                    act.wait_ge(sig["qt_done"], i + (3 if not square else 1))
                done(base, 4, i, p)
                act.activation(cy[b][:, :], acc[b][:, :], ACT.Copy, scale=tap4[:, p, 3:4]).then_inc(sig["qy_tap"], 1)
                act.wait_ge(acc_free[b], 2 * i + ((base + p) // 2 + 2))
                act.activation(th[b][:, :], cy[b][:, :], ACT.Tanh, scale=0.5).then_inc(sig["qth_ok"], 1)
                if square:
                    act.wait_ge(sig["q_done"], 4 * i + p + 1)
                    act.activation(sq[:, 4 * i + p, :], qkv[:, 4 * i + p, :], ACT.Square).then_inc(sig["sq_done"], 1)

            with act.Fori(0, 2) as i:
                for p in range(H):
                    hi(U_QK + 2, 4, i, p, KT)
                    conv_silu(i, p, U_QK, True)
            act.wait_ge(sig["colu_ok"], 1)
            act.activation(bet[:, 0, :, :], lg[:, :, 0:H], ACT.Exp, scale=-1.0).then_inc(sig["eb_done"], 1)
            act.activation(spu[:, 1, :, :], spu[:, 0, :, :], ACT.Abs).then_inc(sig["abs_ok"], 1)
            act.wait_ge(sig["abs_ok"], 1)
            act.activation(spu[:, 2, :, :], spu[:, 1, :, :], ACT.Exp, scale=-1.0).then_inc(sig["eb_done"], 1)
            for p in range(H):
                hi(U_V + 2, 4, 0, p, KT)
                conv_silu(0, p, U_V, False)
            act.wait_ge(sig["gc_mm"], 1)
            act.copy(gcols[:, :, Q_GC, :], fb[1][:, 0:16].rearrange("p (t h) -> p t h", h=H)).then_inc(sig["gcc_ok"], 1)
            act.activation(ec16[:, :, :], fb[1][:, 0:16].rearrange("p (t h) -> p t h", h=H), ACT.Exp)\
               .then_inc(sig["gcc_ok"], 1)

            def act_rows(i):
                act.wait_ge(sig["kd0_ok"], i + 1)
                act.activation(kd[:, 1, :], kd[:, 0, :], ACT.Exp).then_inc(sig["kdx_ok"], 1)
                act.activation(kd[:, 2, :], four(gb[0])[:, :, P - 1], ACT.Exp)
                act.activation(erow[:, :, :], four(gb[0]), ACT.Exp).then_inc(sig["erow_ok"], 1)
                act.activation(dec[:, :, :], dec[:, :, :], ACT.Exp).then_inc(sig["dec_ok"], 1)

            def act_cum(i):
                act.wait_ge(sig["cum_mm"], i + 1)
                act.copy(fcum[:, :, :], four(fb[2])).then_inc(sig["cum_done"], 1)

            def act_x(i):
                act.wait_ge(sig["xtr_mm"], i + 1)
                act.copy(xi[:, :, :], four(gb[0])).then_inc(sig["xi0_ok"], 1)

            def act_z(lev):
                def go(i):
                    act.wait_ge(sig["z_mm"], 6 * i + lev)
                    act.copy(half(zlev[lev][:, :, :], lev, 0), packed(gb[0], lev)).then_inc(sig["z_ok"], 1)
                return go

            def act_vn(i):
                act.wait_ge(sig["vn_mm"], i + 1)
                act.copy(vn[:, :, :], four(gb[1])).then_inc(sig["vn_ok"], 1)

            def act_o(i):
                act.wait_ge(sig["o_mm"], i + 1)
                act.copy(ogd[:, :, bass.ds(P * i, P)], four(gb[2])).then_inc(sig["o_ok"], 1)

            def act_fvt(i):
                act.wait_ge(sig["fvt_mm"], i + 1)
                act.copy(fvt[:, :, :], four(fb[1])).then_inc(sig["fvt_ok"], 1)

            def act_exp(t):
                def go(i):
                    act.wait_ge(sig["nmx_ok"], 4 * i + t + 1)
                    n = (t + 1) * P
                    act.activation(pr[t % 2][:, 0:n], pr[t % 2][:, 0:n], ACT.Exp, bias=fst[:, 1, t:t + 1],
                                   accum_out=fst[:, 2, t:t + 1]).then_inc(sig["exp_ok"], 1)
                return go

            def act_pt(t):
                def go(i):
                    act.wait_ge(sig["pt_mm"], 4 * i + t + 1)
                    if t:
                        act.wait_ge(sig["pv_mm"], 4 * i + t)
                    act.copy(pt[:, 0:t + 1, :], four(fb[1])[:, 0:t + 1, :]).then_inc(sig["pt_ok"], 1)
                return go

            def act_fx(i):
                act.wait_ge(sig["pv_mm"], 4 * i + 4)
                act.copy(fx_h[:, i, :], fb[2][:, :]).then_inc(sig["fxh_ok"], 1)

            mixer = {1: [act_rows], 3: [act_cum], 6: [act_x], 15: [act_fvt, act_exp(0)], 16: [act_exp(1)],
                     17: [act_pt(0)], 18: [act_exp(2)], 19: [act_pt(1), act_vn],
                     20: [act_exp(3)], 21: [act_pt(2), act_o], 23: [act_pt(3)]}
            for lev in range(1, NLEV):
                mixer.setdefault(5 + 2 * lev, []).append(act_z(lev))

            with act.Fori(0, H) as i:
                for p in range(6):
                    for g in range(4 * p, 4 * p + 4):
                        for step in mixer.get(g, ()):
                            step(i)
                    hi(U_MIX + 2, 6, i, p, KT)
                    done(U_MIX, 6, i, p)
                    b = p % 2
                    if p == 0:
                        act.mul(fq[:, :], acc[b][:, :], HD ** -0.5).then_inc(acc_free[b], 1)
                    elif p in (1, 2, 3):
                        act.copy((fk, fv, cs)[p - 1][:, :], acc[b][:, :]).then_inc(acc_free[b], 1)
                    elif p == 5:
                        evacuated(act, U_MIX, 6, i, p)
                        act.copy(sc_h[:, i, :], us[:, :]).then_inc(sig["sch_ok"], 1)
                        act_fx(i)

            for h in range(H):
                act.activation(osq[:, h, :], ogd[:, h, :], ACT.Square).then_inc(sig["osq_ok"], 1)
            for p in range(H):
                hi(U_Z + 2, 4, 0, p, H if p == 3 else KT)
                done(U_Z, 4, 0, p)
                if p >= 2:
                    evacuated(act, U_Z, 4, 0, p - 2)
                act.activation(zt[p % 2][:, :], acc[p % 2][:, :], ACT.Tanh, scale=0.5).then_inc(sig["zth_ok"], 1)
            for h in range(H):
                act.wait_ge(sig["oa2_ok"], h + 1)
                act.copy(oa_h[:, h, :], ogd[:, h, :]).then_inc(sig["oah_ok"], 1)

            def act_merge(i, last):
                for p in range(6):
                    hi(U_BR + 2, 6, i, p, KT if p % 2 == 0 or (last and p == 5) else H)
                    if p % 2 == 0:
                        done(U_BR, 6, i, p)
                        act.wait_ge(acc_free[1], 3 * i + ((U_BR + p) // 2 + 1))
                        act.activation(tg[:, :], acc[0][:, :], ACT.Tanh, scale=0.5).then_inc(acc_free[0], 1)
                act.wait_ge(sig["m2_ok"], 2 * i + 2)
                act.mul(mg_h[:, i, :], mg[:, :], 0.5).then_inc(sig["mgh_ok"], 1)

            with act.Fori(0, KT - 1) as i:
                act_merge(i, False)
            act_merge(KT - 1, True)

            with act.Fori(0, KT // 2) as i:
                for p in range(2):
                    hi(U_O + 2, 2, i, p, KT)
                    evacuated(act, U_O, 2, i, p)
                    act.wait_ge(sig["rss_ok"], 2 * i + p + 1)
                    act.activation(sq2[:, :], res[:, 2 * i + p, :], ACT.Square).then_inc(sig["rsq_ok"], 1)
            for k in range(KT):
                act.wait_ge(sig["nf_done"], KT + k + 1)
                act.copy(xn_h[:, k, :], (sq2 if k % 2 else sqsum)[:, :]).then_inc(sig["nh_done"], 1)

            with act.Fori(0, KF // 2) as i:
                for p in range(4):
                    b = p % 2
                    hi(U_UP + 2, 4, i, p, KT)
                    if p == 0:
                        act.wait_ge(acc_free[1], 2 * i + (U_UP // 2 + 1))
                        t0 = PRM["conv_ffn"].start
                        act.copy(tapf[:, :, :], prm[:, bass.ds(t0 + 12 * i, 12)].rearrange("p (a j) -> p a j", j=3))\
                           .then_inc(sig["f_tap"], 1)
                        act.wait_ge(sig["f_tap"], i + 1)
                    done(U_UP, 4, i, p)
                    act.activation(yc[p][:, :], acc[b][:, :], ACT.Copy, scale=tapf[:, p, 2:3]).then_inc(sig["fy_tap"], 1)
                    if b == 0:
                        evacuated(act, U_UP, 4, i, p)
                        act.activation(yt[p // 2][:, :], yc[p][:, :], ACT.Tanh, scale=0.5).then_inc(sig["fth_ok"], 1)
                    else:
                        act.wait_ge(sig["f_hv"], 2 * i + p // 2 + 1)
                        act.mul(ff_h[:, 2 * i + p // 2, :], hv[p // 2][:, :], 0.5).then_inc(sig["f_h"], 1)

            def act_down(i, last):
                for p in range(6):
                    if not (last and p >= 4):
                        hi(U_DN + 2, 6, i, p, KDN[(p + 2) % 3])
                    if p % 3 == 2:
                        act.wait_ge(acc_free[p // 3], i + (U_DN // 2 + 2))
                        act.wait_ge(sig["rss_ok"], 2 * i + (p // 3 + KT + 2))
                        act.activation(sq2[:, :], res[:, 2 * i + p // 3, :], ACT.Square).then_inc(sig["rsq_ok"], 1)

            with act.Fori(0, KT // 2 - 1) as i:
                act_down(i, False)
            act_down(KT // 2 - 1, True)

        @block.gpsimd
        def _(pool):
            pool.wait_ge(sig["cst_in"], 16)
            for z in zlev[1:] + [state]:
                pool.memset(z[:, :, :], 0.0).then_inc(sig["zer_ok"], 1)

            def prep(i, first):
                if first:
                    pool.wait_ge(sig["gcols_ok"], 1)
                else:
                    pool.wait_ge(sig["st_ok"], i + 1)
                    pool.wait_ge(sig["lt_ok"], i)
                    pool.wait_ge(sig["ks_mm"], i)
                pool.tensor_copy(gcs[:, :, :], gcols[:, i, :, :]).then_inc(sig["stage_ok"], 1)
                pool.tensor_copy(fcs[:, :], fcols[:, i, :]).then_inc(sig["stage_ok"], 1)
                pool.tensor_copy(stg[:, :, :], qkv[:, :, bass.ds(P * i, P)]).then_inc(sig["stage_ok"], 1)
                pool.wait_ge(sig["stage_ok"], 3 * i + 3)
                pool.tensor_tensor(dec[:, :, :], tiles(cst[:, C_TRI, :]), heads(gcs[:, Q_G, :]), ALU.mult)
                pool.tensor_tensor(kb[:, :, :], tiles(ident), heads(gcs[:, Q_BRK, :]), ALU.mult)
                pool.tensor_tensor(qh[:, :, :], tiles(ident), heads(gcs[:, Q_RQ, :]), ALU.mult)
                if not first:
                    pool.wait_ge(sig["lgt_ok"], 4 * i)
                pool.tensor_tensor(fcum[:, :, :], tiles(cst[:, C_TRI, :]), heads(fcs[:, 0:4]), ALU.mult)\
                    .then_inc(sig["fc_ok"], 1)
                pool.wait_ge(sig["fc_ok"], i + 1)
                pool.tensor_tensor(fcum[:, :, :], fcum[:, :, :], heads(fcs[:, 4:8]), ALU.add).then_inc(sig["prep_ok"], 1)

            def masks(i):
                pool.wait_ge(sig["lt_ok"], i + 1)
                for lev in range(1, NLEV):
                    if lev > 2:
                        pool.wait_ge(sig["z_mm"], 6 * i + lev - 2)
                    pool.tensor_tensor(olev[lev % 2][:, :, :], lt[:, :, :], tiles(cst[:, C_LEV + lev, :]), ALU.mult)\
                        .then_inc(sig["olev_ok"], 1)

            prep(0, True)
            with pool.Fori(0, H - 1) as i:
                masks(i)
                prep(i + 1, False)
            masks(H - 1)

        @block.vector
        def _(dve):
            links = [0]

            def link(ins):
                links[0] += 1
                ins.then_inc(sig["v_chain"], 1)
                dve.wait_ge(sig["v_chain"], links[0])

            def lo(base, per, i, p, kt):
                slot = p % 2
                dve.wait_ge(hi_done, per * i + (base + p + 1))
                dve.tensor_tensor(w_l[slot][:, 0:kt * P], raw[slot][:, 0:kt * P], w_h[slot][:, 0:kt * P].bitcast(F32),
                                  ALU.subtract).then_inc(lo_done, 1)

            def done(base, per, i, p):
                dve.wait_ge(unit_done, per * i + (base + p + 1))

            def rsqrt(y, x, a):
                link(dve.tensor_scalar(a.bitcast(I32), x.bitcast(I32), 1, None, ALU.arith_shift_right))
                link(dve.tensor_scalar(y.bitcast(I32), a.bitcast(I32), -1.0, float(0x5F3759DF), ALU.mult, ALU.add))
                for _ in range(3):
                    link(dve.tensor_tensor(a, y, y, ALU.mult))
                    link(dve.scalar_tensor_tensor(out=a, in0=a, scalar=-0.5, in1=x, op0=ALU.mult, op1=ALU.mult))
                    link(dve.scalar_tensor_tensor(out=y, in0=a, scalar=1.5, in1=y, op0=ALU.add, op1=ALU.mult))

            def token_factors():
                link(dve.tensor_scalar(col[:, 0, :], fb[0][:, 0:NT], 1.0 / D, EPS, ALU.mult, ALU.add))
                rsqrt(col[:, 1, :], col[:, 0, :], col[:, 2, :])
                dve.tensor_tensor(diag[:, :, :], tiles(ident, NT), heads(col[:, 1, :]), ALU.mult).then_inc(sig["diag_ok"], 1)

            def norm_blocks(n, src, gain):
                def low(k):
                    dve.wait_ge(sig["nh_done"], KT * n + k + 1)
                    dve.tensor_tensor(xn_l[:, k, :], (sq2 if k % 2 else sqsum)[:, :], xn_h[:, k, :].bitcast(F32),
                                      ALU.subtract).then_inc(sig["nl_done"], 1)
                dve.wait_ge(sig["rown_mm"], n + 1)
                for k in range(KT):
                    if k >= 2:
                        dve.wait_ge(sig["nl_done"], KT * n + k - 1)
                    g0 = PRM[gain].start + k
                    dve.scalar_tensor_tensor(out=(sq2 if k % 2 else sqsum)[:, :], in0=src[:, k, :], scalar=prm[:, g0:g0 + 1],
                                             in1=fb[1][:, :], op0=ALU.mult, op1=ALU.mult).then_inc(sig["nf_done"], 1)
                    if k:
                        low(k - 1)
                low(KT - 1)

            for j, free in enumerate((acc_free[0], acc_free[1], sig["st_ok"], sig["o_ok"], sig["fxl_ok"], sig["mgl_ok"], sig["f_l"], sig["f_l"])):
                dve.memset(col[:, 3 + j // 4, j % 4:j % 4 + 1], 0.0).then_inc(free, 1)
            lo(0, 2, 0, 0, KT)
            lo(0, 2, 0, 1, KT)
            dve.wait_ge(sig["cst_in"], 16)
            dve.wait_ge(sig["prm_in"], 16)
            dve.wait_ge(sig["xstat_mm"], 1)
            token_factors()
            norm_blocks(0, x_in, "g1")
            dve.wait_ge(sig["wsh_done"], 1)
            dve.tensor_tensor(ws_l[:, :], ws_raw[:, :], ws_h[:, :].bitcast(F32), ALU.subtract).then_inc(sig["wsl_done"], 1)

            def add_tap(y, x, tap, back):
                return dve.scalar_tensor_tensor(out=y[:, back:T], in0=x[:, 0:T - back], scalar=tap, in1=y[:, back:T],
                                                op0=ALU.mult, op1=ALU.add)

            def conv_silu(i, p, base):
                b, u = p % 2, 4 * i + (base + p)
                dve.wait_ge(sig["qy_tap"], u + 1)
                for j in (2, 1):
                    add_tap(cy[b], acc[b], tap4[:, p, j:j + 1], 3 - j).then_inc(sig["qc_ok"], 1)
                    dve.wait_ge(sig["qc_ok"], 2 * u + 3 - j)
                add_tap(cy[b], acc[b], tap4[:, p, 0:1], 3).then_inc(acc_free[b], 1)
                dve.wait_ge(sig["qth_ok"], u + 1)
                dve.scalar_tensor_tensor(out=qkv[:, 4 * i + (base + p), :], in0=th[b][:, :], scalar=1.0, in1=cy[b][:, :],
                                         op0=ALU.add, op1=ALU.mult).then_inc(sig["q_done"], 1)

            with dve.Fori(0, 2) as i:
                for p in range(H):
                    lo(U_QK + 2, 4, i, p, KT)
                    conv_silu(i, p, U_QK)

            dve.wait_ge(sig["small_mm"], 1)
            link(dve.tensor_copy(lg[:, :, :], fb[2][:, 0:12 * NT].rearrange("p (t c) -> p t c", c=12)))

            def rep(name):
                return prm[:, PRM[name]].unsqueeze(1).broadcast_to([P, NT, H])

            dve.tensor_tensor(spu[:, 0, :, 0:H], lg[:, :, H:2 * H], rep("dt_bias"), ALU.add)
            link(dve.tensor_tensor(spu[:, 0, :, H:], lg[:, :, 2 * H:], rep("fox_bias"), ALU.add))
            link(dve.tensor_scalar(spu[:, 0, :, H:], spu[:, 0, :, H:], -1.0, None, ALU.mult))
            dve.tensor_scalar(spu[:, 3, :, :], spu[:, 0, :, :], 0.0, None, ALU.max).then_inc(sig["colu_ok"], 1)
            lo(U_V + 2, 4, 0, 0, KT)
            dve.wait_ge(sig["eb_done"], 2)
            link(dve.tensor_scalar(bet[:, 1, :, :], bet[:, 0, :, :], 1.0, None, ALU.add))
            link(dve.reciprocal(bet[:, 2, :, :], bet[:, 1, :, :]))
            e, z, w, q = spu[:, 2, :, :], spu[:, 5, :, :], spu[:, 6, :, :], spu[:, 7, :, :]
            link(dve.tensor_scalar(w, e, 2.0, None, ALU.add))
            link(dve.reciprocal(q, w))
            link(dve.tensor_tensor(z, e, q, ALU.mult))
            link(dve.tensor_tensor(w, z, z, ALU.mult))
            link(dve.tensor_scalar(q, w, 1.0 / 17, None, ALU.mult))
            for n in (15, 13, 11, 9, 7, 5, 3):
                link(dve.scalar_tensor_tensor(out=q, in0=q, scalar=1.0 / n, in1=w, op0=ALU.add, op1=ALU.mult))
            link(dve.scalar_tensor_tensor(out=q, in0=q, scalar=1.0, in1=z, op0=ALU.add, op1=ALU.mult))
            sp = spu[:, 4, :, :]
            link(dve.scalar_tensor_tensor(out=sp, in0=q, scalar=2.0, in1=spu[:, 3, :, :], op0=ALU.mult, op1=ALU.add))
            dve.wait_ge(sig["ea_ok"], 1)
            dve.scalar_tensor_tensor(out=g16[:, :, :], in0=sp[:, :, 0:H], scalar=-1.0,
                                     in1=ea[:, :].unsqueeze(1).broadcast_to([P, NT, H]),
                                     op0=ALU.mult, op1=ALU.mult).then_inc(sig["colx"], 1)
            link(dve.tensor_copy(fcols[:, :, 0:NT], sp[:, :, H:].rearrange("p t h -> p h t")))
            link(dve.memset(fcols[:, :, NT:NT + 1], 0.0))
            for t in range(1, NT):
                link(dve.tensor_tensor(fcols[:, :, NT + t:NT + t + 1], fcols[:, :, NT + t - 1:NT + t],
                                       fcols[:, :, t - 1:t], ALU.add))
            conv_silu(0, 0, U_V)
            lo(U_V + 2, 4, 0, 1, KT)
            dve.wait_ge(sig["stat_mm"], 1)
            n2 = [nrm[:, j, :, :, :].rearrange("p a t h -> p (a t h)") for j in range(3)]
            link(dve.tensor_scalar(n2[0], fb[0][:, 0:32], 4.0 * EPS, None, ALU.add))
            rsqrt(n2[1], n2[0], n2[2])
            rq, rk = nrm[:, 1, 0, :, :], nrm[:, 1, 1, :, :]
            link(dve.tensor_scalar(gcols[:, :, Q_RQ, :], rq, HD ** -0.5, None, ALU.mult))
            link(dve.tensor_copy(gcols[:, :, Q_RK, :], rk))
            link(dve.tensor_copy(gcols[:, :, Q_G, :], g16[:, :, :]))
            link(dve.tensor_tensor(gcols[:, :, Q_BRK, :], bet[:, 2, :, :], rk, ALU.mult))
            link(dve.tensor_scalar(gcols[:, :, Q_HB, :], bet[:, 2, :, :], 0.5, None, ALU.mult))
            conv_silu(0, 1, U_V)
            for p in (2, 3):
                lo(U_V + 2, 4, 0, p, KT)
                conv_silu(0, p, U_V)
            dve.wait_ge(sig["gcc_ok"], 2)
            dve.scalar_tensor_tensor(out=gcols[:, :, Q_NBE, :], in0=gcols[:, :, Q_BRK, :], scalar=-1.0, in1=ec16[:, :, :],
                                     op0=ALU.mult, op1=ALU.mult).then_inc(sig["gcols_ok"], 1)

            def hcol(ap, h):
                return ap[:, h:h + 1]

            def v_rows(i):
                dve.wait_ge(sig["rows_mm"], i + 1)
                for h in range(H):
                    dve.scalar_tensor_tensor(out=dec[:, h, :], in0=gb[0][:, h * P:(h + 1) * P], scalar=gcs[:, Q_GC, h:h + 1],
                                             in1=cst[:, C_NEGT, :], op0=ALU.subtract, op1=ALU.min)
                dve.tensor_tensor(kd[:, 0, :], four(gb[0])[:, :, P - 1], gcs[:, Q_GC, :], ALU.subtract).then_inc(sig["kd0_ok"], 1)
                dve.tensor_tensor(kb[:, :, :], stg[:, H:2 * H, :], four(gb[1]), ALU.mult).then_inc(sig["kb_ok"], 1)
                dve.tensor_tensor(qh[:, :, :], stg[:, 0:H, :], four(gb[2]), ALU.mult).then_inc(sig["qh_ok"], 1)
                dve.wait_ge(sig["kdx_ok"], i + 1)
                dve.tensor_tensor(kd[:, 1, :], kd[:, 1, :], gcs[:, Q_RK, :], ALU.mult).then_inc(sig["kd1_ok"], 1)
                dve.wait_ge(sig["kvt_mm"], i + 1)
                dve.tensor_tensor(vb[:, :, :], four(fb[1]), heads(gcs[:, Q_HB, :]), ALU.mult).then_inc(sig["vb_ok"], 1)
                dve.wait_ge(sig["kd1_ok"], i + 1)
                dve.tensor_tensor(ktok[:, :, :], four(fb[0]), heads(kd[:, 1, :]), ALU.mult).then_inc(sig["ktok_ok"], 1)

            def v_kk(i):
                dve.wait_ge(sig["kk_mm"], i + 1)
                dve.wait_ge(sig["dec_ok"], i + 1)
                for h in range(H):
                    hs = slice(h * P, (h + 1) * P)
                    mm = dve.scalar_tensor_tensor(out=lt[:, h, :], in0=gb[1][:, hs], scalar=gcs[:, Q_RK, h:h + 1],
                                                  in1=dec[:, h, :], op0=ALU.mult, op1=ALU.mult)
                mm.then_inc(sig["lt_ok"], 1)
                dve.wait_ge(sig["lt_ok"], i + 1)
                dve.tensor_tensor(xi[:, :, :], lt[:, :, :], tiles(cst[:, C_LEV, :]), ALU.mult).then_inc(sig["ot0_ok"], 1)
                for h in range(H):
                    hs = slice(h * P, (h + 1) * P)
                    mm = dve.scalar_tensor_tensor(out=at[:, h, :], in0=gb[2][:, hs], scalar=gcs[:, Q_RK, h:h + 1],
                                                  in1=dec[:, h, :], op0=ALU.mult, op1=ALU.mult)
                mm.then_inc(sig["at_ok"], 1)
                dve.wait_ge(sig["ot0_ok"], i + 1)
                dve.tensor_tensor(xt[:, :, :], tiles(ident), xi[:, :, :], ALU.subtract).then_inc(sig["xt0_ok"], 1)
                dve.wait_ge(sig["erow_ok"], i + 1)
                dve.tensor_tensor(erow[:, :, :], erow[:, :, :], qh[:, :, :], ALU.mult).then_inc(sig["qe_ok"], 1)

            def v_r(i):
                dve.wait_ge(sig["ks_mm"], i + 1)
                for h in range(H):
                    hs = slice(h * P, (h + 1) * P)
                    mm = dve.scalar_tensor_tensor(out=vb[:, h, :], in0=fb[2][:, hs], scalar=gcs[:, Q_NBE, h:h + 1],
                                                  in1=vb[:, h, :], op0=ALU.mult, op1=ALU.add)
                mm.then_inc(sig["r_ok"], 1)

            def v_lev(lev):
                def go(i):
                    dve.wait_ge(sig["xz_mm"], 6 * i + lev)
                    if lev < NLEV - 1:
                        v = half(xi[:, :, :], lev, 0)
                        dve.tensor_tensor(v, v, packed(gb[1], lev), ALU.subtract).then_inc(sig["xi_ok"], 1)
                    v = half(xt[:, :, :], lev, 1)
                    dve.tensor_tensor(v, v, packed(gb[2], lev), ALU.subtract).then_inc(sig["xt_ok"], 1)
                return go

            def v_state(i):
                dve.wait_ge(sig["ds_mm"], i + 1)
                for h in range(H):
                    mm = dve.scalar_tensor_tensor(out=state[:, h, :], in0=state[:, h, :], scalar=kd[:, 2, h:h + 1],
                                                  in1=gb[0][:, h * P:(h + 1) * P], op0=ALU.mult, op1=ALU.add)
                mm.then_inc(sig["st_ok"], 1)

            def v_soft(t):
                def go(i):
                    n, d = (t + 1) * P, slice(t * P, (t + 1) * P)
                    x = pr[t % 2]
                    dve.wait_ge(sig["s_mm"], 4 * i + t + 1)
                    dve.tensor_tensor(x[:, 0:n], fb[0][:, 0:n], fcum[:, 0:t + 1, :].rearrange("p t c -> p (t c)"), ALU.add)\
                        .then_inc(sig["lgt_ok"], 1)
                    dve.wait_ge(sig["lgt_ok"], 4 * i + t + 1)
                    dve.tensor_tensor(x[:, d], x[:, d], cst[:, C_CAUSAL, :], ALU.add).then_inc(sig["msk_ok"], 1)
                    dve.wait_ge(sig["msk_ok"], 4 * i + t + 1)
                    dve.reduce_max(fst[:, 0, t:t + 1], x[:, 0:n], AX_X).then_inc(sig["mx_ok"], 1)
                    dve.wait_ge(sig["mx_ok"], 4 * i + t + 1)
                    dve.tensor_scalar(fst[:, 1, t:t + 1], fst[:, 0, t:t + 1], -1.0, None, ALU.mult).then_inc(sig["nmx_ok"], 1)
                return go

            def v_pn(t):
                def go(i):
                    n = (t + 1) * P
                    dve.wait_ge(sig["exp_ok"], 4 * i + t + 1)
                    dve.reciprocal(fst[:, 3, t:t + 1], fst[:, 2, t:t + 1]).then_inc(sig["ri_ok"], 1)
                    dve.wait_ge(sig["ri_ok"], 4 * i + t + 1)
                    dve.tensor_scalar(pr[t % 2][:, 0:n], pr[t % 2][:, 0:n], fst[:, 3, t:t + 1], None, ALU.mult)\
                        .then_inc(sig["pn_ok"], 1)
                return go

            def v_fx(i):
                dve.wait_ge(sig["fxh_ok"], i + 1)
                dve.tensor_tensor(fx_l[:, i, :], fb[2][:, :], fx_h[:, i, :].bitcast(F32), ALU.subtract)\
                    .then_inc(sig["fxl_ok"], 1)

            mixer = {1: [v_rows], 4: [v_kk], 5: [v_r],
                     14: [v_soft(0)], 15: [v_pn(0)], 16: [v_soft(1)], 17: [v_pn(1)],
                     18: [v_soft(2)], 19: [v_pn(2)], 20: [v_soft(3)], 21: [v_pn(3), v_state]}
            for lev in range(1, NLEV):
                mixer.setdefault(6 + 2 * lev, []).insert(0, v_lev(lev))

            with dve.Fori(0, H) as i:
                for p in range(6):
                    for g in range(4 * p, 4 * p + 4):
                        for step in mixer.get(g, ()):
                            step(i)
                    lo(U_MIX + 2, 6, i, p, KT)
                    if p == 4:
                        done(U_MIX, 6, i, p)
                        evacuated(dve, U_MIX, 6, i, 3)
                        dve.tensor_tensor(us[:, :], cs[:, :], acc[0][:, :], ALU.mult).then_inc(acc_free[0], 1)
                        evacuated(dve, U_MIX, 6, i, 4)
                        t0 = PRM["conv_sc"].start
                        dve.tensor_copy(tap3[:, :], prm[:, bass.ds(t0 + 3 * i, 3)]).then_inc(sig["sct_ok"], 1)
                        dve.wait_ge(sig["sct_ok"], i + 1)
                        dve.tensor_scalar(cs[:, :], us[:, :], tap3[:, 2:3], None, ALU.mult).then_inc(sig["scc_ok"], 1)
                        for j in (1, 0):
                            dve.wait_ge(sig["scc_ok"], 3 * i + 2 - j)
                            add_tap(cs, us, tap3[:, j:j + 1], 2 - j).then_inc(sig["scc_ok"], 1)
                    if p == 5:
                        done(U_MIX, 6, i, p)
                        dve.wait_ge(sig["scc_ok"], 3 * i + 3)
                        dve.tensor_tensor(us[:, :], cs[:, :], acc[1][:, :], ALU.mult).then_inc(acc_free[1], 1)
                        dve.wait_ge(sig["sch_ok"], i + 1)
                        dve.tensor_tensor(sc_l[:, i, :], us[:, :], sc_h[:, i, :].bitcast(F32), ALU.subtract)\
                            .then_inc(sig["scl_ok"], 1)
                        v_fx(i)

            def v_z(p):
                lo(U_Z + 2, 4, 0, p, H if p == 3 else KT)
                dve.wait_ge(sig["zth_ok"], p + 1)
                dve.scalar_tensor_tensor(out=zg[:, p, :], in0=zt[p % 2][:, :], scalar=1.0, in1=acc[p % 2][:, :],
                                         op0=ALU.add, op1=ALU.mult).then_inc(acc_free[p % 2], 1)

            def v_odiag(h):
                dve.tensor_tensor(osq[:, h, :].rearrange("p (t c) -> p t c", t=NT), tiles(ident), heads(onrm[:, 1, h, :]),
                                  ALU.mult).then_inc(sig["odiag_ok"], 1)

            def v_oa(h):
                dve.wait_ge(sig["orow_mm"], h + 1)
                dve.scalar_tensor_tensor(out=ogd[:, h, :], in0=ogd[:, h, :], scalar=gn_half[:, 0:1], in1=gb[h % 2][:, :],
                                         op0=ALU.mult, op1=ALU.mult).then_inc(sig["oa1_ok"], 1)
                dve.wait_ge(sig["oa1_ok"], h + 1)
                evacuated(dve, U_Z, 4, 0, h)
                dve.tensor_tensor(ogd[:, h, :], ogd[:, h, :], zg[:, h, :], ALU.mult).then_inc(sig["oa2_ok"], 1)

            def v_oal(h):
                dve.wait_ge(sig["oah_ok"], h + 1)
                dve.tensor_tensor(oa_l[:, h, :], ogd[:, h, :], oa_h[:, h, :].bitcast(F32), ALU.subtract)\
                    .then_inc(sig["oal_ok"], 1)

            link(dve.tensor_scalar(gn_half[:, :], prm[:, PRM["gdn_norm"]], 0.5, None, ALU.mult))
            v_z(0)
            dve.wait_ge(sig["ostat_mm"], 1)
            o2 = [onrm[:, j, :, :].rearrange("p h t -> p (h t)") for j in range(3)]
            link(dve.tensor_scalar(o2[0], fb[0][:, 0:16], 1.0 / HD, EPS, ALU.mult, ALU.add))
            rsqrt(o2[1], o2[0], o2[2])
            for h in range(H):
                v_odiag(h)
            v_z(1)
            v_z(2)
            v_oa(0)
            v_oa(1)
            v_z(3)
            v_oa(2)
            v_oa(3)
            for h in range(H):
                v_oal(h)

            def v_merge(i, last):
                for p in range(6):
                    lo(U_BR + 2, 6, i, p, KT if p % 2 == 0 or (last and p == 5) else H)
                    if p % 2:
                        done(U_BR, 6, i, p)
                        evacuated(dve, U_BR, 6, i, p - 1)
                        if p == 1:
                            dve.wait_ge(sig["mgl_ok"], i + 1)
                        dst = mg if p == 1 else mg2
                        dve.scalar_tensor_tensor(out=dst[:, :], in0=tg[:, :], scalar=1.0, in1=acc[1][:, :],
                                                 op0=ALU.add, op1=ALU.mult).then_inc(acc_free[1], 1)
                        if p > 1:
                            evacuated(dve, U_BR, 6, i, p)
                            dve.tensor_tensor(mg[:, :], mg[:, :], mg2[:, :], ALU.add).then_inc(sig["m2_ok"], 1)
                            if p == 3:
                                dve.wait_ge(sig["m2_ok"], 2 * i + 1)
                dve.wait_ge(sig["mgh_ok"], i + 1)
                dve.scalar_tensor_tensor(out=mg_l[:, i, :], in0=mg[:, :], scalar=0.5, in1=mg_h[:, i, :].bitcast(F32),
                                         op0=ALU.mult, op1=ALU.subtract).then_inc(sig["mgl_ok"], 1)

            with dve.Fori(0, KT - 1) as i:
                v_merge(i, False)
            v_merge(KT - 1, True)

            dve.memset(sqsum[:, :], 0.0).then_inc(sig["rss_ok"], 1)
            dve.wait_ge(sig["xres_in"], 16)
            with dve.Fori(0, KT // 2) as i:
                for p in range(2):
                    lo(U_O + 2, 2, i, p, KT)
                    done(U_O, 2, i, p)
                    dve.tensor_tensor(res[:, 2 * i + p, :], x_res[:, 2 * i + p, :], acc[p][:, :], ALU.add)\
                        .then_inc(acc_free[p], 1)
                    dve.wait_ge(sig["rsq_ok"], 2 * i + p + 1)
                    dve.tensor_tensor(sqsum[:, :], sqsum[:, :], sq2[:, :], ALU.add).then_inc(sig["rss_ok"], 1)
            dve.wait_ge(sig["rstat_mm"], 1)
            token_factors()
            norm_blocks(1, res, "g2")

            def f_low(n, q):
                dve.wait_ge(sig["f_h"], n + 1)
                dve.scalar_tensor_tensor(out=ff_l[:, n, :], in0=hv[q][:, :], scalar=0.5, in1=ff_h[:, n, :].bitcast(F32),
                                         op0=ALU.mult, op1=ALU.subtract).then_inc(sig["f_l"], 1)

            with dve.Fori(0, KF // 2) as i:
                for p in range(4):
                    b, q, u = p % 2, p // 2, 4 * i + p
                    lo(U_UP + 2, 4, i, p, KT)
                    if p == 2:
                        f_low(2 * i, 0)
                    dve.wait_ge(sig["fy_tap"], u + 1)
                    add_tap(yc[p], acc[b], tapf[:, p, 1:2], 1).then_inc(sig["fc1_ok"], 1)
                    dve.wait_ge(sig["fc1_ok"], u + 1)
                    add_tap(yc[p], acc[b], tapf[:, p, 0:1], 2).then_inc(acc_free[b], 1)
                    if b:
                        dve.wait_ge(sig["fth_ok"], 2 * i + q + 1)
                        dve.scalar_tensor_tensor(out=yc[p - 1][:, :], in0=yt[q][:, :], scalar=1.0, in1=yc[p - 1][:, :],
                                                 op0=ALU.add, op1=ALU.mult).then_inc(sig["f_sg"], 1)
                        dve.wait_ge(sig["f_sg"], 2 * i + q + 1)
                        evacuated(dve, U_UP, 4, i, p)
                        dve.wait_ge(sig["f_l"], 2 * i + q + 1)
                        dve.tensor_tensor(hv[q][:, :], yc[p - 1][:, :], yc[p][:, :], ALU.mult).then_inc(sig["f_hv"], 1)
                f_low(2 * i + 1, 1)

            dve.memset(sqsum[:, :], 0.0).then_inc(sig["rss_ok"], 1)

            def v_down(i, last):
                for p in range(6):
                    if not (last and p >= 4):
                        lo(U_DN + 2, 6, i, p, KDN[(p + 2) % 3])
                    if p % 3 == 2:
                        m, b = 2 * i + p // 3, p // 3
                        done(U_DN, 6, i, p)
                        dve.tensor_tensor(res[:, m, :], res[:, m, :], acc[b][:, :], ALU.add).then_inc(acc_free[b], 1)
                        dve.wait_ge(sig["rsq_ok"], m + KT + 1)
                        dve.tensor_tensor(sqsum[:, :], sqsum[:, :], sq2[:, :], ALU.add).then_inc(sig["rss_ok"], 1)

            with dve.Fori(0, KT // 2 - 1) as i:
                v_down(i, False)
            v_down(KT // 2 - 1, True)

            dve.wait_ge(sig["rstat_mm"], 2)
            token_factors()
            dve.wait_ge(sig["rown_mm"], 3)
            for k in range(KT):
                g0 = PRM["gf"].start + k
                dve.scalar_tensor_tensor(out=res[:, k, :], in0=res[:, k, :], scalar=prm[:, g0:g0 + 1], in1=fb[1][:, :],
                                         op0=ALU.mult, op1=ALU.mult).then_inc(sig["out_ok"], 1)


def kernel(x, norm1_g, w_in, conv_qkv, a_log, dt_bias, gdn_norm, w_br_a, conv_sc, w_br_b, fox_bias, w_br_c, w_o,
           norm2_g, w_up, conv_ffn, w_down, norm_f):
    import numpy as np
    import concourse.bacc as bacc
    from concourse import mybir
    from concourse.bass_utils import run_bass_kernel_spmd

    def blocks(w, kt):
        n = w.shape[1] // P
        return w.reshape(kt, P, n, P).transpose(2, 1, 0, 3).reshape(n, P, kt * P)

    def columns(v):
        return v.reshape(-1, P).T

    def tap_columns(v, kinds):
        taps = v.shape[0]
        return v.reshape(taps, kinds, -1, P).transpose(3, 2, 1, 0).reshape(P, -1)

    w_in = w_in[0]
    W = H * HD
    at = [0]

    def take(n):
        at[0] += n
        return w_in[:, at[0] - n:at[0]]

    qkv_a, z_a, beta, alog, bch, qkv_c, flog, gates = (
        take(3 * W), take(W), take(H), take(H), take(3 * W), take(3 * W), take(H), take(3 * D))

    def part(a, j, n):
        return a[:, j * n:(j + 1) * n]

    mix = [blocks(part(qkv_c, 0, W), KT), blocks(part(qkv_c, 1, W), KT), blocks(part(qkv_c, 2, W), KT),
           blocks(part(bch, 1, W), KT), blocks(part(bch, 2, W), KT), blocks(part(bch, 0, W), KT)]
    idx = np.arange(P)
    row, colm = idx[:, None], idx[None, :]
    consts = np.zeros((P, NCONST, P), np.float32)
    consts[:, C_ID] = row == colm
    consts[:, C_ONE] = 1.0
    consts[:, C_TRI] = row <= colm
    consts[:, C_NEGT] = np.where(colm >= row, 0.0, NEG)
    consts[:, C_CAUSAL] = np.where(colm <= row, 0.0, NEG)
    for lev in range(NLEV):
        b = 1 << lev
        consts[:, C_LEV + lev] = (row // (2 * b) == colm // (2 * b)) & (row % (2 * b) < b) & (colm % (2 * b) >= b)

    def everywhere(v):
        return np.broadcast_to(v, (P, v.shape[-1]))

    params = np.concatenate([
        columns(norm1_g[0]), columns(norm2_g[0]), columns(norm_f), tap_columns(conv_qkv[0], 1),
        tap_columns(conv_sc[0], 1), tap_columns(conv_ffn[0], 2), columns(gdn_norm[0]),
        everywhere(a_log), everywhere(dt_bias), everywhere(fox_bias)], axis=1)
    w_small = np.concatenate([beta, alog, flog], axis=1).reshape(KT, P, 12).transpose(1, 0, 2).reshape(P, KT * 12)
    arrays = {
        "xT": x[0].T,
        "consts": consts.reshape(P, NCONST * P),
        "params": params,
        "w_small": w_small,
        "w_qkv": blocks(qkv_a, KT),
        "w_mix": np.stack(mix, axis=1).reshape(6 * H, P, KT * P),
        "w_z": blocks(z_a, KT),
        "w_gate": np.stack([blocks(part(gates, j, D), KT) for j in range(3)], axis=1).reshape(3 * KT, P, KT * P),
        "w_br": np.stack([blocks(w[0], H) for w in (w_br_a, w_br_b, w_br_c)], axis=1).reshape(3 * KT, P, H * P),
        "w_o": blocks(w_o[0], KT),
        "w_up": np.stack([blocks(part(w_up[0], j, FF), KT) for j in range(2)], axis=1).reshape(2 * KF, P, KT * P),
        "w_dn": blocks(w_down[0], KF),
    }
    arrays = {n: np.ascontiguousarray(a) for n, a in arrays.items()}
    nc = bacc.Bacc("TRN2", target_bir_lowering=False, num_devices=1)
    args = [nc.dram_tensor(n, a.shape, mybir.dt.from_np(a.dtype), kind="ExternalInput").ap() for n, a in arrays.items()]
    outT = nc.dram_tensor("outT", (D, T), mybir.dt.float32, kind="ExternalOutput").ap()
    build(nc, *args, outT)
    r = run_bass_kernel_spmd(nc, [arrays], core_ids=[0])
    return np.ascontiguousarray(r.results[0]["outT"].T)[None]
```

```python
from contextlib import ExitStack

import numpy as np

import concourse.bass as bass
from concourse import mybir

ALU = mybir.AluOpType
ACT = mybir.ActivationFunctionType
F32 = mybir.dt.float32
F32R = mybir.dt.float32r
I32 = mybir.dt.int32
AX_X = mybir.AxisListType.X

P = 128
D = 1024
T = 512
KT = D // P
NT = T // P
H = 4
HD = 128
FF = 2816
KF = FF // P
EPS = 1e-6
NLEV = 7
NEG = -1.0e30

U_QK = 0
U_V = U_QK + 2 * H
U_MIX = U_V + H
U_Z = U_MIX + 6 * H
U_BR = U_Z + H
U_O = U_BR + 6 * KT
U_UP = U_O + KT
U_DN = U_UP + 2 * KF
KDN = (8, 8, KF - 16)

C_ID, C_ONE, C_TRI, C_NEGT, C_CAUSAL, C_LEV = 0, 1, 2, 3, 4, 5
NCONST = C_LEV + NLEV

PRM = {}
_at = 0
for _n, _w in (("g1", KT), ("g2", KT), ("gf", KT), ("conv_qkv", 3 * H * 4), ("conv_sc", H * 3),
               ("conv_ffn", KF * 2 * 3), ("gdn_norm", 1), ("a_log", H), ("dt_bias", H), ("fox_bias", H)):
    PRM[_n] = slice(_at, _at + _w)
    _at += _w
NPRM = _at

Q_G, Q_BRK, Q_RQ, Q_RK, Q_GC, Q_NBE, Q_HB = range(7)


def build(nc, xT, consts, params, w_small, w_qkv, w_mix, w_z, w_gate, w_br, w_o, w_up, w_dn, outT):
    ctx = ExitStack()
    with ctx:
        def sb(name, shape, dt=F32, scope=ctx):
            return scope.enter_context(nc.sbuf_tensor(name, shape, dt))

        def bank(name):
            return ctx.enter_context(nc.psum_tensor(name, [P, 512], F32))

        def sem(name):
            return ctx.enter_context(nc.semaphore(name))

        cst = sb("cst", [P, NCONST, P])
        prm = sb("prm", [P, NPRM])
        raw = [sb(f"raw{s}", [P, KT * P]) for s in range(2)]
        w_h = [sb(f"w_h{s}", [P, KT * P], F32R) for s in range(2)]
        w_l = [sb(f"w_l{s}", [P, KT * P], F32R) for s in range(2)]
        xn_h = sb("xn_h", [P, KT, T], F32R)
        xn_l = sb("xn_l", [P, KT, T], F32R)
        ws_raw = sb("ws_raw", [P, KT * 12])
        ws_h = sb("ws_h", [P, KT * 12], F32R)
        ws_l = sb("ws_l", [P, KT * 12], F32R)
        col = sb("col", [P, 8, NT])
        diag = sb("diag", [P, NT, P])
        sqsum = sb("sqsum", [P, T])
        sq2 = sb("sq2", [P, T])
        ident = cst[:, C_ID, :]
        ones = cst[:, C_ONE, :]

        s_br = ExitStack()
        ogd = sb("ogd", [P, H, T], F32, s_br)
        sc_h = sb("sc_h", [P, H, T], F32R, s_br)
        sc_l = sb("sc_l", [P, H, T], F32R, s_br)
        fx_h = sb("fx_h", [P, H, T], F32R, s_br)
        fx_l = sb("fx_l", [P, H, T], F32R, s_br)

        s_x = ExitStack()
        x_in = sb("x_in", [P, KT, T], F32, s_x)
        x_sq = sb("x_sq", [P, KT, T], F32, s_x)
        s_x.close()

        s_mix = ExitStack()
        qkv = sb("qkv", [P, 3 * H, T], F32, s_mix)
        lg = sb("lg", [P, NT, 12], F32, s_mix)
        spu = sb("spu", [P, 8, NT, 2 * H], F32, s_mix)
        ea = sb("ea", [P, H], F32, s_mix)
        bet = sb("bet", [P, 3, NT, H], F32, s_mix)
        g16 = sb("g16", [P, NT, H], F32, s_mix)
        ec16 = sb("ec16", [P, NT, H], F32, s_mix)
        nrm = sb("nrm", [P, 3, 2, NT, H], F32, s_mix)
        gcols = sb("gcols", [P, NT, 7, H], F32, s_mix)
        fcols = sb("fcols", [P, H, 8], F32, s_mix)
        s_qkv = ExitStack()
        sq = sb("sq", [P, 2 * H, T], F32, s_qkv)
        cy = [sb(f"cy{s}", [P, T], F32, s_qkv) for s in range(2)]
        th = [sb(f"th{s}", [P, T], F32, s_qkv) for s in range(2)]
        tap4 = sb("tap4", [P, H, 4], F32, s_qkv)
        s_qkv.close()
        gcs = sb("gcs", [P, 7, H], F32, s_mix)
        kd = sb("kd", [P, 3, H], F32, s_mix)
        stg = sb("stg", [P, 3 * H, P], F32, s_mix)
        kb = sb("kb", [P, H, P], F32, s_mix)
        qh = sb("qh", [P, H, P], F32, s_mix)
        erow = sb("erow", [P, H, P], F32, s_mix)
        dec = sb("dec", [P, H, P], F32, s_mix)
        lt = sb("lt", [P, H, P], F32, s_mix)
        at = sb("at", [P, H, P], F32, s_mix)
        olev = [sb(f"olev{s}", [P, H, P], F32, s_mix) for s in range(2)]
        xi = sb("xi", [P, H, P], F32, s_mix)
        xt = sb("xt", [P, H, P], F32, s_mix)
        zlev = [None] + [sb(f"zlev{s}", [P, H, P], F32, s_mix) for s in range(1, NLEV)]
        ktok = sb("ktok", [P, H, P], F32, s_mix)
        vb = sb("vb", [P, H, P], F32, s_mix)
        vn = sb("vn", [P, H, P], F32, s_mix)
        state = sb("state", [P, H, P], F32, s_mix)
        fq = sb("fq", [P, T], F32, s_mix)
        fk = sb("fk", [P, T], F32, s_mix)
        fv = sb("fv", [P, T], F32, s_mix)
        fvt = sb("fvt", [P, NT, P], F32, s_mix)
        fcs = sb("fcs", [P, 8], F32, s_mix)
        fcum = sb("fcum", [P, NT, P], F32, s_mix)
        pr = [sb(f"pr{s}", [P, T], F32, s_mix) for s in range(2)]
        pt = sb("pt", [P, NT, P], F32, s_mix)
        fst = sb("fst", [P, 4, NT], F32, s_mix)
        cs = sb("cs", [P, T], F32, s_mix)
        us = sb("us", [P, T], F32, s_mix)
        tap3 = sb("tap3", [P, 3], F32, s_mix)
        s_mix.close()

        s_bp = ExitStack()
        zg = sb("zg", [P, H, T], F32, s_bp)
        oa_h = sb("oa_h", [P, H, T], F32R, s_bp)
        oa_l = sb("oa_l", [P, H, T], F32R, s_bp)
        osq = sb("osq", [P, H, T], F32, s_bp)
        gn_half = sb("gn_half", [P, 1], F32, s_bp)
        onrm = sb("onrm", [P, 4, H, NT], F32, s_bp)
        zt = [sb(f"zt{s}", [P, T], F32, s_bp) for s in range(2)]
        tg = sb("tg", [P, T], F32, s_bp)
        mg = sb("mg", [P, T], F32, s_bp)
        mg2 = sb("mg2", [P, T], F32, s_bp)
        mg_h = sb("mg_h", [P, KT, T], F32R, s_bp)
        mg_l = sb("mg_l", [P, KT, T], F32R, s_bp)
        x_res = sb("x_res", [P, KT, T], F32, s_bp)
        s_bp.close()
        s_br.close()

        res = sb("res", [P, KT, T])
        ff_h = sb("ff_h", [P, KF, T], F32R)
        ff_l = sb("ff_l", [P, KF, T], F32R)
        yc = [sb(f"yc{s}", [P, T]) for s in range(4)]
        yt = [sb(f"yt{s}", [P, T]) for s in range(2)]
        hv = [sb(f"hv{s}", [P, T]) for s in range(2)]
        tapf = sb("tapf", [P, 4, 3])

        acc = [bank(f"acc{s}") for s in range(2)]
        gb = [bank(f"gb{s}") for s in range(3)]
        fb = [bank(f"fb{s}") for s in range(3)]

        raw_in = [sem(f"raw_in{s}") for s in range(2)]
        hi_done = sem("hi_done")
        lo_done = sem("lo_done")
        half_done = sem("half_done")
        acc_free = [sem(f"acc_free{b}") for b in range(2)]
        sig = {n: sem(n) for n in """
            abs_ok at_ok colu_ok colx cst_in cum_done cum_mm dec_ok diag_ok ds_mm ea_ok eb_done erow_ok exp_ok
            f_h f_hv f_l f_sg f_tap fc1_ok fc_ok fprep_ok fth_ok fvt_mm fvt_ok fxh_ok fxl_ok fy_tap gc_mm gcc_ok
            gcols_ok gcs_ok kb_ok kd0_ok kd1_ok kdx_ok kk_mm kq_mm ks_mm ktok_ok kvt_mm lgt_ok lt_ok m2_ok
            mgh_ok mgl_ok msk_ok mx_ok nf_done nh_done nl_done nmx_ok o_mm o_ok oa1_ok oa2_ok oah_ok oal_ok
            odiag_ok olev_ok orow_mm osq_ok ostat_mm ot0_ok out_ok out_st pn_ok prep_ok prm_in pt_mm pt_ok pv_mm
            q_done qc_ok qe_ok qh_ok qt_done qth_ok qy_tap r_ok ri_ok rown_mm rows_mm rsq_ok rss_ok rstat_mm
            s_mm scc_ok sch_ok scl_ok sct_ok small_mm sq_done st_ok stage_ok stat_mm v_chain vb_ok vn_mm vn_ok
            ws_in wsh_done wsl_done xi0_ok xi_ok xres_in xsq_done xstat_mm xsum_ok xt0_ok xt_ok xtr_mm xz_mm
            z_mm z_ok zer_ok zth_ok""".split()}
        xin = [sem(f"xin{c}") for c in range(4)]


        block = ctx.enter_context(nc.Block())

        def heads(ap):
            return ap.unsqueeze(2).broadcast_to([P, ap.shape[1], P])

        def tiles(ap, n=H):
            return ap.unsqueeze(1).broadcast_to([P, n, P])

        def four(b):
            return b[:, :].rearrange("p (h c) -> p h c", h=H)

        def half(ap, lev, up):
            v = ap.rearrange("p h (g two b) -> p (h g) two b", two=2, b=1 << lev)
            return v[:, :, up, :]

        def half1(ap, lev, up):
            v = ap.rearrange("p (g two b) -> p g two b", two=2, b=1 << lev)
            return v[:, :, up, :]

        def packed(b, lev):
            return b[:, 0:H * 64].rearrange("p (g b) -> p g b", b=1 << lev)

        def evacuated(eng, base, per, i, p):
            eng.wait_ge(acc_free[p % 2], per // 2 * i + ((base + p) // 2 + 2))

        @block.sync
        def _(sp):
            def fetch(slot, src, kt):
                sp.dma_start(raw[slot][:, 0:kt * P], src).then_inc(raw_in[slot], 16)

            xv = xT.rearrange("(c k p) t -> c p k t", c=4, p=P)
            for c in range(4):
                sp.dma_start(x_in[:, 2 * c:2 * c + 2, :], xv[c]).then_inc(xin[c], 16)
            sp.dma_start(cst[:, :, :], consts.rearrange("p (n c) -> p n c", c=P)).then_inc(sig["cst_in"], 16)
            sp.dma_start(prm[:, :], params).then_inc(sig["prm_in"], 16)
            sp.dma_start(ws_raw[:, :], w_small).then_inc(sig["ws_in"], 16)
            for u in range(2):
                fetch(u, w_qkv[u], KT)
            with sp.Fori(1, 6) as i:
                for p in range(2):
                    sp.wait_ge(lo_done, 4 * i + 2 * p - 2)
                    fetch(p, w_qkv[2 * i + p], KT)
            with sp.Fori(0, 12) as i:
                for p in range(2):
                    sp.wait_ge(lo_done, 4 * i + 2 * (U_MIX + p - 1))
                    fetch(p, w_mix[2 * i + p], KT)
            for i in range(H):
                sp.wait_ge(lo_done, 2 * (U_Z + i - 1))
                fetch(i % 2, w_z[i], KT)
            sp.wait_ge(sig["fxl_ok"], H + 1)
            sp.wait_ge(sig["scl_ok"], H)
            sp.wait_ge(sig["st_ok"], H + 1)
            sp.dma_start(x_res[:, :, :], xT.rearrange("(k p) t -> p k t", p=P)).then_inc(sig["xres_in"], 16)
            with sp.Fori(0, KT) as i:
                for p in range(3):
                    sp.wait_ge(lo_done, 12 * i + 2 * (U_BR + 2 * p - 1))
                    fetch(0, w_gate[3 * i + p], KT)
                    sp.wait_ge(lo_done, 12 * i + 2 * (U_BR + 2 * p))
                    fetch(1, w_br[3 * i + p], H)
            with sp.Fori(0, KT // 2) as i:
                for p in range(2):
                    sp.wait_ge(lo_done, 4 * i + 2 * (U_O + p - 1))
                    fetch(p, w_o[2 * i + p], KT)
            with sp.Fori(0, KF) as i:
                for p in range(2):
                    sp.wait_ge(lo_done, 4 * i + 2 * (U_UP + p - 1))
                    fetch(p, w_up[2 * i + p], KT)
            with sp.Fori(0, KT // 2) as i:
                for p in range(6):
                    k0 = 8 * (p % 3)
                    sp.wait_ge(lo_done, 12 * i + 2 * (U_DN + p - 1))
                    fetch(p % 2, w_dn[2 * i + p // 3][:, k0 * P:(k0 + KDN[p % 3]) * P], KDN[p % 3])
            for k in range(KT):
                sp.wait_ge(sig["out_ok"], k + 1)
                sp.dma_start(outT[k * P:(k + 1) * P, :], res[:, k, :]).then_inc(sig["out_st"], 16)
            sp.wait_ge(sig["out_st"], 16 * KT)

        @block.tensor
        def _(pe):
            def passes(out, wh, wl, xh, xl, start, stop):
                pe.matmul(out, wh, xh, start=start, stop=False)
                pe.matmul(out, wh, xl, start=False, stop=False)
                return pe.matmul(out, wl, xh, start=False, stop=stop)

            def unit(base, per, i, p, xh, xl, kt, k0=0, bnk=None, start=True, stop=True, gaps=None, k_wait=None):
                slot = p % 2
                out = acc[slot if bnk is None else bnk][:, :]
                for k in range(kt):
                    if gaps and k % 2 == 0:
                        gaps(k // 2)
                    if k == 0:
                        if start and bnk is None:
                            pe.wait_ge(acc_free[slot], per // 2 * i + ((base + p) // 2 + 1))
                    if k % (kt // 2) == 0:
                        pe.wait_ge(lo_done, 2 * per * i + (2 * (base + p) + k // (kt // 2) + 1))
                    if k_wait:
                        k_wait(k)
                    wk = slice(k * P, (k + 1) * P)
                    mm = passes(out, w_h[slot][:, wk], w_l[slot][:, wk], xh[:, k0 + k, :], xl[:, k0 + k, :],
                                start and k == 0, stop and k == kt - 1)
                    if (k + 1) % (kt // 2) == 0:
                        mm.then_inc(half_done, 1)

            def column_sums(out, sqt, n):
                for j in range(n):
                    mm = pe.matmul(out[:, j:j + 1], sqt(j), ones[:, 0:1], start=True, stop=True)
                return mm

            pe.wait_ge(sig["cst_in"], 16)
            pe.wait_ge(sig["xsum_ok"], 4)
            column_sums(fb[0][:, 0:NT], lambda j: x_sq[:, 0, P * j:P * j + P], NT).then_inc(sig["xstat_mm"], 1)
            pe.wait_ge(sig["diag_ok"], 1)
            pe.matmul(fb[1][:, :], ones, diag[:, :, :], start=True, stop=True).then_inc(sig["rown_mm"], 1)

            def xn_ready(k):
                pe.wait_ge(sig["nl_done"], k + 1)

            with pe.Fori(0, 2) as i:
                for p in range(H):
                    unit(U_QK, 4, i, p, xn_h, xn_l, KT, k_wait=xn_ready if p == 0 else None)
            pe.wait_ge(sig["wsl_done"], 1)
            for t in range(NT):
                for k in range(KT):
                    ts, ws = slice(t * P, (t + 1) * P), slice(12 * k, 12 * k + 12)
                    o = fb[2][:, 12 * t:12 * t + 12]
                    pe.matmul(o, xn_h[:, k, ts], ws_h[:, ws], start=(k == 0), stop=False)
                    pe.matmul(o, xn_h[:, k, ts], ws_l[:, ws], start=False, stop=False)
                    mm = pe.matmul(o, xn_l[:, k, ts], ws_h[:, ws], start=False, stop=(k == KT - 1))
            mm.then_inc(sig["small_mm"], 1)

            def v_gap(p):
                def gap(q):
                    if p == 1 and q == 0:
                        pe.wait_ge(sig["sq_done"], 2 * H)
                        column_sums(fb[0][:, 0:32],
                                    lambda j: sq[:, 4 * (j // 16) + j % 4, P * (j // 4 % 4):P * (j // 4 % 4) + P],
                                    32).then_inc(sig["stat_mm"], 1)
                    if p == 1 and q == 3:
                        pe.wait_ge(sig["colx"], 1)
                        pe.matmul(fb[1][:, 0:16], cst[:, C_TRI, :], g16[:, :, :], start=True, stop=True)\
                          .then_inc(sig["gc_mm"], 1)
                return gap

            for p in range(H):
                unit(U_V, 4, 0, p, xn_h, xn_l, KT, gaps=v_gap(p))

            def rows(i):
                pe.wait_ge(sig["prep_ok"], i + 1)
                pe.wait_ge(sig["st_ok"], i + 1)
                pe.wait_ge(sig["o_ok"], i + 1)
                pe.matmul(gb[0][:, :], ones, dec[:, :, :], start=True, stop=True)
                pe.matmul(gb[1][:, :], ones, kb[:, :, :], start=True, stop=True)
                pe.matmul(gb[2][:, :], ones, qh[:, :, :], start=True, stop=True).then_inc(sig["rows_mm"], 1)

            def kv_turn(i):
                pe.wait_ge(sig["stage_ok"], 3 * i + 3)
                for h in range(H):
                    pe.transpose(fb[0][:, h * P:(h + 1) * P], stg[:, H + h, :], ident)
                for h in range(H):
                    mm = pe.transpose(fb[1][:, h * P:(h + 1) * P], stg[:, 2 * H + h, :], ident)
                mm.then_inc(sig["kvt_mm"], 1)

            def cum_row(i):
                pe.wait_ge(sig["fprep_ok"], i + 1)
                pe.wait_ge(sig["fxl_ok"], i + 1)
                pe.matmul(fb[2][:, :], ones, fcum[:, :, :], start=True, stop=True).then_inc(sig["cum_mm"], 1)

            def kk(i):
                pe.wait_ge(sig["kb_ok"], i + 1)
                pe.wait_ge(sig["qh_ok"], i + 1)
                for h in range(H):
                    mm = pe.matmul(gb[1][:, h * P:(h + 1) * P], stg[:, H + h, :], kb[:, h, :], start=True, stop=True)
                mm.then_inc(sig["kk_mm"], 1)
                for h in range(H):
                    mm = pe.matmul(gb[2][:, h * P:(h + 1) * P], stg[:, H + h, :], qh[:, h, :], start=True, stop=True)
                mm.then_inc(sig["kq_mm"], 1)

            def k_state(i):
                pe.wait_ge(sig["cum_done"], i + 1)
                for h in range(H):
                    mm = pe.matmul(fb[2][:, h * P:(h + 1) * P], stg[:, H + h, :], state[:, h, :], start=True, stop=True)
                mm.then_inc(sig["ks_mm"], 1)

            def x_turn(i):
                pe.wait_ge(sig["xt0_ok"], i + 1)
                pe.wait_ge(sig["erow_ok"], i + 1)
                for h in range(H):
                    mm = pe.transpose(gb[0][:, h * P:(h + 1) * P], xt[:, h, :], ident)
                mm.then_inc(sig["xtr_mm"], 1)

            def lev_z(lev):
                def go(i):
                    pe.wait_ge(sig["olev_ok"], 6 * i + lev)
                    if lev == 1:
                        pe.wait_ge(sig["xi0_ok"], i + 1)
                    else:
                        pe.wait_ge(sig["xi_ok"], 5 * i + lev - 1)
                    for h in range(H):
                        mm = pe.matmul(gb[0][:, 64 * h:64 * h + 64], olev[lev % 2][:, h, :], half1(xi[:, h, :], lev, 0),
                                       start=True, stop=True)
                    mm.then_inc(sig["z_mm"], 1)
                return go

            def lev_xz(lev):
                def go(i):
                    pe.wait_ge(sig["z_ok"], 6 * i + lev)
                    if lev == 1:
                        pe.wait_ge(sig["at_ok"], i + 1)
                    else:
                        pe.wait_ge(sig["xt_ok"], 6 * i + lev - 1)
                    if lev < NLEV - 1:
                        for h in range(H):
                            pe.matmul(gb[1][:, 64 * h:64 * h + 64], xt[:, h, :], half1(zlev[lev][:, h, :], lev, 0),
                                      start=True, stop=True)
                    for h in range(H):
                        mm = pe.matmul(gb[2][:, 64 * h:64 * h + 64], zlev[lev][:, h, :], half1(xt[:, h, :], lev, 1),
                                       start=True, stop=True)
                    mm.then_inc(sig["xz_mm"], 1)
                return go

            def v_new(i):
                pe.wait_ge(sig["xt_ok"], 6 * i + 6)
                pe.wait_ge(sig["r_ok"], i + 1)
                for h in range(H):
                    mm = pe.matmul(gb[1][:, h * P:(h + 1) * P], xt[:, h, :], vb[:, h, :], start=True, stop=True)
                mm.then_inc(sig["vn_mm"], 1)

            def out_state(i):
                pe.wait_ge(sig["vn_ok"], i + 1)
                pe.wait_ge(sig["qe_ok"], i + 1)
                pe.wait_ge(sig["ktok_ok"], i + 1)
                for h in range(H):
                    o = gb[2][:, h * P:(h + 1) * P]
                    pe.matmul(o, state[:, h, :], erow[:, h, :], start=True, stop=False)
                    mm = pe.matmul(o, vn[:, h, :], at[:, h, :], start=False, stop=True)
                mm.then_inc(sig["o_mm"], 1)
                for h in range(H):
                    mm = pe.matmul(gb[0][:, h * P:(h + 1) * P], ktok[:, h, :], vn[:, h, :], start=True, stop=True)
                mm.then_inc(sig["ds_mm"], 1)

            def fv_turn(i):
                evacuated(pe, U_MIX, 6, i, 2)
                pe.wait_ge(sig["vb_ok"], i + 1)
                for t in range(NT):
                    mm = pe.transpose(fb[1][:, t * P:(t + 1) * P], fv[:, t * P:(t + 1) * P], ident)
                mm.then_inc(sig["fvt_mm"], 1)

            def scores(t):
                def go(i):
                    if t == 0:
                        evacuated(pe, U_MIX, 6, i, 1)
                        evacuated(pe, U_MIX, 6, i, 0)
                        pe.wait_ge(sig["ktok_ok"], i + 1)
                    else:
                        pe.wait_ge(sig["lgt_ok"], 4 * i + t)
                    pe.matmul(fb[0][:, 0:(t + 1) * P], fq[:, t * P:(t + 1) * P], fk[:, 0:(t + 1) * P],
                              start=True, stop=True).then_inc(sig["s_mm"], 1)
                return go

            def p_turn(t):
                def go(i):
                    pe.wait_ge(sig["pn_ok"], 4 * i + t + 1)
                    if t == 0:
                        pe.wait_ge(sig["fvt_ok"], i + 1)
                    else:
                        pe.wait_ge(sig["pt_ok"], 4 * i + t)
                    for j in range(t + 1):
                        mm = pe.transpose(fb[1][:, j * P:(j + 1) * P], pr[t % 2][:, j * P:(j + 1) * P], ident)
                    mm.then_inc(sig["pt_mm"], 1)
                return go

            def p_v(t):
                def go(i):
                    pe.wait_ge(sig["pt_ok"], 4 * i + t + 1)
                    if t == 0:
                        pe.wait_ge(sig["r_ok"], i + 1)
                    for j in range(t + 1):
                        mm = pe.matmul(fb[2][:, t * P:(t + 1) * P], fvt[:, j, :], pt[:, j, :],
                                       start=(j == 0), stop=(j == t))
                    mm.then_inc(sig["pv_mm"], 1)
                return go

            mixer = {
                0: [rows], 1: [kv_turn], 2: [cum_row], 3: [kk], 4: [k_state], 5: [x_turn],
                10: [scores(0)], 12: [scores(1)], 13: [fv_turn], 14: [p_turn(0)], 15: [scores(2), p_v(0)],
                16: [p_turn(1)], 17: [scores(3), p_v(1)], 18: [v_new], 19: [p_turn(2)], 20: [p_v(2), out_state],
                21: [p_turn(3)], 22: [p_v(3)],
            }
            for lev in range(1, NLEV):
                mixer.setdefault(4 + 2 * lev, []).insert(0, lev_z(lev))
                mixer.setdefault(5 + 2 * lev, []).insert(0, lev_xz(lev))

            with pe.Fori(0, H) as i:
                for p in range(6):
                    def gap(q, p=p):
                        for step in mixer.get(4 * p + q, ()):
                            step(i)
                    unit(U_MIX, 6, i, p, xn_h, xn_l, KT, gaps=gap)

            def z_gap(p):
                def gap(q):
                    if p == 1 and q == 0:
                        pe.wait_ge(sig["osq_ok"], H)
                        column_sums(fb[0][:, 0:16], lambda j: osq[:, j // 4, P * (j % 4):P * (j % 4) + P], 16)\
                            .then_inc(sig["ostat_mm"], 1)
                    if p >= 2 and q % 2 == 1:
                        h = 2 * (p - 2) + q // 2
                        pe.wait_ge(sig["odiag_ok"], h + 1)
                        if h >= 2:
                            pe.wait_ge(sig["oa1_ok"], h - 1)
                        pe.matmul(gb[h % 2][:, :], ones, osq[:, h, :], start=True, stop=True).then_inc(sig["orow_mm"], 1)
                return gap

            for p in range(H):
                unit(U_Z, 4, 0, p, xn_h, xn_l, KT, gaps=z_gap(p))

            with pe.Fori(0, KT) as i:
                for p, (bh, bl) in enumerate(((oa_h, oa_l), (sc_h, sc_l), (fx_h, fx_l))):
                    unit(U_BR, 6, i, 2 * p, xn_h, xn_l, KT)
                    if p == 0:
                        pe.wait_ge(sig["oal_ok"], H)
                    unit(U_BR, 6, i, 2 * p + 1, bh, bl, H)
            with pe.Fori(0, KT // 2) as i:
                for p in range(2):
                    if p == 0:
                        pe.wait_ge(sig["mgl_ok"], KT + 1)
                    unit(U_O, 2, i, p, mg_h, mg_l, KT)

            def sums_and_row(n):
                pe.wait_ge(sig["rss_ok"], (KT + 1) * n)
                column_sums(fb[0][:, 0:NT], lambda j: sqsum[:, P * j:P * j + P], NT).then_inc(sig["rstat_mm"], 1)
                pe.wait_ge(sig["diag_ok"], n + 1)
                pe.matmul(fb[1][:, :], ones, diag[:, :, :], start=True, stop=True).then_inc(sig["rown_mm"], 1)

            sums_and_row(1)

            def xn2_ready(k):
                pe.wait_ge(sig["nl_done"], KT + k + 1)

            with pe.Fori(0, KF // 2) as i:
                for p in range(4):
                    unit(U_UP, 4, i, p, xn_h, xn_l, KT, k_wait=xn2_ready if p == 0 else None)
            with pe.Fori(0, KT // 2) as i:
                for p in range(6):
                    if p == 0:
                        pe.wait_ge(sig["f_l"], KF + 2)
                    if p % 3 == 0:
                        pe.wait_ge(acc_free[p // 3], i + (U_DN // 2 + 1))
                    unit(U_DN, 6, i, p, ff_h, ff_l, KDN[p % 3], k0=8 * (p % 3), bnk=p // 3,
                         start=p % 3 == 0, stop=p % 3 == 2)
            sums_and_row(2)

        @block.scalar
        def _(act):
            def hi(base, per, i, p, kt, hf):
                slot, c = p % 2, slice(hf * kt // 2 * P, (hf + 1) * kt // 2 * P)
                if hf == 0:
                    act.wait_ge(raw_in[slot], 8 * per * i + (8 * (base + p - slot) + 16))
                if base + p >= 2:
                    act.wait_ge(half_done, 2 * per * i + (2 * (base + p) - 3 + hf))
                act.copy(w_h[slot][:, c], raw[slot][:, c]).then_inc(hi_done, 1)

            def done(base, per, i, p):
                act.wait_ge(half_done, 2 * per * i + (2 * (base + p) + 2))

            for c in range(4):
                act.wait_ge(xin[c], 16)
                act.activation(x_sq[:, 2 * c:2 * c + 2, :], x_in[:, 2 * c:2 * c + 2, :], ACT.Square)\
                   .then_inc(sig["xsq_done"], 1)
            for p in range(2):
                for hf in range(2):
                    hi(0, 2, 0, p, KT, hf)
            for k in range(KT):
                act.wait_ge(sig["nf_done"], k + 1)
                act.copy(xn_h[:, k, :], (sq2 if k % 2 else sqsum)[:, :]).then_inc(sig["nh_done"], 1)
            act.wait_ge(sig["ws_in"], 16)
            act.copy(ws_h[:, :], ws_raw[:, :]).then_inc(sig["wsh_done"], 1)
            act.wait_ge(sig["prm_in"], 16)
            act.activation(ea[:, :], prm[:, PRM["a_log"]], ACT.Exp).then_inc(sig["ea_ok"], 1)

            def conv_silu(i, p, base, square):
                b = p % 2
                hi(base + 2, 4, i, p, KT, 0)
                if p == 0:
                    act.wait_ge(acc_free[1], 2 * i + (base // 2 + 1))
                    t0 = PRM["conv_qkv"].start
                    k = i if square else 2
                    act.copy(tap4[:, :, :], prm[:, bass.ds(t0 + 4 * H * k, 4 * H)].rearrange("p (h j) -> p h j", j=4))\
                       .then_inc(sig["qt_done"], 1)
                    act.wait_ge(sig["qt_done"], i + (3 if not square else 1))
                done(base, 4, i, p)
                act.activation(cy[b][:, :], acc[b][:, :], ACT.Copy, scale=tap4[:, p, 3:4]).then_inc(sig["qy_tap"], 1)
                hi(base + 2, 4, i, p, KT, 1)
                act.wait_ge(acc_free[b], 2 * i + ((base + p) // 2 + 2))
                act.activation(th[b][:, :], cy[b][:, :], ACT.Tanh, scale=0.5).then_inc(sig["qth_ok"], 1)
                if square:
                    act.wait_ge(sig["q_done"], 4 * i + p + 1)
                    act.activation(sq[:, 4 * i + p, :], qkv[:, 4 * i + p, :], ACT.Square).then_inc(sig["sq_done"], 1)

            with act.Fori(0, 2) as i:
                for p in range(H):
                    conv_silu(i, p, U_QK, True)
            act.wait_ge(sig["colu_ok"], 1)
            act.activation(bet[:, 0, :, :], lg[:, :, 0:H], ACT.Exp, scale=-1.0).then_inc(sig["eb_done"], 1)
            act.activation(spu[:, 1, :, :], spu[:, 0, :, :], ACT.Abs).then_inc(sig["abs_ok"], 1)
            act.wait_ge(sig["abs_ok"], 1)
            act.activation(spu[:, 2, :, :], spu[:, 1, :, :], ACT.Exp, scale=-1.0).then_inc(sig["eb_done"], 1)
            def stage(i, j):
                act.copy(stg[:, H * j:H * j + H, :], qkv[:, H * j:H * j + H, bass.ds(P * i, P)]).then_inc(sig["stage_ok"], 1)

            for p in range(2):
                conv_silu(0, p, U_V, False)
            act.wait_ge(sig["gc_mm"], 1)
            act.copy(gcols[:, :, Q_GC, :], fb[1][:, 0:16].rearrange("p (t h) -> p t h", h=H)).then_inc(sig["gcc_ok"], 1)
            act.activation(ec16[:, :, :], fb[1][:, 0:16].rearrange("p (t h) -> p t h", h=H), ACT.Exp)\
               .then_inc(sig["gcc_ok"], 1)
            for p in (2, 3):
                conv_silu(0, p, U_V, False)
            act.wait_ge(sig["stat_mm"], 1)
            stage(0, 0)
            stage(0, 1)
            act.wait_ge(sig["q_done"], 3 * H)
            stage(0, 2)

            def act_rows(i):
                act.wait_ge(sig["kd0_ok"], i + 1)
                act.activation(kd[:, 1, :], kd[:, 0, :], ACT.Exp).then_inc(sig["kdx_ok"], 1)
                act.activation(kd[:, 2, :], four(gb[0])[:, :, P - 1], ACT.Exp)
                act.activation(erow[:, :, :], four(gb[0]), ACT.Exp).then_inc(sig["erow_ok"], 1)
                act.activation(dec[:, :, :], dec[:, :, :], ACT.Exp).then_inc(sig["dec_ok"], 1)

            def act_cum(i):
                act.wait_ge(sig["cum_mm"], i + 1)
                act.copy(fcum[:, :, :], four(fb[2])).then_inc(sig["cum_done"], 1)

            def act_x(i):
                act.wait_ge(sig["xtr_mm"], i + 1)
                act.copy(xi[:, :, :], four(gb[0])).then_inc(sig["xi0_ok"], 1)

            def act_z(lev):
                def go(i):
                    act.wait_ge(sig["z_mm"], 6 * i + lev)
                    act.copy(half(zlev[lev][:, :, :], lev, 0), packed(gb[0], lev)).then_inc(sig["z_ok"], 1)
                return go

            def act_vn(i):
                act.wait_ge(sig["vn_mm"], i + 1)
                act.copy(vn[:, :, :], four(gb[1])).then_inc(sig["vn_ok"], 1)

            def act_o(i):
                act.wait_ge(sig["o_mm"], i + 1)
                act.copy(ogd[:, :, bass.ds(P * i, P)], four(gb[2])).then_inc(sig["o_ok"], 1)

            def act_fvt(i):
                act.wait_ge(sig["fvt_mm"], i + 1)
                act.copy(fvt[:, :, :], four(fb[1])).then_inc(sig["fvt_ok"], 1)

            def act_exp(t):
                def go(i):
                    act.wait_ge(sig["nmx_ok"], 4 * i + t + 1)
                    n = (t + 1) * P
                    act.activation(pr[t % 2][:, 0:n], pr[t % 2][:, 0:n], ACT.Exp, bias=fst[:, 1, t:t + 1],
                                   accum_out=fst[:, 2, t:t + 1]).then_inc(sig["exp_ok"], 1)
                return go

            def act_pt(t):
                def go(i):
                    act.wait_ge(sig["pt_mm"], 4 * i + t + 1)
                    if t:
                        act.wait_ge(sig["pv_mm"], 4 * i + t)
                    act.copy(pt[:, 0:t + 1, :], four(fb[1])[:, 0:t + 1, :]).then_inc(sig["pt_ok"], 1)
                return go

            def act_fx(i):
                act.wait_ge(sig["pv_mm"], 4 * i + 4)
                act.copy(fx_h[:, i, :], fb[2][:, :]).then_inc(sig["fxh_ok"], 1)

            def act_stage(j):
                def go(i):
                    act.wait_ge((sig["qh_ok"], sig["ks_mm"], sig["kvt_mm"])[j], i + 1)
                    stage((i + 1) % H, j)
                return go

            mixer = {0: [act_rows], 2: [act_cum], 5: [act_x], 14: [act_fvt], 11: [act_exp(0)], 13: [act_exp(1)],
                     15: [act_pt(0)], 16: [act_exp(2)], 17: [act_pt(1)], 18: [act_exp(3), act_vn],
                     20: [act_pt(2), act_o], 22: [act_pt(3)]}
            for lev in range(1, NLEV):
                mixer.setdefault(4 + 2 * lev, []).insert(0, act_z(lev))
            for j in range(3):
                mixer.setdefault(7 + 2 * j, []).append(act_stage(j))

            def act_unit(i, p):
                b = p % 2
                done(U_MIX, 6, i, p)
                if p == 0:
                    act.mul(fq[:, :], acc[b][:, :], HD ** -0.5).then_inc(acc_free[b], 1)
                elif p in (1, 2, 3):
                    act.copy((fk, fv, cs)[p - 1][:, :], acc[b][:, :]).then_inc(acc_free[b], 1)
                hi(U_MIX + 2, 6, i, p, KT, 1)

            with act.Fori(0, H) as i:
                for g in range(24):
                    for step in mixer.get(g, ()):
                        step(i)
                    if g % 4 == 3:
                        hi(U_MIX + 2, 6, i, g // 4, KT, 0)
                    if g % 4 == 0 and g:
                        act_unit(i, g // 4 - 1)
                act_fx(i)
                act_unit(i, 5)
                evacuated(act, U_MIX, 6, i, 5)
                act.copy(sc_h[:, i, :], us[:, :]).then_inc(sig["sch_ok"], 1)

            for h in range(H):
                act.activation(osq[:, h, :], ogd[:, h, :], ACT.Square).then_inc(sig["osq_ok"], 1)
            for p in range(H):
                hi(U_Z + 2, 4, 0, p, H if p == 3 else KT, 0)
                done(U_Z, 4, 0, p)
                hi(U_Z + 2, 4, 0, p, H if p == 3 else KT, 1)
                if p >= 2:
                    evacuated(act, U_Z, 4, 0, p - 2)
                act.activation(zt[p % 2][:, :], acc[p % 2][:, :], ACT.Tanh, scale=0.5).then_inc(sig["zth_ok"], 1)
            for h in range(H):
                act.wait_ge(sig["oa2_ok"], h + 1)
                act.copy(oa_h[:, h, :], ogd[:, h, :]).then_inc(sig["oah_ok"], 1)

            def act_merge(i, last):
                for p in range(6):
                    kt = KT if p % 2 == 0 or (last and p == 5) else H
                    if kt == H or p % 2 == 0:
                        hi(U_BR + 2, 6, i, p, kt, 0)
                    else:
                        done(U_BR, 6, i, p)
                        hi(U_BR + 2, 6, i, p, kt, 0)
                    if p % 2 == 0:
                        done(U_BR, 6, i, p)
                        act.wait_ge(acc_free[1], 3 * i + ((U_BR + p) // 2 + 1))
                        act.activation(tg[:, :], acc[0][:, :], ACT.Tanh, scale=0.5).then_inc(acc_free[0], 1)
                    hi(U_BR + 2, 6, i, p, kt, 1)
                act.wait_ge(sig["m2_ok"], 2 * i + 2)
                act.mul(mg_h[:, i, :], mg[:, :], 0.5).then_inc(sig["mgh_ok"], 1)

            with act.Fori(0, KT - 1) as i:
                act_merge(i, False)
            act_merge(KT - 1, True)

            with act.Fori(0, KT // 2) as i:
                for p in range(2):
                    hi(U_O + 2, 2, i, p, KT, 0)
                    hi(U_O + 2, 2, i, p, KT, 1)
                    evacuated(act, U_O, 2, i, p)
                    act.wait_ge(sig["rss_ok"], 2 * i + p + 1)
                    act.activation(sq2[:, :], res[:, 2 * i + p, :], ACT.Square).then_inc(sig["rsq_ok"], 1)
            for k in range(KT):
                act.wait_ge(sig["nf_done"], KT + k + 1)
                act.copy(xn_h[:, k, :], (sq2 if k % 2 else sqsum)[:, :]).then_inc(sig["nh_done"], 1)

            with act.Fori(0, KF // 2) as i:
                for p in range(4):
                    b = p % 2
                    hi(U_UP + 2, 4, i, p, KT, 0)
                    if p == 0:
                        act.wait_ge(acc_free[1], 2 * i + (U_UP // 2 + 1))
                        t0 = PRM["conv_ffn"].start
                        act.copy(tapf[:, :, :], prm[:, bass.ds(t0 + 12 * i, 12)].rearrange("p (a j) -> p a j", j=3))\
                           .then_inc(sig["f_tap"], 1)
                        act.wait_ge(sig["f_tap"], i + 1)
                    done(U_UP, 4, i, p)
                    act.activation(yc[p][:, :], acc[b][:, :], ACT.Copy, scale=tapf[:, p, 2:3]).then_inc(sig["fy_tap"], 1)
                    hi(U_UP + 2, 4, i, p, KT, 1)
                    if b == 0:
                        evacuated(act, U_UP, 4, i, p)
                        act.activation(yt[p // 2][:, :], yc[p][:, :], ACT.Tanh, scale=0.5).then_inc(sig["fth_ok"], 1)
                    else:
                        act.wait_ge(sig["f_hv"], 2 * i + p // 2 + 1)
                        act.mul(ff_h[:, 2 * i + p // 2, :], hv[p // 2][:, :], 0.5).then_inc(sig["f_h"], 1)

            def down_hi(i, p, hf):
                if hf == 0 and KDN[(p + 2) % 3] > KDN[p % 3]:
                    done(U_DN, 6, i, p)
                hi(U_DN + 2, 6, i, p, KDN[(p + 2) % 3], hf)

            def act_down(i, last):
                for p in range(6):
                    if not (last and p >= 4):
                        down_hi(i, p, 0)
                        down_hi(i, p, 1)
                    if p % 3 == 2:
                        act.wait_ge(acc_free[p // 3], i + (U_DN // 2 + 2))
                        act.wait_ge(sig["rss_ok"], 2 * i + (p // 3 + KT + 2))
                        act.activation(sq2[:, :], res[:, 2 * i + p // 3, :], ACT.Square).then_inc(sig["rsq_ok"], 1)

            with act.Fori(0, KT // 2 - 1) as i:
                act_down(i, False)
            act_down(KT // 2 - 1, True)

        @block.gpsimd
        def _(pool):
            pool.wait_ge(sig["cst_in"], 16)
            for z in zlev[1:] + [state]:
                pool.memset(z[:, :, :], 0.0).then_inc(sig["zer_ok"], 1)

            def prep(i, first):
                if first:
                    pool.wait_ge(sig["gcols_ok"], 1)
                else:
                    pool.wait_ge(sig["at_ok"], i)
                    pool.wait_ge(sig["r_ok"], i)
                    pool.wait_ge(sig["qe_ok"], i)
                pool.tensor_copy(gcs[:, :, :], gcols[:, i, :, :]).then_inc(sig["gcs_ok"], 1)
                pool.tensor_copy(fcs[:, :], fcols[:, i, :]).then_inc(sig["gcs_ok"], 1)
                pool.wait_ge(sig["gcs_ok"], 2 * i + 2)
                pool.tensor_tensor(dec[:, :, :], tiles(cst[:, C_TRI, :]), heads(gcs[:, Q_G, :]), ALU.mult)
                pool.tensor_tensor(kb[:, :, :], tiles(ident), heads(gcs[:, Q_BRK, :]), ALU.mult)
                pool.tensor_tensor(qh[:, :, :], tiles(ident), heads(gcs[:, Q_RQ, :]), ALU.mult).then_inc(sig["prep_ok"], 1)
                if not first:
                    pool.wait_ge(sig["lgt_ok"], 4 * i)
                pool.tensor_tensor(fcum[:, :, :], tiles(cst[:, C_TRI, :]), heads(fcs[:, 0:4]), ALU.mult)\
                    .then_inc(sig["fc_ok"], 1)
                pool.wait_ge(sig["fc_ok"], i + 1)
                pool.tensor_tensor(fcum[:, :, :], fcum[:, :, :], heads(fcs[:, 4:8]), ALU.add).then_inc(sig["fprep_ok"], 1)

            def masks(i):
                pool.wait_ge(sig["lt_ok"], i + 1)
                for lev in range(1, NLEV):
                    if lev > 2:
                        pool.wait_ge(sig["z_mm"], 6 * i + lev - 2)
                    pool.tensor_tensor(olev[lev % 2][:, :, :], lt[:, :, :], tiles(cst[:, C_LEV + lev, :]), ALU.mult)\
                        .then_inc(sig["olev_ok"], 1)

            prep(0, True)
            with pool.Fori(0, H - 1) as i:
                masks(i)
                prep(i + 1, False)
            masks(H - 1)

        @block.vector
        def _(dve):
            links = [0]

            def link(ins):
                links[0] += 1
                ins.then_inc(sig["v_chain"], 1)
                dve.wait_ge(sig["v_chain"], links[0])

            def lo(base, per, i, p, kt, hf):
                slot, c = p % 2, slice(hf * kt // 2 * P, (hf + 1) * kt // 2 * P)
                dve.wait_ge(hi_done, 2 * per * i + (2 * (base + p) + hf + 1))
                dve.tensor_tensor(w_l[slot][:, c], raw[slot][:, c], w_h[slot][:, c].bitcast(F32), ALU.subtract)\
                    .then_inc(lo_done, 1)

            def done(base, per, i, p):
                dve.wait_ge(half_done, 2 * per * i + (2 * (base + p) + 2))

            def rsqrt(y, x, a):
                link(dve.tensor_scalar(a.bitcast(I32), x.bitcast(I32), 1, None, ALU.arith_shift_right))
                link(dve.tensor_scalar(y.bitcast(I32), a.bitcast(I32), -1.0, float(0x5F3759DF), ALU.mult, ALU.add))
                for _ in range(3):
                    link(dve.tensor_tensor(a, y, y, ALU.mult))
                    link(dve.scalar_tensor_tensor(out=a, in0=a, scalar=-0.5, in1=x, op0=ALU.mult, op1=ALU.mult))
                    link(dve.scalar_tensor_tensor(out=y, in0=a, scalar=1.5, in1=y, op0=ALU.add, op1=ALU.mult))

            def token_factors():
                link(dve.tensor_scalar(col[:, 0, :], fb[0][:, 0:NT], 1.0 / D, EPS, ALU.mult, ALU.add))
                rsqrt(col[:, 1, :], col[:, 0, :], col[:, 2, :])
                dve.tensor_tensor(diag[:, :, :], tiles(ident, NT), heads(col[:, 1, :]), ALU.mult).then_inc(sig["diag_ok"], 1)

            def norm_blocks(n, src, gain):
                def low(k):
                    dve.wait_ge(sig["nh_done"], KT * n + k + 1)
                    dve.tensor_tensor(xn_l[:, k, :], (sq2 if k % 2 else sqsum)[:, :], xn_h[:, k, :].bitcast(F32),
                                      ALU.subtract).then_inc(sig["nl_done"], 1)
                dve.wait_ge(sig["rown_mm"], n + 1)
                for k in range(KT):
                    if k >= 2:
                        dve.wait_ge(sig["nl_done"], KT * n + k - 1)
                    g0 = PRM[gain].start + k
                    dve.scalar_tensor_tensor(out=(sq2 if k % 2 else sqsum)[:, :], in0=src[:, k, :], scalar=prm[:, g0:g0 + 1],
                                             in1=fb[1][:, :], op0=ALU.mult, op1=ALU.mult).then_inc(sig["nf_done"], 1)
                    if k:
                        low(k - 1)
                low(KT - 1)

            for j, free in enumerate((acc_free[0], acc_free[1], sig["st_ok"], sig["o_ok"], sig["fxl_ok"], sig["mgl_ok"], sig["f_l"], sig["f_l"])):
                dve.memset(col[:, 3 + j // 4, j % 4:j % 4 + 1], 0.0).then_inc(free, 1)
            for p in range(2):
                for hf in range(2):
                    lo(0, 2, 0, p, KT, hf)
            for c in range(1, 4):
                dve.wait_ge(sig["xsq_done"], c + 1)
                if c > 1:
                    dve.wait_ge(sig["xsum_ok"], c - 1)
                dve.tensor_tensor(x_sq[:, 0:2, :], x_sq[:, 0:2, :], x_sq[:, 2 * c:2 * c + 2, :], ALU.add)\
                    .then_inc(sig["xsum_ok"], 1)
            dve.wait_ge(sig["xsum_ok"], 3)
            dve.tensor_tensor(x_sq[:, 0, :], x_sq[:, 0, :], x_sq[:, 1, :], ALU.add).then_inc(sig["xsum_ok"], 1)
            dve.wait_ge(sig["cst_in"], 16)
            dve.wait_ge(sig["prm_in"], 16)
            dve.wait_ge(sig["xstat_mm"], 1)
            token_factors()
            norm_blocks(0, x_in, "g1")
            dve.wait_ge(sig["wsh_done"], 1)
            dve.tensor_tensor(ws_l[:, :], ws_raw[:, :], ws_h[:, :].bitcast(F32), ALU.subtract).then_inc(sig["wsl_done"], 1)

            def add_tap(y, x, tap, back):
                return dve.scalar_tensor_tensor(out=y[:, back:T], in0=x[:, 0:T - back], scalar=tap, in1=y[:, back:T],
                                                op0=ALU.mult, op1=ALU.add)

            def conv_silu(i, p, base):
                b, u = p % 2, 4 * i + (base + p)
                lo(base + 2, 4, i, p, KT, 0)
                dve.wait_ge(sig["qy_tap"], u + 1)
                for j in (2, 1):
                    add_tap(cy[b], acc[b], tap4[:, p, j:j + 1], 3 - j).then_inc(sig["qc_ok"], 1)
                    dve.wait_ge(sig["qc_ok"], 2 * u + 3 - j)
                add_tap(cy[b], acc[b], tap4[:, p, 0:1], 3).then_inc(acc_free[b], 1)
                lo(base + 2, 4, i, p, KT, 1)
                dve.wait_ge(sig["qth_ok"], u + 1)
                dve.scalar_tensor_tensor(out=qkv[:, 4 * i + (base + p), :], in0=th[b][:, :], scalar=1.0, in1=cy[b][:, :],
                                         op0=ALU.add, op1=ALU.mult).then_inc(sig["q_done"], 1)

            with dve.Fori(0, 2) as i:
                for p in range(H):
                    conv_silu(i, p, U_QK)

            dve.wait_ge(sig["small_mm"], 1)
            link(dve.tensor_copy(lg[:, :, :], fb[2][:, 0:12 * NT].rearrange("p (t c) -> p t c", c=12)))

            def rep(name):
                return prm[:, PRM[name]].unsqueeze(1).broadcast_to([P, NT, H])

            dve.tensor_tensor(spu[:, 0, :, 0:H], lg[:, :, H:2 * H], rep("dt_bias"), ALU.add)
            link(dve.tensor_tensor(spu[:, 0, :, H:], lg[:, :, 2 * H:], rep("fox_bias"), ALU.add))
            link(dve.tensor_scalar(spu[:, 0, :, H:], spu[:, 0, :, H:], -1.0, None, ALU.mult))
            dve.tensor_scalar(spu[:, 3, :, :], spu[:, 0, :, :], 0.0, None, ALU.max).then_inc(sig["colu_ok"], 1)
            dve.wait_ge(sig["eb_done"], 2)
            link(dve.tensor_scalar(bet[:, 1, :, :], bet[:, 0, :, :], 1.0, None, ALU.add))
            link(dve.reciprocal(bet[:, 2, :, :], bet[:, 1, :, :]))
            e, z, w, q = spu[:, 2, :, :], spu[:, 5, :, :], spu[:, 6, :, :], spu[:, 7, :, :]
            link(dve.tensor_scalar(w, e, 2.0, None, ALU.add))
            link(dve.reciprocal(q, w))
            link(dve.tensor_tensor(z, e, q, ALU.mult))
            link(dve.tensor_tensor(w, z, z, ALU.mult))
            link(dve.tensor_scalar(q, w, 1.0 / 17, None, ALU.mult))
            for n in (15, 13, 11, 9, 7, 5, 3):
                link(dve.scalar_tensor_tensor(out=q, in0=q, scalar=1.0 / n, in1=w, op0=ALU.add, op1=ALU.mult))
            link(dve.scalar_tensor_tensor(out=q, in0=q, scalar=1.0, in1=z, op0=ALU.add, op1=ALU.mult))
            sp = spu[:, 4, :, :]
            link(dve.scalar_tensor_tensor(out=sp, in0=q, scalar=2.0, in1=spu[:, 3, :, :], op0=ALU.mult, op1=ALU.add))
            dve.wait_ge(sig["ea_ok"], 1)
            dve.scalar_tensor_tensor(out=g16[:, :, :], in0=sp[:, :, 0:H], scalar=-1.0,
                                     in1=ea[:, :].unsqueeze(1).broadcast_to([P, NT, H]),
                                     op0=ALU.mult, op1=ALU.mult).then_inc(sig["colx"], 1)
            link(dve.tensor_copy(fcols[:, :, 0:NT], sp[:, :, H:].rearrange("p t h -> p h t")))
            link(dve.memset(fcols[:, :, NT:NT + 1], 0.0))
            for t in range(1, NT):
                link(dve.tensor_tensor(fcols[:, :, NT + t:NT + t + 1], fcols[:, :, NT + t - 1:NT + t],
                                       fcols[:, :, t - 1:t], ALU.add))
            conv_silu(0, 0, U_V)
            dve.wait_ge(sig["stat_mm"], 1)
            n2 = [nrm[:, j, :, :, :].rearrange("p a t h -> p (a t h)") for j in range(3)]
            link(dve.tensor_scalar(n2[0], fb[0][:, 0:32], 4.0 * EPS, None, ALU.add))
            rsqrt(n2[1], n2[0], n2[2])
            rq, rk = nrm[:, 1, 0, :, :], nrm[:, 1, 1, :, :]
            link(dve.tensor_scalar(gcols[:, :, Q_RQ, :], rq, HD ** -0.5, None, ALU.mult))
            link(dve.tensor_copy(gcols[:, :, Q_RK, :], rk))
            link(dve.tensor_copy(gcols[:, :, Q_G, :], g16[:, :, :]))
            link(dve.tensor_tensor(gcols[:, :, Q_BRK, :], bet[:, 2, :, :], rk, ALU.mult))
            link(dve.tensor_scalar(gcols[:, :, Q_HB, :], bet[:, 2, :, :], 0.5, None, ALU.mult))
            conv_silu(0, 1, U_V)
            dve.wait_ge(sig["gcc_ok"], 2)
            dve.scalar_tensor_tensor(out=gcols[:, :, Q_NBE, :], in0=gcols[:, :, Q_BRK, :], scalar=-1.0, in1=ec16[:, :, :],
                                     op0=ALU.mult, op1=ALU.mult).then_inc(sig["gcols_ok"], 1)
            for p in (2, 3):
                conv_silu(0, p, U_V)

            def hcol(ap, h):
                return ap[:, h:h + 1]

            def v_rows(i):
                dve.wait_ge(sig["rows_mm"], i + 1)
                for h in range(H):
                    dve.scalar_tensor_tensor(out=dec[:, h, :], in0=gb[0][:, h * P:(h + 1) * P], scalar=gcs[:, Q_GC, h:h + 1],
                                             in1=cst[:, C_NEGT, :], op0=ALU.subtract, op1=ALU.min)
                dve.tensor_tensor(kd[:, 0, :], four(gb[0])[:, :, P - 1], gcs[:, Q_GC, :], ALU.subtract).then_inc(sig["kd0_ok"], 1)
                dve.wait_ge(sig["stage_ok"], 3 * i + 2)
                dve.tensor_tensor(kb[:, :, :], stg[:, H:2 * H, :], four(gb[1]), ALU.mult).then_inc(sig["kb_ok"], 1)
                dve.tensor_tensor(qh[:, :, :], stg[:, 0:H, :], four(gb[2]), ALU.mult).then_inc(sig["qh_ok"], 1)
                dve.wait_ge(sig["kdx_ok"], i + 1)
                dve.tensor_tensor(kd[:, 1, :], kd[:, 1, :], gcs[:, Q_RK, :], ALU.mult).then_inc(sig["kd1_ok"], 1)

            def v_kv(i):
                dve.wait_ge(sig["kvt_mm"], i + 1)
                dve.tensor_tensor(vb[:, :, :], four(fb[1]), heads(gcs[:, Q_HB, :]), ALU.mult).then_inc(sig["vb_ok"], 1)
                dve.wait_ge(sig["kd1_ok"], i + 1)
                dve.tensor_tensor(ktok[:, :, :], four(fb[0]), heads(kd[:, 1, :]), ALU.mult).then_inc(sig["ktok_ok"], 1)

            def rk_decay(dst, b, i):
                for h in range(H):
                    mm = dve.scalar_tensor_tensor(out=dst[:, h, :], in0=gb[b][:, h * P:(h + 1) * P],
                                                  scalar=gcs[:, Q_RK, h:h + 1], in1=dec[:, h, :], op0=ALU.mult, op1=ALU.mult)
                return mm

            def v_kk(i):
                dve.wait_ge(sig["kk_mm"], i + 1)
                dve.wait_ge(sig["dec_ok"], i + 1)
                rk_decay(lt, 1, i).then_inc(sig["lt_ok"], 1)
                dve.wait_ge(sig["lt_ok"], i + 1)
                dve.tensor_tensor(xi[:, :, :], lt[:, :, :], tiles(cst[:, C_LEV, :]), ALU.mult).then_inc(sig["ot0_ok"], 1)
                dve.wait_ge(sig["ot0_ok"], i + 1)
                dve.tensor_tensor(xt[:, :, :], tiles(ident), xi[:, :, :], ALU.subtract).then_inc(sig["xt0_ok"], 1)

            def v_kq(i):
                dve.wait_ge(sig["kq_mm"], i + 1)
                rk_decay(at, 2, i).then_inc(sig["at_ok"], 1)
                dve.wait_ge(sig["erow_ok"], i + 1)
                dve.tensor_tensor(erow[:, :, :], erow[:, :, :], qh[:, :, :], ALU.mult).then_inc(sig["qe_ok"], 1)

            def v_r(i):
                dve.wait_ge(sig["ks_mm"], i + 1)
                for h in range(H):
                    hs = slice(h * P, (h + 1) * P)
                    mm = dve.scalar_tensor_tensor(out=vb[:, h, :], in0=fb[2][:, hs], scalar=gcs[:, Q_NBE, h:h + 1],
                                                  in1=vb[:, h, :], op0=ALU.mult, op1=ALU.add)
                mm.then_inc(sig["r_ok"], 1)

            def v_lev(lev):
                def go(i):
                    dve.wait_ge(sig["xz_mm"], 6 * i + lev)
                    if lev < NLEV - 1:
                        v = half(xi[:, :, :], lev, 0)
                        dve.tensor_tensor(v, v, packed(gb[1], lev), ALU.subtract).then_inc(sig["xi_ok"], 1)
                    v = half(xt[:, :, :], lev, 1)
                    dve.tensor_tensor(v, v, packed(gb[2], lev), ALU.subtract).then_inc(sig["xt_ok"], 1)
                return go

            def v_state(i):
                dve.wait_ge(sig["ds_mm"], i + 1)
                for h in range(H):
                    mm = dve.scalar_tensor_tensor(out=state[:, h, :], in0=state[:, h, :], scalar=kd[:, 2, h:h + 1],
                                                  in1=gb[0][:, h * P:(h + 1) * P], op0=ALU.mult, op1=ALU.add)
                mm.then_inc(sig["st_ok"], 1)

            def v_soft(t):
                def go(i):
                    n, d = (t + 1) * P, slice(t * P, (t + 1) * P)
                    x = pr[t % 2]
                    dve.wait_ge(sig["s_mm"], 4 * i + t + 1)
                    dve.tensor_tensor(x[:, 0:n], fb[0][:, 0:n], fcum[:, 0:t + 1, :].rearrange("p t c -> p (t c)"), ALU.add)\
                        .then_inc(sig["lgt_ok"], 1)
                    dve.wait_ge(sig["lgt_ok"], 4 * i + t + 1)
                    dve.tensor_tensor(x[:, d], x[:, d], cst[:, C_CAUSAL, :], ALU.add).then_inc(sig["msk_ok"], 1)
                    dve.wait_ge(sig["msk_ok"], 4 * i + t + 1)
                    dve.reduce_max(fst[:, 0, t:t + 1], x[:, 0:n], AX_X).then_inc(sig["mx_ok"], 1)
                    dve.wait_ge(sig["mx_ok"], 4 * i + t + 1)
                    dve.tensor_scalar(fst[:, 1, t:t + 1], fst[:, 0, t:t + 1], -1.0, None, ALU.mult).then_inc(sig["nmx_ok"], 1)
                return go

            def v_pn(t):
                def go(i):
                    n = (t + 1) * P
                    dve.wait_ge(sig["exp_ok"], 4 * i + t + 1)
                    dve.reciprocal(fst[:, 3, t:t + 1], fst[:, 2, t:t + 1]).then_inc(sig["ri_ok"], 1)
                    dve.wait_ge(sig["ri_ok"], 4 * i + t + 1)
                    dve.tensor_scalar(pr[t % 2][:, 0:n], pr[t % 2][:, 0:n], fst[:, 3, t:t + 1], None, ALU.mult)\
                        .then_inc(sig["pn_ok"], 1)
                return go

            def v_fx(i):
                dve.wait_ge(sig["fxh_ok"], i + 1)
                dve.tensor_tensor(fx_l[:, i, :], fb[2][:, :], fx_h[:, i, :].bitcast(F32), ALU.subtract)\
                    .then_inc(sig["fxl_ok"], 1)

            mixer = {0: [v_rows], 1: [v_kv], 3: [v_kk], 4: [v_r], 5: [v_kq],
                     10: [v_soft(0)], 12: [v_soft(1)], 11: [v_pn(0)], 14: [v_pn(1)],
                     15: [v_soft(2)], 17: [v_pn(2), v_soft(3)], 19: [v_pn(3)], 20: [v_state]}
            for lev in range(1, NLEV):
                mixer.setdefault(5 + 2 * lev, []).insert(0, v_lev(lev))

            def v_conv(i):
                done(U_MIX, 6, i, 4)
                evacuated(dve, U_MIX, 6, i, 3)
                dve.tensor_tensor(us[:, :], cs[:, :], acc[0][:, :], ALU.mult).then_inc(acc_free[0], 1)
                t0 = PRM["conv_sc"].start
                dve.tensor_copy(tap3[:, :], prm[:, bass.ds(t0 + 3 * i, 3)]).then_inc(sig["sct_ok"], 1)
                dve.wait_ge(sig["sct_ok"], i + 1)
                evacuated(dve, U_MIX, 6, i, 4)
                dve.tensor_scalar(cs[:, :], us[:, :], tap3[:, 2:3], None, ALU.mult).then_inc(sig["scc_ok"], 1)
                for j in (1, 0):
                    dve.wait_ge(sig["scc_ok"], 3 * i + 2 - j)
                    add_tap(cs, us, tap3[:, j:j + 1], 2 - j).then_inc(sig["scc_ok"], 1)

            with dve.Fori(0, H) as i:
                for g in range(24):
                    for step in mixer.get(g, ()):
                        step(i)
                    if g % 4 == 3:
                        lo(U_MIX + 2, 6, i, g // 4, KT, 0)
                    if g % 4 == 0 and g:
                        lo(U_MIX + 2, 6, i, g // 4 - 1, KT, 1)
                    if g == 21:
                        v_conv(i)
                v_fx(i)
                done(U_MIX, 6, i, 5)
                dve.wait_ge(sig["scc_ok"], 3 * i + 3)
                dve.tensor_tensor(us[:, :], cs[:, :], acc[1][:, :], ALU.mult).then_inc(acc_free[1], 1)
                lo(U_MIX + 2, 6, i, 5, KT, 1)
                dve.wait_ge(sig["sch_ok"], i + 1)
                dve.tensor_tensor(sc_l[:, i, :], us[:, :], sc_h[:, i, :].bitcast(F32), ALU.subtract)\
                    .then_inc(sig["scl_ok"], 1)

            def v_z(p):
                lo(U_Z + 2, 4, 0, p, H if p == 3 else KT, 0)
                lo(U_Z + 2, 4, 0, p, H if p == 3 else KT, 1)
                dve.wait_ge(sig["zth_ok"], p + 1)
                dve.scalar_tensor_tensor(out=zg[:, p, :], in0=zt[p % 2][:, :], scalar=1.0, in1=acc[p % 2][:, :],
                                         op0=ALU.add, op1=ALU.mult).then_inc(acc_free[p % 2], 1)

            def v_odiag(h):
                dve.tensor_tensor(osq[:, h, :].rearrange("p (t c) -> p t c", t=NT), tiles(ident), heads(onrm[:, 1, h, :]),
                                  ALU.mult).then_inc(sig["odiag_ok"], 1)

            def v_oa(h):
                dve.wait_ge(sig["orow_mm"], h + 1)
                dve.scalar_tensor_tensor(out=ogd[:, h, :], in0=ogd[:, h, :], scalar=gn_half[:, 0:1], in1=gb[h % 2][:, :],
                                         op0=ALU.mult, op1=ALU.mult).then_inc(sig["oa1_ok"], 1)
                dve.wait_ge(sig["oa1_ok"], h + 1)
                evacuated(dve, U_Z, 4, 0, h)
                dve.tensor_tensor(ogd[:, h, :], ogd[:, h, :], zg[:, h, :], ALU.mult).then_inc(sig["oa2_ok"], 1)

            def v_oal(h):
                dve.wait_ge(sig["oah_ok"], h + 1)
                dve.tensor_tensor(oa_l[:, h, :], ogd[:, h, :], oa_h[:, h, :].bitcast(F32), ALU.subtract)\
                    .then_inc(sig["oal_ok"], 1)

            link(dve.tensor_scalar(gn_half[:, :], prm[:, PRM["gdn_norm"]], 0.5, None, ALU.mult))
            v_z(0)
            dve.wait_ge(sig["ostat_mm"], 1)
            o2 = [onrm[:, j, :, :].rearrange("p h t -> p (h t)") for j in range(3)]
            link(dve.tensor_scalar(o2[0], fb[0][:, 0:16], 1.0 / HD, EPS, ALU.mult, ALU.add))
            rsqrt(o2[1], o2[0], o2[2])
            for h in range(H):
                v_odiag(h)
            v_z(1)
            v_z(2)
            v_oa(0)
            v_oa(1)
            v_z(3)
            v_oa(2)
            v_oa(3)
            for h in range(H):
                v_oal(h)

            def v_merge(i, last):
                for p in range(6):
                    lo(U_BR + 2, 6, i, p, KT if p % 2 == 0 or (last and p == 5) else H, 0)
                    if p % 2:
                        done(U_BR, 6, i, p)
                        evacuated(dve, U_BR, 6, i, p - 1)
                        if p == 1:
                            dve.wait_ge(sig["mgl_ok"], i + 1)
                        dst = mg if p == 1 else mg2
                        dve.scalar_tensor_tensor(out=dst[:, :], in0=tg[:, :], scalar=1.0, in1=acc[1][:, :],
                                                 op0=ALU.add, op1=ALU.mult).then_inc(acc_free[1], 1)
                        if p > 1:
                            evacuated(dve, U_BR, 6, i, p)
                            dve.tensor_tensor(mg[:, :], mg[:, :], mg2[:, :], ALU.add).then_inc(sig["m2_ok"], 1)
                            if p == 3:
                                dve.wait_ge(sig["m2_ok"], 2 * i + 1)
                    lo(U_BR + 2, 6, i, p, KT if p % 2 == 0 or (last and p == 5) else H, 1)
                dve.wait_ge(sig["mgh_ok"], i + 1)
                dve.scalar_tensor_tensor(out=mg_l[:, i, :], in0=mg[:, :], scalar=0.5, in1=mg_h[:, i, :].bitcast(F32),
                                         op0=ALU.mult, op1=ALU.subtract).then_inc(sig["mgl_ok"], 1)

            with dve.Fori(0, KT - 1) as i:
                v_merge(i, False)
            v_merge(KT - 1, True)

            dve.memset(sqsum[:, :], 0.0).then_inc(sig["rss_ok"], 1)
            dve.wait_ge(sig["xres_in"], 16)
            with dve.Fori(0, KT // 2) as i:
                for p in range(2):
                    lo(U_O + 2, 2, i, p, KT, 0)
                    lo(U_O + 2, 2, i, p, KT, 1)
                    done(U_O, 2, i, p)
                    dve.tensor_tensor(res[:, 2 * i + p, :], x_res[:, 2 * i + p, :], acc[p][:, :], ALU.add)\
                        .then_inc(acc_free[p], 1)
                    dve.wait_ge(sig["rsq_ok"], 2 * i + p + 1)
                    dve.tensor_tensor(sqsum[:, :], sqsum[:, :], sq2[:, :], ALU.add).then_inc(sig["rss_ok"], 1)
            dve.wait_ge(sig["rstat_mm"], 1)
            token_factors()
            norm_blocks(1, res, "g2")

            def f_low(n, q):
                dve.wait_ge(sig["f_h"], n + 1)
                dve.scalar_tensor_tensor(out=ff_l[:, n, :], in0=hv[q][:, :], scalar=0.5, in1=ff_h[:, n, :].bitcast(F32),
                                         op0=ALU.mult, op1=ALU.subtract).then_inc(sig["f_l"], 1)

            with dve.Fori(0, KF // 2) as i:
                for p in range(4):
                    b, q, u = p % 2, p // 2, 4 * i + p
                    lo(U_UP + 2, 4, i, p, KT, 0)
                    if p == 2:
                        f_low(2 * i, 0)
                    dve.wait_ge(sig["fy_tap"], u + 1)
                    add_tap(yc[p], acc[b], tapf[:, p, 1:2], 1).then_inc(sig["fc1_ok"], 1)
                    dve.wait_ge(sig["fc1_ok"], u + 1)
                    add_tap(yc[p], acc[b], tapf[:, p, 0:1], 2).then_inc(acc_free[b], 1)
                    lo(U_UP + 2, 4, i, p, KT, 1)
                    if b:
                        dve.wait_ge(sig["fth_ok"], 2 * i + q + 1)
                        dve.scalar_tensor_tensor(out=yc[p - 1][:, :], in0=yt[q][:, :], scalar=1.0, in1=yc[p - 1][:, :],
                                                 op0=ALU.add, op1=ALU.mult).then_inc(sig["f_sg"], 1)
                        dve.wait_ge(sig["f_sg"], 2 * i + q + 1)
                        evacuated(dve, U_UP, 4, i, p)
                        dve.wait_ge(sig["f_l"], 2 * i + q + 1)
                        dve.tensor_tensor(hv[q][:, :], yc[p - 1][:, :], yc[p][:, :], ALU.mult).then_inc(sig["f_hv"], 1)
                f_low(2 * i + 1, 1)

            dve.memset(sqsum[:, :], 0.0).then_inc(sig["rss_ok"], 1)

            def v_down(i, last):
                for p in range(6):
                    if not (last and p >= 4):
                        lo(U_DN + 2, 6, i, p, KDN[(p + 2) % 3], 0)
                        lo(U_DN + 2, 6, i, p, KDN[(p + 2) % 3], 1)
                    if p % 3 == 2:
                        m, b = 2 * i + p // 3, p // 3
                        done(U_DN, 6, i, p)
                        dve.tensor_tensor(res[:, m, :], res[:, m, :], acc[b][:, :], ALU.add).then_inc(acc_free[b], 1)
                        dve.wait_ge(sig["rsq_ok"], m + KT + 1)
                        dve.tensor_tensor(sqsum[:, :], sqsum[:, :], sq2[:, :], ALU.add).then_inc(sig["rss_ok"], 1)

            with dve.Fori(0, KT // 2 - 1) as i:
                v_down(i, False)
            v_down(KT // 2 - 1, True)

            dve.wait_ge(sig["rstat_mm"], 2)
            token_factors()
            dve.wait_ge(sig["rown_mm"], 3)
            for k in range(KT):
                g0 = PRM["gf"].start + k
                dve.scalar_tensor_tensor(out=res[:, k, :], in0=res[:, k, :], scalar=prm[:, g0:g0 + 1], in1=fb[1][:, :],
                                         op0=ALU.mult, op1=ALU.mult).then_inc(sig["out_ok"], 1)


def kernel(x, norm1_g, w_in, conv_qkv, a_log, dt_bias, gdn_norm, w_br_a, conv_sc, w_br_b, fox_bias, w_br_c, w_o,
           norm2_g, w_up, conv_ffn, w_down, norm_f):
    import numpy as np
    import concourse.bacc as bacc
    from concourse import mybir
    from concourse.bass_utils import run_bass_kernel_spmd

    def blocks(w, kt):
        n = w.shape[1] // P
        return w.reshape(kt, P, n, P).transpose(2, 1, 0, 3).reshape(n, P, kt * P)

    def columns(v):
        return v.reshape(-1, P).T

    def tap_columns(v, kinds):
        taps = v.shape[0]
        return v.reshape(taps, kinds, -1, P).transpose(3, 2, 1, 0).reshape(P, -1)

    w_in = w_in[0]
    W = H * HD
    at = [0]

    def take(n):
        at[0] += n
        return w_in[:, at[0] - n:at[0]]

    qkv_a, z_a, beta, alog, bch, qkv_c, flog, gates = (
        take(3 * W), take(W), take(H), take(H), take(3 * W), take(3 * W), take(H), take(3 * D))

    def part(a, j, n):
        return a[:, j * n:(j + 1) * n]

    mix = [blocks(part(qkv_c, 0, W), KT), blocks(part(qkv_c, 1, W), KT), blocks(part(qkv_c, 2, W), KT),
           blocks(part(bch, 1, W), KT), blocks(part(bch, 2, W), KT), blocks(part(bch, 0, W), KT)]
    idx = np.arange(P)
    row, colm = idx[:, None], idx[None, :]
    consts = np.zeros((P, NCONST, P), np.float32)
    consts[:, C_ID] = row == colm
    consts[:, C_ONE] = 1.0
    consts[:, C_TRI] = row <= colm
    consts[:, C_NEGT] = np.where(colm >= row, 0.0, NEG)
    consts[:, C_CAUSAL] = np.where(colm <= row, 0.0, NEG)
    for lev in range(NLEV):
        b = 1 << lev
        consts[:, C_LEV + lev] = (row // (2 * b) == colm // (2 * b)) & (row % (2 * b) < b) & (colm % (2 * b) >= b)

    def everywhere(v):
        return np.broadcast_to(v, (P, v.shape[-1]))

    params = np.concatenate([
        columns(norm1_g[0]), columns(norm2_g[0]), columns(norm_f), tap_columns(conv_qkv[0], 1),
        tap_columns(conv_sc[0], 1), tap_columns(conv_ffn[0], 2), columns(gdn_norm[0]),
        everywhere(a_log), everywhere(dt_bias), everywhere(fox_bias)], axis=1)
    w_small = np.concatenate([beta, alog, flog], axis=1).reshape(KT, P, 12).transpose(1, 0, 2).reshape(P, KT * 12)
    arrays = {
        "xT": x[0].T,
        "consts": consts.reshape(P, NCONST * P),
        "params": params,
        "w_small": w_small,
        "w_qkv": blocks(qkv_a, KT),
        "w_mix": np.stack(mix, axis=1).reshape(6 * H, P, KT * P),
        "w_z": blocks(z_a, KT),
        "w_gate": np.stack([blocks(part(gates, j, D), KT) for j in range(3)], axis=1).reshape(3 * KT, P, KT * P),
        "w_br": np.stack([blocks(w[0], H) for w in (w_br_a, w_br_b, w_br_c)], axis=1).reshape(3 * KT, P, H * P),
        "w_o": blocks(w_o[0], KT),
        "w_up": np.stack([blocks(part(w_up[0], j, FF), KT) for j in range(2)], axis=1).reshape(2 * KF, P, KT * P),
        "w_dn": blocks(w_down[0], KF),
    }
    arrays = {n: np.ascontiguousarray(a) for n, a in arrays.items()}
    nc = bacc.Bacc("TRN2", target_bir_lowering=False, num_devices=1)
    args = [nc.dram_tensor(n, a.shape, mybir.dt.from_np(a.dtype), kind="ExternalInput").ap() for n, a in arrays.items()]
    outT = nc.dram_tensor("outT", (D, T), mybir.dt.float32, kind="ExternalOutput").ap()
    build(nc, *args, outT)
    r = run_bass_kernel_spmd(nc, [arrays], core_ids=[0])
    return np.ascontiguousarray(r.results[0]["outT"].T)[None]
```

```python
from contextlib import ExitStack

import numpy as np

import concourse.bass as bass
from concourse import mybir

ALU = mybir.AluOpType
ACT = mybir.ActivationFunctionType
F32 = mybir.dt.float32
F32R = mybir.dt.float32r
I32 = mybir.dt.int32
AX_X = mybir.AxisListType.X

P = 128
D = 1024
T = 512
KT = D // P
NT = T // P
H = 4
HD = 128
FF = 2816
KF = FF // P
EPS = 1e-6
NLEV = 7
NEG = -1.0e30
WARM = 4

U_QK = 0
U_V = U_QK + 2 * H
U_MIX = U_V + H
U_Z = U_MIX + 6 * H
U_BR = U_Z + H
U_O = U_BR + 6 * KT
U_UP = U_O + KT
U_DN = U_UP + 2 * KF
KDN = (8, 8, KF - 16)

C_ID, C_ONE, C_TRI, C_NEGT, C_CAUSAL, C_LEV = 0, 1, 2, 3, 4, 5
NCONST = C_LEV + NLEV

PRM = {}
_at = 0
for _n, _w in (("g1", KT), ("g2", KT), ("gf", KT), ("conv_qkv", 3 * H * 4), ("conv_sc", H * 3),
               ("conv_ffn", KF * 2 * 3), ("gdn_norm", 1), ("a_log", H), ("dt_bias", H), ("fox_bias", H)):
    PRM[_n] = slice(_at, _at + _w)
    _at += _w
NPRM = _at

Q_G, Q_BRK, Q_RQ, Q_RK, Q_GC, Q_NBE, Q_HB = range(7)


def build(nc, xT, consts, params, w_small, w_qkv, w_mix, w_z, w_gate, w_br, w_o, w_up, w_dn, outT):
    ctx = ExitStack()
    with ctx:
        def sb(name, shape, dt=F32, scope=ctx):
            return scope.enter_context(nc.sbuf_tensor(name, shape, dt))

        def bank(name):
            return ctx.enter_context(nc.psum_tensor(name, [P, 512], F32))

        def sem(name):
            return ctx.enter_context(nc.semaphore(name))

        cst = sb("cst", [P, NCONST, P])
        prm = sb("prm", [P, NPRM])
        raw = [sb(f"raw{s}", [P, KT * P]) for s in range(2)]
        w_h = [sb(f"w_h{s}", [P, KT * P], F32R) for s in range(2)]
        w_l = [sb(f"w_l{s}", [P, KT * P], F32R) for s in range(2)]
        xn_h = sb("xn_h", [P, KT, T], F32R)
        xn_l = sb("xn_l", [P, KT, T], F32R)
        ws_raw = sb("ws_raw", [P, KT * 12])
        ws_h = sb("ws_h", [P, KT * 12], F32R)
        ws_l = sb("ws_l", [P, KT * 12], F32R)
        col = sb("col", [P, 8, NT])
        s_norm = ExitStack()
        diag = sb("diag", [P, NT, P], F32, s_norm)
        sqsum = sb("sqsum", [P, T], F32, s_norm)
        sq2 = sb("sq2", [P, T], F32, s_norm)
        s_norm.close()
        row_lo = [sb(f"row_lo{j}", [P, H, P], F32R) for j in range(3)]
        rms_row = sb("rms_row", [P, T])
        ones_r = sb("ones_r", [P, P], F32R)
        ident = cst[:, C_ID, :]
        ones = cst[:, C_ONE, :]

        s_xg = ExitStack()
        xg_h = sb("xg_h", [P, KT, T], F32R, s_xg)
        xg_l = sb("xg_l", [P, KT, T], F32R, s_xg)
        s_xg.close()

        s_br = ExitStack()
        sc_h = sb("sc_h", [P, H, T], F32R, s_br)
        sc_l = sb("sc_l", [P, H, T], F32R, s_br)
        fx_h = sb("fx_h", [P, H, T], F32R, s_br)
        fx_l = sb("fx_l", [P, H, T], F32R, s_br)
        ogd = sb("ogd", [P, H, T], F32, s_br)

        s_mix = ExitStack()
        qkv = sb("qkv", [P, 3 * H, T], F32, s_mix)
        lg = sb("lg", [P, NT, 12], F32, s_mix)
        spu = sb("spu", [P, 8, NT, 2 * H], F32, s_mix)
        ea = sb("ea", [P, H], F32, s_mix)
        bet = sb("bet", [P, 3, NT, H], F32, s_mix)
        g16 = sb("g16", [P, NT, H], F32, s_mix)
        ec16 = sb("ec16", [P, NT, H], F32, s_mix)
        nrm = sb("nrm", [P, 3, 2, NT, H], F32, s_mix)
        gcols = sb("gcols", [P, NT, 7, H], F32, s_mix)
        fcols = sb("fcols", [P, H, 8], F32, s_mix)
        gch = sb("gch", [P, NT, 3, H], F32R, s_mix)
        gcl = sb("gcl", [P, NT, 3, H], F32R, s_mix)
        s_qkv = ExitStack()
        sq = sb("sq", [P, 2 * H, T], F32, s_qkv)
        cy = [sb(f"cy{s}", [P, T], F32, s_qkv) for s in range(2)]
        th = [sb(f"th{s}", [P, T], F32, s_qkv) for s in range(2)]
        lgt = sb("lgt", [P, T], F32, s_qkv)
        yq = [sb(f"yq{s}", [P, T], F32, s_qkv) for s in range(2)]
        x_in = sb("x_in", [P, KT, T], F32, s_qkv)
        x_sq = sb("x_sq", [P, KT, T], F32, s_qkv)
        s_qkv.close()
        gcs = sb("gcs", [P, 7, H], F32, s_mix)
        kd = sb("kd", [P, 3, H], F32, s_mix)
        stg = sb("stg", [P, 3 * H, P], F32, s_mix)
        s_rows = ExitStack()
        dec = sb("dec", [P, H, P], F32, s_rows)
        kb = sb("kb", [P, H, P], F32, s_rows)
        qh = sb("qh", [P, H, P], F32, s_rows)
        s_rows.close()
        row_hi = [sb(f"row_hi{j}", [P, H, P], F32R, s_mix) for j in range(3)]
        erow = sb("erow", [P, H, P], F32, s_mix)
        lt = sb("lt", [P, H, P], F32, s_mix)
        at = sb("at", [P, H, P], F32, s_mix)
        olev = [sb(f"olev{s}", [P, H, P], F32, s_mix) for s in range(2)]
        xi = sb("xi", [P, H, P], F32, s_mix)
        xt = sb("xt", [P, H, P], F32, s_mix)
        fq = sb("fq", [P, T], F32, s_mix)
        fk = sb("fk", [P, T], F32, s_mix)
        fv = sb("fv", [P, T], F32, s_mix)
        zlev = [None] + [sb(f"zlev{s}", [P, H, P], F32, s_mix) for s in range(1, NLEV)]
        ktok = sb("ktok", [P, H, P], F32, s_mix)
        vb = sb("vb", [P, H, P], F32, s_mix)
        vn = sb("vn", [P, H, P], F32, s_mix)
        state = sb("state", [P, H, P], F32, s_mix)
        fvt = sb("fvt", [P, NT, P], F32, s_mix)
        fcs = sb("fcs", [P, 8], F32, s_mix)
        fcum = sb("fcum", [P, NT, P], F32, s_mix)
        pr = [sb(f"pr{s}", [P, T], F32, s_mix) for s in range(2)]
        pt = sb("pt", [P, NT, P], F32, s_mix)
        fst = sb("fst", [P, 4, NT], F32, s_mix)
        cs = sb("cs", [P, T], F32, s_mix)
        us = sb("us", [P, T], F32, s_mix)
        tap3 = sb("tap3", [P, 3], F32, s_mix)
        s_mix.close()

        s_bp = ExitStack()
        zg = sb("zg", [P, H, T], F32, s_bp)
        oa_h = sb("oa_h", [P, H, T], F32R, s_bp)
        oa_l = sb("oa_l", [P, H, T], F32R, s_bp)
        osq = sb("osq", [P, H, T], F32, s_bp)
        gn_half = sb("gn_half", [P, 1], F32, s_bp)
        onrm = sb("onrm", [P, 4, H, NT], F32, s_bp)
        zt = [sb(f"zt{s}", [P, T], F32, s_bp) for s in range(2)]
        tg = sb("tg", [P, T], F32, s_bp)
        mg = sb("mg", [P, T], F32, s_bp)
        mg2 = sb("mg2", [P, T], F32, s_bp)
        mg_h = sb("mg_h", [P, KT, T], F32R, s_bp)
        mg_l = sb("mg_l", [P, KT, T], F32R, s_bp)
        x_res = sb("x_res", [P, KT, T], F32, s_bp)
        rsg = [sb(f"rsg{s}", [P, T], F32, s_bp) for s in range(2)]
        s_bp.close()
        s_br.close()

        res = sb("res", [P, KT, T])
        ff_h = sb("ff_h", [P, KF, T], F32R)
        ff_l = sb("ff_l", [P, KF, T], F32R)
        yr = [sb(f"yr{s}", [P, T]) for s in range(2)]
        yc = [sb(f"yc{s}", [P, T]) for s in range(4)]
        yt = [sb(f"yt{s}", [P, T]) for s in range(2)]
        hv = [sb(f"hv{s}", [P, T]) for s in range(2)]
        tapf = sb("tapf", [P, 4, 3])

        acc = [bank(f"acc{s}") for s in range(2)]
        gb = [bank(f"gb{s}") for s in range(3)]
        fb = [bank(f"fb{s}") for s in range(3)]

        raw_in = [[sem(f"raw_in{s}{hf}") for hf in range(2)] for s in range(2)]
        hi_done = sem("hi_done")
        lo_done = sem("lo_done")
        half_done = sem("half_done")
        acc_free = [sem(f"acc_free{b}") for b in range(2)]
        signals = {
            "cst_in": "constant tiles landed", "prm_in": "parameters landed", "ws_in": "narrow columns' weights landed",
            "xres_in": "the input landed again, for the residual", "zeros_ok": "zeros for the warm-up products",
            "ones_ok": "ones as float32r", "v_chain": "VectorE's own: links of straight chains of small steps",
            "xgh_ok": "hi of input x gain, per block", "xg_ok": "lo of input x gain, per block",
            "xsq_pool": "squares by GpSimd, per chunk", "xsq_act": "squares by ScalarE", "xsq_dve": "squares by VectorE",
            "xsum_pool": "first half's squares added", "xsum_ok": "all squares added to two tiles",
            "nv_done": "input x row of factors, per block (GpSimd)",
            "nh_done": "hi of the normalised input, later of the residual x gain, per block",
            "nl_done": "lo of the same, per block",
            "rstat_mm": "column sums of squares", "diag_ok": "diagonal tiles of 1 / rms",
            "rown_mm": "row of 1 / rms, in fb[1]", "row_ok": "that row in rms_row",
            "rsq_ok": "squares of a residual block", "rss_ok": "running sum of squares (once more when cleared)",
            "rsg_ok": "residual block x gain",
            "gb0_free": "times gb[0] was evacuated", "gb1_free": "times gb[1] was evacuated",
            "fb1_free": "fb[1] evacuated", "qy_tap": "first tap (ScalarE)", "qc_ok": "taps between, two per unit",
            "qy_ok": "last tap of a unit of q or k", "qth_ok": "tanh(y / 2)", "q_done": "2 silu(y)",
            "sq_done": "squares of q or k", "wsh_done": "hi of the narrow weights",
            "wsl_done": "lo of the narrow weights",
            "small_mm": "narrow products", "small_cp": "their copy out of the bank", "small_tr": "turned to columns",
            "colu_ok": "softplus arguments", "eb_done": "exp(-beta), then exp(-|u|)", "abs_ok": "|u|",
            "ea_ok": "exp(a_log)", "colx": "log decays", "gc_mm": "their sums within the chunk",
            "gcc_ok": "those sums, then their exp", "stat_mm": "sums of squares, one of the eight heads of q and k",
            "gcl_ok": "hi and lo of the log decay, then of the other two row columns", "gcols_ok": "all columns",
            "gcs_ok": "columns of the chunk, of the attention head", "prep_ok": "right sides of the rows",
            "rows_mm": "rows of cumulated decay, beta / |k|, 1 / |q|",
            "kd0_ok": "decay to the chunk's end, exponent (bank 0 read)", "kdx_ok": "its exp", "kd1_ok": "its exp / |k|",
            "erow_ok": "exp of the decay row", "dec_ok": "decay matrix", "kb_ok": "k x beta / |k|", "qh_ok": "q / |q|",
            "stage_ok": "q, k, v of the chunk, three per chunk", "kvt_mm": "k and v turned",
            "vb_ok": "beta v, token-major", "ktok_ok": "k decayed to the chunk's end, token-major", "kk_mm": "k k^T",
            "kq_mm": "k q^T", "lt_ok": "strict triangle, transposed", "at_ok": "decayed k q^T",
            "qe_ok": "q x exp of its decay", "ks_mm": "k x state", "r_ok": "right side of the triangular system",
            "ot0_ok": "level 0 of the triangle", "xt0_ok": "X^T after level 0", "xtr_mm": "X of it, in the bank",
            "xi0_ok": "X after level 0", "olev_ok": "the triangle's part of a level, six per chunk",
            "z_mm": "O X of a level, six", "z_ok": "its copy, six", "xz_mm": "X Z and Z^T X^T of a level, six",
            "xi_ok": "X of a level, five", "xt_ok": "X^T of a level, six", "vn_mm": "new values", "vn_ok": "their copy",
            "o_mm": "outputs", "o_ok": "their copy (starts at 1)", "ds_mm": "state update",
            "st_ok": "state (starts at 1)",
            "fc_ok": "right side of the forget row, within tiles", "fprep_ok": "with the tiles before",
            "cum_mm": "forget row", "cum_done": "its copy", "fvt_mm": "v turned", "fvt_ok": "its copy",
            "s_mm": "scores of a query tile, four per head as all below", "lgt_ok": "with the forget row added",
            "msk_ok": "masked", "mx_ok": "row maximum", "nmx_ok": "minus it", "exp_ok": "exp and row sum",
            "ri_ok": "1 / row sum", "pn_ok": "probabilities", "pt_mm": "turned", "pt_ok": "their copy",
            "pv_mm": "times v", "fxh_ok": "hi of the head's output (once)", "fxl_ok": "lo of it (once; starts at 1)",
            "sct_ok": "taps", "scc_ok": "first tap, then the others, three per group", "sch_ok": "hi of the gated output",
            "scl_ok": "lo of it",
            "osq_ok": "squares", "ostat_mm": "their sums", "odiag_ok": "diagonal tiles of 1 / rms",
            "orow_mm": "row of 1 / rms", "zth_ok": "tanh(z / 2)", "oa1_ok": "normalised output",
            "oa2_ok": "times silu(z)", "oah_ok": "hi of it", "oal_ok": "lo of it",
            "m2_ok": "second, then third branch added", "mgh_ok": "hi of the merged rows",
            "mgl_ok": "lo of them (starts at 1)",
            "f_tap": "taps of four units", "fy_tap": "first tap of a unit", "fc1_ok": "second tap",
            "fy_ok": "third tap (starts at 1)", "fth_ok": "tanh(gate / 2) of a pair", "f_sg": "2 silu(gate)",
            "f_hv": "twice the hidden rows", "f_h": "hi of them", "f_l": "lo of them (starts at 2)",
            "out_ok": "normalised block", "out_st": "block stored",
        }
        sig = {name: sem(name) for name in signals}
        xin = [sem(f"xin{c}") for c in range(4)]

        qkv_bank = [(acc[0], acc_free[0]), (acc[1], acc_free[1]), (gb[0], sig["gb0_free"]), (gb[1], sig["gb1_free"])] * 2\
            + [(acc[0], acc_free[0]), (acc[1], acc_free[1]), (gb[1], sig["gb1_free"]), (fb[1], sig["fb1_free"])]

        def freed(u):
            return (4 if u % 4 < 2 else 0) + sum(qkv_bank[w][1] is qkv_bank[u][1] for w in range(u))

        obank = gb + fb[1:2]

        block = ctx.enter_context(nc.Block())

        def heads(ap):
            return ap.unsqueeze(2).broadcast_to([P, ap.shape[1], P])

        def tiles(ap, n=H):
            return ap.unsqueeze(1).broadcast_to([P, n, P])

        def four(b):
            return b[:, :].rearrange("p (h c) -> p h c", h=H)

        def half(ap, lev, up):
            v = ap.rearrange("p h (g two b) -> p (h g) two b", two=2, b=1 << lev)
            return v[:, :, up, :]

        def half1(ap, lev, up):
            v = ap.rearrange("p (g two b) -> p g two b", two=2, b=1 << lev)
            return v[:, :, up, :]

        def packed(b, lev):
            return b[:, 0:H * 64].rearrange("p (g b) -> p g b", b=1 << lev)

        def evacuated(eng, base, per, i, p):
            eng.wait_ge(acc_free[p % 2], per // 2 * i + ((base + p) // 2 + 2))

        @block.sync
        def _(sp):
            def fetch(slot, src, kt, split=None, longer=False):
                for hf in range(2):
                    if split is not None:
                        sp.wait_ge(lo_done, split + (1 if hf or longer else 0))
                    c = slice(hf * kt // 2 * P, (hf + 1) * kt // 2 * P)
                    sp.dma_start(raw[slot][:, c], src[:, c]).then_inc(raw_in[slot][hf], 16)

            xv = xT.rearrange("(c k p) t -> c p k t", c=4, p=P)
            sp.dma_start(prm[:, :], params).then_inc(sig["prm_in"], 16)
            fetch(0, w_qkv[0], KT)
            for c in range(4):
                sp.dma_start(x_in[:, 2 * c:2 * c + 2, :], xv[c]).then_inc(xin[c], 16)
            fetch(1, w_qkv[1], KT)
            sp.dma_start(cst[:, :, :], consts.rearrange("p (n c) -> p n c", c=P)).then_inc(sig["cst_in"], 16)
            sp.dma_start(ws_raw[:, :], w_small).then_inc(sig["ws_in"], 16)
            with sp.Fori(1, 6) as i:
                for p in range(2):
                    fetch(p, w_qkv[2 * i + p], KT, 4 * i + (2 * p - 3))
            with sp.Fori(0, 12) as i:
                for p in range(2):
                    fetch(p, w_mix[2 * i + p], KT, 4 * i + (2 * (U_MIX + p) - 3))
            for i in range(H):
                fetch(i % 2, w_z[i], KT, 2 * (U_Z + i) - 3)
            sp.wait_ge(sig["fxl_ok"], H + 1)
            sp.wait_ge(sig["scl_ok"], H)
            sp.wait_ge(sig["st_ok"], H + 1)
            sp.dma_start(x_res[:, :, :], xT.rearrange("(k p) t -> p k t", p=P)).then_inc(sig["xres_in"], 16)
            with sp.Fori(0, KT) as i:
                for p in range(3):
                    fetch(0, w_gate[3 * i + p], KT, 12 * i + (2 * (U_BR + 2 * p) - 3))
                    fetch(1, w_br[3 * i + p], H, 12 * i + (2 * (U_BR + 2 * p) - 1))
            with sp.Fori(0, KT // 2) as i:
                for p in range(2):
                    fetch(p, w_o[2 * i + p], KT, 4 * i + (2 * (U_O + p) - 3), longer=p == 1)
            with sp.Fori(0, KF) as i:
                for p in range(2):
                    fetch(p, w_up[2 * i + p], KT, 4 * i + (2 * (U_UP + p) - 3))
            with sp.Fori(0, KT // 2) as i:
                for p in range(6):
                    k0 = 8 * (p % 3)
                    fetch(p % 2, w_dn[2 * i + p // 3][:, k0 * P:(k0 + KDN[p % 3]) * P], KDN[p % 3],
                          12 * i + (2 * (U_DN + p) - 3), longer=KDN[p % 3] > KDN[(p + 1) % 3])
            for k in range(KT):
                sp.wait_ge(sig["out_ok"], k + 1)
                sp.dma_start(outT[k * P:(k + 1) * P, :], res[:, k, :]).then_inc(sig["out_st"], 16)
            sp.wait_ge(sig["out_st"], 16 * KT)

        @block.tensor
        def _(pe):
            def passes(out, wh, wl, xh, xl, start, stop):
                pe.matmul(out, wh, xh, start=start, stop=False)
                pe.matmul(out, wh, xl, start=False, stop=False)
                return pe.matmul(out, wl, xh, start=False, stop=stop)

            def unit(base, per, i, p, xh, xl, kt, k0=0, bnk=None, start=True, stop=True, gaps=None, k_wait=None, out=None):
                slot = p % 2
                own = out is None and bnk is None
                out = acc[slot if bnk is None else bnk][:, :] if out is None else out
                for k in range(kt):
                    if gaps and k % 2 == 0:
                        gaps(k // 2)
                    if k == 0:
                        if own:
                            pe.wait_ge(acc_free[slot], per // 2 * i + ((base + p) // 2 + 1))
                    if k % (kt // 2) == 0:
                        pe.wait_ge(lo_done, 2 * per * i + (2 * (base + p) + k // (kt // 2) + 1))
                    if k_wait:
                        k_wait(k)
                    wk = slice(k * P, (k + 1) * P)
                    mm = passes(out, w_h[slot][:, wk], w_l[slot][:, wk], xh[:, k0 + k, :], xl[:, k0 + k, :],
                                start and k == 0, stop and k == kt - 1)
                    if (k + 1) % (kt // 2) == 0:
                        mm.then_inc(half_done, 1)

            def column_sums(out, sqt, n):
                for j in range(n):
                    mm = pe.matmul(out[:, j:j + 1], sqt(j), ones[:, 0:1], start=True, stop=True)
                return mm

            pe.wait_ge(sig["zeros_ok"], 1)
            for _ in range(WARM):
                pe.matmul(fb[2][:, :], rms_row[:, 0:P], rms_row[:, :], start=True, stop=True)

            def xg_ready(k):
                pe.wait_ge(sig["xg_ok"], k + 1)

            def input_gap(p):
                def gap(q):
                    if p == 1 and q == 3:
                        pe.wait_ge(sig["cst_in"], 16)
                        pe.wait_ge(sig["xsum_ok"], 1)
                        for j in range(NT):
                            for a in range(2):
                                mm = pe.matmul(fb[0][:, j:j + 1], x_sq[:, a, P * j:P * j + P], ones[:, 0:1],
                                               start=a == 0, stop=a == 1)
                        mm.then_inc(sig["rstat_mm"], 1)
                    if p == 2 and q == 3:
                        token_row(0)
                    if p >= 4 and q == 2:
                        square_sums(p - 4)
                return gap

            def token_row(n):
                pe.wait_ge(sig["diag_ok"], n + 1)
                pe.matmul(fb[1][:, :], ones, diag[:, :, :], start=True, stop=True).then_inc(sig["rown_mm"], 1)

            def qkv_unit(u, xh, xl, gaps, k_wait=None):
                if freed(u):
                    pe.wait_ge(qkv_bank[u][1], freed(u))
                unit(U_QK, 2, 0, u, xh, xl, KT, out=qkv_bank[u][0][:, :], k_wait=k_wait, gaps=gaps)

            def square_sums(u):
                pe.wait_ge(sig["sq_done"], u + 1)
                for t in range(NT):
                    c = 4 * H * (u // H) + H * t + u % H
                    mm = pe.matmul(fb[0][:, c:c + 1], sq[:, u, P * t:P * (t + 1)], ones[:, 0:1], start=True, stop=True)
                mm.then_inc(sig["stat_mm"], 1)

            for u in range(U_V):
                qkv_unit(u, xg_h, xg_l, input_gap(u), xg_ready if u == 0 else None)
            pe.wait_ge(sig["wsl_done"], 1)
            for k in range(KT):
                pe.wait_ge(sig["nl_done"], k + 1)
                if k == 4:
                    square_sums(4)
                ws = slice(12 * k, 12 * k + 12)
                mm = passes(fb[2][0:12, :], ws_h[:, ws], ws_l[:, ws], xn_h[:, k, :], xn_l[:, k, :], k == 0, k == KT - 1)
            mm.then_inc(sig["small_mm"], 1)

            def v_gap(p):
                def gap(q):
                    if p == 0 and q == 1:
                        pe.wait_ge(sig["small_cp"], 1)
                        pe.wait_ge(sig["gb0_free"], 2)
                        for t in range(NT):
                            mm = pe.transpose(gb[0][:, 12 * t:12 * t + 12], lgt[0:12, t * P:(t + 1) * P],
                                              ident[0:12, 0:12])
                        mm.then_inc(sig["small_tr"], 1)
                    if (p, q) in ((0, 2), (0, 3), (1, 1)):
                        square_sums({2: 5, 3: 6, 1: 7}[q])
                    if p == 2 and q == 1:
                        pe.wait_ge(sig["colx"], 1)
                        pe.matmul(fb[2][:, 0:16], cst[:, C_TRI, :], g16[:, :, :], start=True, stop=True)\
                          .then_inc(sig["gc_mm"], 1)
                return gap

            for p in range(H):
                qkv_unit(U_V + p, xn_h, xn_l, v_gap(p))

            pe.wait_ge(sig["ones_ok"], 1)
            def rows(i):
                pe.wait_ge(sig["prep_ok"], i + 1)
                pe.wait_ge(sig["gb1_free"], 3)
                pe.wait_ge(sig["st_ok"], i + 1)
                pe.wait_ge(sig["o_ok"], i + 1)
                for j in range(3):
                    pe.matmul(gb[j][:, :], ones_r[:, :], row_hi[j][:, :, :], start=True, stop=False)
                    mm = pe.matmul(gb[j][:, :], ones_r[:, :], row_lo[j][:, :, :], start=False, stop=True)
                mm.then_inc(sig["rows_mm"], 1)

            def kv_turn(i):
                pe.wait_ge(sig["stage_ok"], 3 * i + 3)
                for h in range(H):
                    pe.transpose(fb[0][:, h * P:(h + 1) * P], stg[:, H + h, :], ident)
                for h in range(H):
                    mm = pe.transpose(fb[1][:, h * P:(h + 1) * P], stg[:, 2 * H + h, :], ident)
                mm.then_inc(sig["kvt_mm"], 1)

            def cum_row(i):
                pe.wait_ge(sig["fprep_ok"], i + 1)
                pe.wait_ge(sig["fxl_ok"], i + 1)
                pe.matmul(fb[2][:, :], ones, fcum[:, :, :], start=True, stop=True).then_inc(sig["cum_mm"], 1)

            def kk(i):
                pe.wait_ge(sig["kb_ok"], i + 1)
                pe.wait_ge(sig["qh_ok"], i + 1)
                for h in range(H):
                    mm = pe.matmul(gb[1][:, h * P:(h + 1) * P], stg[:, H + h, :], kb[:, h, :], start=True, stop=True)
                mm.then_inc(sig["kk_mm"], 1)
                for h in range(H):
                    mm = pe.matmul(gb[2][:, h * P:(h + 1) * P], stg[:, H + h, :], qh[:, h, :], start=True, stop=True)
                mm.then_inc(sig["kq_mm"], 1)

            def k_state(i):
                pe.wait_ge(sig["cum_done"], i + 1)
                for h in range(H):
                    mm = pe.matmul(fb[2][:, h * P:(h + 1) * P], stg[:, H + h, :], state[:, h, :], start=True, stop=True)
                mm.then_inc(sig["ks_mm"], 1)

            def x_turn(i):
                pe.wait_ge(sig["xt0_ok"], i + 1)
                pe.wait_ge(sig["erow_ok"], i + 1)
                for h in range(H):
                    mm = pe.transpose(gb[0][:, h * P:(h + 1) * P], xt[:, h, :], ident)
                mm.then_inc(sig["xtr_mm"], 1)

            def lev_z(lev):
                def go(i):
                    pe.wait_ge(sig["olev_ok"], 6 * i + lev)
                    if lev == 1:
                        pe.wait_ge(sig["xi0_ok"], i + 1)
                    else:
                        pe.wait_ge(sig["xi_ok"], 5 * i + lev - 1)
                    for h in range(H):
                        mm = pe.matmul(gb[0][:, 64 * h:64 * h + 64], olev[lev % 2][:, h, :], half1(xi[:, h, :], lev, 0),
                                       start=True, stop=True)
                    mm.then_inc(sig["z_mm"], 1)
                return go

            def lev_xz(lev):
                def go(i):
                    pe.wait_ge(sig["z_ok"], 6 * i + lev)
                    if lev == 1:
                        pe.wait_ge(sig["at_ok"], i + 1)
                    else:
                        pe.wait_ge(sig["xt_ok"], 6 * i + lev - 1)
                    if lev < NLEV - 1:
                        for h in range(H):
                            pe.matmul(gb[1][:, 64 * h:64 * h + 64], xt[:, h, :], half1(zlev[lev][:, h, :], lev, 0),
                                      start=True, stop=True)
                    for h in range(H):
                        mm = pe.matmul(gb[2][:, 64 * h:64 * h + 64], zlev[lev][:, h, :], half1(xt[:, h, :], lev, 1),
                                       start=True, stop=True)
                    mm.then_inc(sig["xz_mm"], 1)
                return go

            def v_new(i):
                pe.wait_ge(sig["xt_ok"], 6 * i + 6)
                pe.wait_ge(sig["r_ok"], i + 1)
                for h in range(H):
                    mm = pe.matmul(gb[1][:, h * P:(h + 1) * P], xt[:, h, :], vb[:, h, :], start=True, stop=True)
                mm.then_inc(sig["vn_mm"], 1)

            def out_state(i):
                pe.wait_ge(sig["vn_ok"], i + 1)
                pe.wait_ge(sig["qe_ok"], i + 1)
                pe.wait_ge(sig["ktok_ok"], i + 1)
                for h in range(H):
                    o = gb[2][:, h * P:(h + 1) * P]
                    pe.matmul(o, state[:, h, :], erow[:, h, :], start=True, stop=False)
                    mm = pe.matmul(o, vn[:, h, :], at[:, h, :], start=False, stop=True)
                mm.then_inc(sig["o_mm"], 1)
                for h in range(H):
                    mm = pe.matmul(gb[0][:, h * P:(h + 1) * P], ktok[:, h, :], vn[:, h, :], start=True, stop=True)
                mm.then_inc(sig["ds_mm"], 1)

            def fv_turn(i):
                evacuated(pe, U_MIX, 6, i, 2)
                pe.wait_ge(sig["vb_ok"], i + 1)
                for t in range(NT):
                    mm = pe.transpose(fb[1][:, t * P:(t + 1) * P], fv[:, t * P:(t + 1) * P], ident)
                mm.then_inc(sig["fvt_mm"], 1)

            def scores(t):
                def go(i):
                    if t == 0:
                        evacuated(pe, U_MIX, 6, i, 1)
                        evacuated(pe, U_MIX, 6, i, 0)
                        pe.wait_ge(sig["ktok_ok"], i + 1)
                    else:
                        pe.wait_ge(sig["lgt_ok"], 4 * i + t)
                    pe.matmul(fb[0][:, 0:(t + 1) * P], fq[:, t * P:(t + 1) * P], fk[:, 0:(t + 1) * P],
                              start=True, stop=True).then_inc(sig["s_mm"], 1)
                return go

            def p_turn(t):
                def go(i):
                    pe.wait_ge(sig["pn_ok"], 4 * i + t + 1)
                    if t == 0:
                        pe.wait_ge(sig["fvt_ok"], i + 1)
                    else:
                        pe.wait_ge(sig["pt_ok"], 4 * i + t)
                    for j in range(t + 1):
                        mm = pe.transpose(fb[1][:, j * P:(j + 1) * P], pr[t % 2][:, j * P:(j + 1) * P], ident)
                    mm.then_inc(sig["pt_mm"], 1)
                return go

            def p_v(t):
                def go(i):
                    pe.wait_ge(sig["pt_ok"], 4 * i + t + 1)
                    if t == 0:
                        pe.wait_ge(sig["r_ok"], i + 1)
                    for j in range(t + 1):
                        mm = pe.matmul(fb[2][:, t * P:(t + 1) * P], fvt[:, j, :], pt[:, j, :],
                                       start=(j == 0), stop=(j == t))
                    mm.then_inc(sig["pv_mm"], 1)
                return go

            mixer = {
                0: [rows], 1: [cum_row], 2: [kv_turn], 3: [kk], 4: [k_state], 5: [x_turn],
                10: [scores(0)], 12: [scores(1)], 13: [fv_turn], 14: [p_turn(0)], 15: [scores(2), p_v(0)],
                16: [p_turn(1)], 17: [scores(3), p_v(1)], 18: [v_new], 19: [p_turn(2)], 20: [p_v(2), out_state],
                21: [p_turn(3)], 22: [p_v(3)],
            }
            for lev in range(1, NLEV):
                mixer.setdefault(4 + 2 * lev, []).insert(0, lev_z(lev))
                mixer.setdefault(5 + 2 * lev, []).insert(0, lev_xz(lev))

            with pe.Fori(0, H) as i:
                for p in range(6):
                    def gap(q, p=p):
                        for step in mixer.get(4 * p + q, ()):
                            step(i)
                    unit(U_MIX, 6, i, p, xn_h, xn_l, KT, gaps=gap)

            def z_gap(p):
                def gap(q):
                    if (p, q) in ((0, 2), (0, 3), (1, 0), (1, 1)):
                        h = (q + 2) % H
                        pe.wait_ge(sig["osq_ok"], h + 1)
                        column_sums(fb[0][:, 4 * h:4 * h + 4], lambda j: osq[:, h, P * j:P * j + P], NT)\
                            .then_inc(sig["ostat_mm"], 1)
                    if p >= 2 and q % 2 == 1:
                        h = 2 * (p - 2) + q // 2
                        pe.wait_ge(sig["odiag_ok"], h + 1)
                        pe.matmul(obank[h][:, :], ones, osq[:, h, :], start=True, stop=True).then_inc(sig["orow_mm"], 1)
                return gap

            for p in range(H):
                unit(U_Z, 4, 0, p, xn_h, xn_l, KT, gaps=z_gap(p))

            def deltanet_ready(k):
                pe.wait_ge(sig["oal_ok"], k + 1)

            with pe.Fori(0, KT) as i:
                for p, (bh, bl) in enumerate(((oa_h, oa_l), (sc_h, sc_l), (fx_h, fx_l))):
                    unit(U_BR, 6, i, 2 * p, xn_h, xn_l, KT)
                    unit(U_BR, 6, i, 2 * p + 1, bh, bl, H, k_wait=deltanet_ready if p == 0 else None)
            def merged_ready(k):
                pe.wait_ge(sig["mgl_ok"], k + 2)

            with pe.Fori(0, KT // 2) as i:
                for p in range(2):
                    unit(U_O, 2, i, p, mg_h, mg_l, KT, k_wait=merged_ready if p == 0 else None)

            def token_sums(n):
                pe.wait_ge(sig["rss_ok"], (KT + 1) * n)
                column_sums(fb[0][:, 0:NT], lambda j: sqsum[:, P * j:P * j + P], NT).then_inc(sig["rstat_mm"], 1)

            def res_ready(k):
                pe.wait_ge(sig["nl_done"], KT + k + 1)

            def norm2_gap(q):
                if q == 3:
                    token_sums(1)

            for p in range(4):
                if p == 1:
                    unit(U_UP, 4, 0, p, xn_h, xn_l, KT, gaps=lambda q: token_row(1) if q == 3 else None)
                else:
                    unit(U_UP, 4, 0, p, xn_h, xn_l, KT, k_wait=res_ready if p == 0 else None,
                         gaps=norm2_gap if p == 0 else None)
            with pe.Fori(1, KF // 2) as i:
                for p in range(4):
                    unit(U_UP, 4, i, p, xn_h, xn_l, KT)
            with pe.Fori(0, KT // 2) as i:
                for p in range(6):
                    pe.wait_ge(sig["f_l"], 8 * (p % 3) + KDN[p % 3] + 2)
                    if p % 3 == 0:
                        pe.wait_ge(acc_free[p // 3], i + (U_DN // 2 + 1))
                    unit(U_DN, 6, i, p, ff_h, ff_l, KDN[p % 3], k0=8 * (p % 3), bnk=p // 3,
                         start=p % 3 == 0, stop=p % 3 == 2)
            token_sums(2)
            token_row(2)

        @block.scalar
        def _(act):
            def hi(base, per, i, p, kt, hf):
                slot, c = p % 2, slice(hf * kt // 2 * P, (hf + 1) * kt // 2 * P)
                act.wait_ge(raw_in[slot][hf], 8 * per * i + (8 * (base + p - slot) + 16))
                if base + p >= 2:
                    act.wait_ge(half_done, 2 * per * i + (2 * (base + p) - 3 + hf))
                act.copy(w_h[slot][:, c], raw[slot][:, c]).then_inc(hi_done, 1)

            def done(base, per, i, p):
                act.wait_ge(half_done, 2 * per * i + (2 * (base + p) + 2))

            for hf in range(2):
                hi(0, 2, 0, 0, KT, hf)
            act.wait_ge(sig["prm_in"], 16)
            for k in range(KT):
                if k % 2 == 0:
                    act.wait_ge(xin[k // 2], 16)
                g0 = PRM["g1"].start + k
                act.activation(xg_h[:, k, :], x_in[:, k, :], ACT.Copy, scale=prm[:, g0:g0 + 1]).then_inc(sig["xgh_ok"], 1)
            for hf in range(2):
                hi(0, 2, 0, 1, KT, hf)
            act.activation(x_sq[:, 4:6, :], x_in[:, 4:6, :], ACT.Square).then_inc(sig["xsq_act"], 1)
            for hf in range(2):
                hi(0, 2, 0, 2, KT, hf)
            act.wait_ge(sig["cst_in"], 16)
            act.copy(ones_r[:, :], ones).then_inc(sig["ones_ok"], 1)
            act.wait_ge(sig["ws_in"], 16)
            act.copy(ws_h[:, :], ws_raw[:, :]).then_inc(sig["wsh_done"], 1)
            act.activation(ea[:, :], prm[:, PRM["a_log"]], ACT.Exp).then_inc(sig["ea_ok"], 1)

            def hi_qkv(u, hf):
                hi(0, 2, 0, u, KT, hf)

            def tap_of(u, j):
                t0 = PRM["conv_qkv"].start + 4 * u + j
                return prm[:, t0:t0 + 1]

            def tanh_of(u):
                if u < U_V:
                    act.wait_ge(sig["qy_ok"], u + 1)
                else:
                    act.wait_ge(qkv_bank[u][1], freed(u) + 1)
                act.activation(th[u % 2][:, :], cy[u % 2][:, :], ACT.Tanh, scale=0.5).then_inc(sig["qth_ok"], 1)

            def square_of(u):
                act.wait_ge(sig["q_done"], u + 1)
                act.activation(sq[:, u, :], qkv[:, u, :], ACT.Square).then_inc(sig["sq_done"], 1)

            def norm_block(k):
                g0 = PRM["g1"].start + k
                act.wait_ge(sig["nv_done"], k + 1)
                act.activation(xn_h[:, k, :], x_in[:, k, :], ACT.Copy, scale=prm[:, g0:g0 + 1])
                act.activation(x_in[:, k, :], x_in[:, k, :], ACT.Copy, scale=prm[:, g0:g0 + 1]).then_inc(sig["nh_done"], 1)

            norm_blocks = {1: (0,), 2: (1, 2), 3: (3, 4), 4: (5, 6), 5: (7,)}

            for u in range(U_V):
                if u < U_V - 1:
                    hi_qkv(u + 3, 0)
                if u == U_V - 1:
                    act.wait_ge(sig["small_mm"], 1)
                    act.copy(lgt[0:12, :], fb[2][0:12, :]).then_inc(sig["small_cp"], 1)
                if u:
                    tanh_of(u - 1)
                if u < U_V - 1:
                    hi_qkv(u + 3, 1)
                act.wait_ge(qkv_bank[u][1], freed(u) + 1)
                act.activation(cy[u % 2][:, :], yq[u % 2][:, :], ACT.Copy, scale=tap_of(u, 3)).then_inc(sig["qy_tap"], 1)
                for k in norm_blocks.get(u, ()):
                    norm_block(k)
                if u:
                    square_of(u - 1)
            tanh_of(U_V - 1)
            hi_qkv(U_V + 2, 0)
            square_of(U_V - 1)
            act.wait_ge(sig["colu_ok"], 1)
            act.activation(bet[:, 0, :, :], lg[:, :, 0:H], ACT.Exp, scale=-1.0).then_inc(sig["eb_done"], 1)
            act.activation(spu[:, 1, :, :], spu[:, 0, :, :], ACT.Abs).then_inc(sig["abs_ok"], 1)
            act.wait_ge(sig["abs_ok"], 1)
            act.activation(spu[:, 2, :, :], spu[:, 1, :, :], ACT.Exp, scale=-1.0).then_inc(sig["eb_done"], 1)
            def v_tap(u):
                done(0, 2, 0, u)
                act.wait_ge(sig["q_done"], u - 1)
                act.activation(cy[u % 2][:, :], qkv_bank[u][0][:, :], ACT.Copy, scale=tap_of(u, 3))\
                   .then_inc(sig["qy_tap"], 1)

            def stage(i, j):
                act.copy(stg[:, H * j:H * j + H, :], qkv[:, H * j:H * j + H, bass.ds(P * i, P)]).then_inc(sig["stage_ok"], 1)

            v_tap(U_V)
            hi_qkv(U_V + 2, 1)
            hi_qkv(U_V + 3, 0)
            tanh_of(U_V)
            v_tap(U_V + 1)
            hi_qkv(U_V + 3, 1)
            hi_qkv(U_V + 4, 0)
            act.wait_ge(sig["gc_mm"], 1)
            act.copy(gcols[:, :, Q_GC, :], fb[2][:, 0:16].rearrange("p (t h) -> p t h", h=H)).then_inc(sig["gcc_ok"], 1)
            act.activation(ec16[:, :, :], fb[2][:, 0:16].rearrange("p (t h) -> p t h", h=H), ACT.Exp)\
               .then_inc(sig["gcc_ok"], 1)
            act.wait_ge(sig["stat_mm"], 2 * H)
            stage(0, 0)
            stage(0, 1)
            hi_qkv(U_V + 4, 1)
            v_tap(U_V + 2)
            tanh_of(U_V + 1)
            hi_qkv(U_V + 5, 0)
            hi_qkv(U_V + 5, 1)
            v_tap(U_V + 3)
            tanh_of(U_V + 2)
            tanh_of(U_V + 3)
            act.wait_ge(sig["q_done"], 3 * H)
            stage(0, 2)

            def act_rows(i):
                act.wait_ge(sig["kd0_ok"], i + 1)
                act.activation(kd[:, 1, :], kd[:, 0, :], ACT.Exp).then_inc(sig["kdx_ok"], 1)
                act.activation(kd[:, 2, :], four(gb[0])[:, :, P - 1], ACT.Exp)
                act.activation(erow[:, :, :], four(gb[0]), ACT.Exp).then_inc(sig["erow_ok"], 1)
                act.activation(dec[:, :, :], dec[:, :, :], ACT.Exp).then_inc(sig["dec_ok"], 1)

            def act_cum(i):
                act.wait_ge(sig["cum_mm"], i + 1)
                act.copy(fcum[:, :, :], four(fb[2])).then_inc(sig["cum_done"], 1)

            def act_x(i):
                act.wait_ge(sig["xtr_mm"], i + 1)
                act.copy(xi[:, :, :], four(gb[0])).then_inc(sig["xi0_ok"], 1)

            def act_z(lev):
                def go(i):
                    act.wait_ge(sig["z_mm"], 6 * i + lev)
                    act.copy(half(zlev[lev][:, :, :], lev, 0), packed(gb[0], lev)).then_inc(sig["z_ok"], 1)
                return go

            def act_vn(i):
                act.wait_ge(sig["vn_mm"], i + 1)
                act.copy(vn[:, :, :], four(gb[1])).then_inc(sig["vn_ok"], 1)

            def act_o(i):
                act.wait_ge(sig["o_mm"], i + 1)
                act.copy(ogd[:, :, bass.ds(P * i, P)], four(gb[2])).then_inc(sig["o_ok"], 1)

            def act_fvt(i):
                act.wait_ge(sig["fvt_mm"], i + 1)
                act.copy(fvt[:, :, :], four(fb[1])).then_inc(sig["fvt_ok"], 1)

            def act_exp(t):
                def go(i):
                    act.wait_ge(sig["nmx_ok"], 4 * i + t + 1)
                    n = (t + 1) * P
                    act.activation(pr[t % 2][:, 0:n], pr[t % 2][:, 0:n], ACT.Exp, bias=fst[:, 1, t:t + 1],
                                   accum_out=fst[:, 2, t:t + 1]).then_inc(sig["exp_ok"], 1)
                return go

            def act_pt(t):
                def go(i):
                    act.wait_ge(sig["pt_mm"], 4 * i + t + 1)
                    if t:
                        act.wait_ge(sig["pv_mm"], 4 * i + t)
                    act.copy(pt[:, 0:t + 1, :], four(fb[1])[:, 0:t + 1, :]).then_inc(sig["pt_ok"], 1)
                return go

            def act_fx(i):
                act.wait_ge(sig["pv_mm"], 4 * i + 4)
                act.copy(fx_h[:, i, :], fb[2][:, :]).then_inc(sig["fxh_ok"], 1)

            def act_stage(j):
                def go(i):
                    act.wait_ge((sig["qh_ok"], sig["ks_mm"], sig["kvt_mm"])[j], i + 1)
                    stage((i + 1) % H, j)
                return go

            mixer = {0: [act_rows], 1: [act_cum], 5: [act_x], 11: [act_exp(0)], 13: [act_exp(1), act_fvt],
                     15: [act_pt(0)], 16: [act_exp(2)], 17: [act_pt(1)], 18: [act_exp(3), act_vn],
                     20: [act_pt(2), act_o], 22: [act_pt(3)]}
            for lev in range(1, NLEV):
                mixer.setdefault(4 + 2 * lev, []).insert(0, act_z(lev))
            for j in range(3):
                mixer.setdefault(7 + 2 * j, []).append(act_stage(j))

            def act_unit(i, p):
                b = p % 2
                done(U_MIX, 6, i, p)
                if p == 0:
                    act.mul(fq[:, :], acc[b][:, :], HD ** -0.5).then_inc(acc_free[b], 1)
                elif p in (1, 2, 3):
                    act.copy((fk, fv, cs)[p - 1][:, :], acc[b][:, :]).then_inc(acc_free[b], 1)
                hi(U_MIX + 2, 6, i, p, KT, 1)

            with act.Fori(0, H) as i:
                for g in range(24):
                    for step in mixer.get(g, ()):
                        step(i)
                    if g % 4 == 3:
                        hi(U_MIX + 2, 6, i, g // 4, KT, 0)
                    if g % 4 == 0 and g:
                        act_unit(i, g // 4 - 1)
                act_fx(i)
                act_unit(i, 5)
                evacuated(act, U_MIX, 6, i, 5)
                act.copy(sc_h[:, i, :], us[:, :]).then_inc(sig["sch_ok"], 1)

            for h in range(H):
                act.activation(osq[:, h, :], ogd[:, h, :], ACT.Square).then_inc(sig["osq_ok"], 1)
            def oa_hi(h):
                act.wait_ge(sig["oa2_ok"], h + 1)
                act.copy(oa_h[:, h, :], ogd[:, h, :]).then_inc(sig["oah_ok"], 1)

            for p in range(H):
                hi(U_Z + 2, 4, 0, p, H if p == 3 else KT, 0)
                if p == 3:
                    for h in range(3):
                        oa_hi(h)
                done(U_Z, 4, 0, p)
                if p >= 2:
                    evacuated(act, U_Z, 4, 0, p - 2)
                act.activation(zt[p % 2][:, :], acc[p % 2][:, :], ACT.Tanh, scale=0.5).then_inc(sig["zth_ok"], 1)
                hi(U_Z + 2, 4, 0, p, H if p == 3 else KT, 1)
            oa_hi(3)

            def act_merge(i, last):
                for p in range(6):
                    kt = KT if p % 2 == 0 or (last and p == 5) else H
                    if kt == H or p % 2 == 0:
                        hi(U_BR + 2, 6, i, p, kt, 0)
                    else:
                        done(U_BR, 6, i, p)
                        hi(U_BR + 2, 6, i, p, kt, 0)
                    if p % 2 == 0:
                        done(U_BR, 6, i, p)
                        act.wait_ge(acc_free[1], 3 * i + ((U_BR + p) // 2 + 1))
                        act.activation(tg[:, :], acc[0][:, :], ACT.Tanh, scale=0.5).then_inc(acc_free[0], 1)
                    hi(U_BR + 2, 6, i, p, kt, 1)
                act.wait_ge(sig["m2_ok"], 2 * i + 2)
                act.mul(mg_h[:, i, :], mg[:, :], 0.5).then_inc(sig["mgh_ok"], 1)

            with act.Fori(0, KT - 1) as i:
                act_merge(i, False)
            act_merge(KT - 1, True)

            with act.Fori(0, KT // 2) as i:
                for p in range(2):
                    hi(U_O + 2, 2, i, p, KT, 0)
                    hi(U_O + 2, 2, i, p, KT, 1)
                    evacuated(act, U_O, 2, i, p)
                    act.wait_ge(sig["rss_ok"], 2 * i + p + 1)
                    act.activation(sq2[:, :], res[:, 2 * i + p, :], ACT.Square).then_inc(sig["rsq_ok"], 1)
                    act.wait_ge(sig["rsg_ok"], 2 * i + p + 1)
                    act.copy(xn_h[:, 2 * i + p, :], rsg[p][:, :]).then_inc(sig["nh_done"], 1)

            def hidden_hi(n, q):
                act.wait_ge(sig["f_hv"], n + 1)
                act.mul(ff_h[:, n, :], hv[q][:, :], 0.5).then_inc(sig["f_h"], 1)

            def act_up(i, first):
                for p in range(4):
                    b, q = p % 2, p // 2
                    hi(U_UP + 2, 4, i, p, KT, 0)
                    if b:
                        act.wait_ge(sig["fy_ok"], 4 * i + p + 1)
                        act.activation(yt[q][:, :], yc[p - 1][:, :], ACT.Tanh, scale=0.5).then_inc(sig["fth_ok"], 1)
                    elif p or not first:
                        hidden_hi(2 * i + (q - 1), 1 - q)
                    hi(U_UP + 2, 4, i, p, KT, 1)
                    if p == 0:
                        act.wait_ge(sig["fy_ok"], 4 * i + 1)
                        t0 = PRM["conv_ffn"].start
                        act.copy(tapf[:, :, :], prm[:, bass.ds(t0 + 12 * i, 12)].rearrange("p (a j) -> p a j", j=3))\
                           .then_inc(sig["f_tap"], 1)
                        act.wait_ge(sig["f_tap"], i + 1)
                    evacuated(act, U_UP, 4, i, p)
                    act.activation(yc[p][:, :], yr[b][:, :], ACT.Copy, scale=tapf[:, p, 2:3]).then_inc(sig["fy_tap"], 1)

            act_up(0, True)
            with act.Fori(1, KF // 2) as i:
                act_up(i, False)
            hidden_hi(KF - 1, 1)

            def down_hi(i, p, hf):
                if hf == 0 and KDN[(p + 2) % 3] > KDN[p % 3]:
                    done(U_DN, 6, i, p)
                hi(U_DN + 2, 6, i, p, KDN[(p + 2) % 3], hf)

            def act_down(i, last):
                for p in range(6):
                    if not (last and p >= 4):
                        down_hi(i, p, 0)
                        down_hi(i, p, 1)
                    if p % 3 == 2:
                        act.wait_ge(acc_free[p // 3], i + (U_DN // 2 + 2))
                        act.wait_ge(sig["rss_ok"], 2 * i + (p // 3 + KT + 2))
                        act.activation(sq2[:, :], res[:, 2 * i + p // 3, :], ACT.Square).then_inc(sig["rsq_ok"], 1)

            with act.Fori(0, KT // 2 - 1) as i:
                act_down(i, False)
            act_down(KT // 2 - 1, True)

        @block.gpsimd
        def _(pool):
            for c in (0, 1):
                pool.wait_ge(xin[c], 16)
                pool.tensor_tensor(x_sq[:, 2 * c:2 * c + 2, :], x_in[:, 2 * c:2 * c + 2, :], x_in[:, 2 * c:2 * c + 2, :],
                                   ALU.mult).then_inc(sig["xsq_pool"], 1)
            pool.wait_ge(sig["xsq_pool"], 2)
            pool.tensor_tensor(x_sq[:, 0:2, :], x_sq[:, 0:2, :], x_sq[:, 2:4, :], ALU.add).then_inc(sig["xsum_pool"], 1)
            pool.wait_ge(sig["xg_ok"], KT)
            pool.wait_ge(sig["row_ok"], 1)
            for k in range(KT):
                pool.tensor_tensor(x_in[:, k, :], x_in[:, k, :], rms_row[:, :], ALU.mult).then_inc(sig["nv_done"], 1)
            for k in range(KT):
                pool.wait_ge(sig["nh_done"], k + 1)
                pool.tensor_tensor(xn_l[:, k, :], x_in[:, k, :], xn_h[:, k, :].bitcast(F32), ALU.subtract)\
                    .then_inc(sig["nl_done"], 1)
            pool.wait_ge(sig["nl_done"], KT)
            for z in zlev[1:] + [state]:
                pool.memset(z[:, :, :], 0.0)

            for u in (U_V + 2, U_V + 3):
                for hf in range(2):
                    pool.wait_ge(hi_done, 2 * u + hf + 1)
                    c = slice(hf * KT // 2 * P, (hf + 1) * KT // 2 * P)
                    pool.tensor_tensor(w_l[u % 2][:, c], raw[u % 2][:, c], w_h[u % 2][:, c].bitcast(F32), ALU.subtract)\
                        .then_inc(lo_done, 1)

            def prep(i, first):
                if not first:
                    pool.wait_ge(sig["at_ok"], i)
                    pool.wait_ge(sig["r_ok"], i)
                    pool.wait_ge(sig["qe_ok"], i)
                for j in range(3):
                    if first:
                        pool.wait_ge(sig["gcl_ok"], 1 if j == 0 else 2)
                    mask = tiles(cst[:, C_TRI, :] if j == 0 else ident)
                    for part, cols in ((row_hi[j], gch), (row_lo[j], gcl)):
                        mm = pool.tensor_tensor(part[:, :, :], mask, heads(cols[:, i, j, :].bitcast(F32)), ALU.mult)
                mm.then_inc(sig["prep_ok"], 1)
                if first:
                    pool.wait_ge(sig["gcols_ok"], 1)
                pool.tensor_copy(gcs[:, :, :], gcols[:, i, :, :]).then_inc(sig["gcs_ok"], 1)
                pool.tensor_copy(fcs[:, :], fcols[:, i, :]).then_inc(sig["gcs_ok"], 1)
                pool.wait_ge(sig["gcs_ok"], 2 * i + 2)
                if not first:
                    pool.wait_ge(sig["lgt_ok"], 4 * i)
                pool.tensor_tensor(fcum[:, :, :], tiles(cst[:, C_TRI, :]), heads(fcs[:, 0:4]), ALU.mult)\
                    .then_inc(sig["fc_ok"], 1)
                pool.wait_ge(sig["fc_ok"], i + 1)
                pool.tensor_tensor(fcum[:, :, :], fcum[:, :, :], heads(fcs[:, 4:8]), ALU.add).then_inc(sig["fprep_ok"], 1)

            def masks(i):
                pool.wait_ge(sig["lt_ok"], i + 1)
                for lev in range(1, NLEV):
                    if lev > 2:
                        pool.wait_ge(sig["z_mm"], 6 * i + lev - 2)
                    pool.tensor_tensor(olev[lev % 2][:, :, :], lt[:, :, :], tiles(cst[:, C_LEV + lev, :]), ALU.mult)\
                        .then_inc(sig["olev_ok"], 1)

            prep(0, True)
            with pool.Fori(0, H - 1) as i:
                masks(i)
                prep(i + 1, False)
            masks(H - 1)

        @block.vector
        def _(dve):
            links = [0]

            def link(ins):
                links[0] += 1
                ins.then_inc(sig["v_chain"], 1)
                dve.wait_ge(sig["v_chain"], links[0])

            def lo(base, per, i, p, kt, hf):
                slot, c = p % 2, slice(hf * kt // 2 * P, (hf + 1) * kt // 2 * P)
                dve.wait_ge(hi_done, 2 * per * i + (2 * (base + p) + hf + 1))
                dve.tensor_tensor(w_l[slot][:, c], raw[slot][:, c], w_h[slot][:, c].bitcast(F32), ALU.subtract)\
                    .then_inc(lo_done, 1)

            def done(base, per, i, p):
                dve.wait_ge(half_done, 2 * per * i + (2 * (base + p) + 2))

            def rsqrt(y, x, a):
                link(dve.tensor_scalar(a.bitcast(I32), x.bitcast(I32), 1, None, ALU.arith_shift_right))
                link(dve.tensor_scalar(y.bitcast(I32), a.bitcast(I32), -1.0, float(0x5F3759DF), ALU.mult, ALU.add))
                for _ in range(3):
                    link(dve.tensor_tensor(a, y, y, ALU.mult))
                    link(dve.scalar_tensor_tensor(out=a, in0=a, scalar=-0.5, in1=x, op0=ALU.mult, op1=ALU.mult))
                    link(dve.scalar_tensor_tensor(out=y, in0=a, scalar=1.5, in1=y, op0=ALU.add, op1=ALU.mult))

            def token_factors():
                link(dve.tensor_scalar(col[:, 0, :], fb[0][:, 0:NT], 1.0 / D, EPS, ALU.mult, ALU.add))
                rsqrt(col[:, 1, :], col[:, 0, :], col[:, 2, :])
                dve.tensor_tensor(diag[:, :, :], tiles(ident, NT), heads(col[:, 1, :]), ALU.mult).then_inc(sig["diag_ok"], 1)

            def token_row(n):
                dve.wait_ge(sig["rstat_mm"], n + 1)
                token_factors()
                dve.wait_ge(sig["rown_mm"], n + 1)
                dve.tensor_copy(rms_row[:, :], fb[1][:, :]).then_inc(sig["row_ok"], 1)
                dve.wait_ge(sig["row_ok"], n + 1)

            dve.memset(rms_row[:, :], 0.0).then_inc(sig["zeros_ok"], 1)
            for j, free in enumerate((*acc_free, *acc_free, *acc_free, *acc_free, sig["st_ok"], sig["o_ok"],
                                      sig["fxl_ok"], sig["mgl_ok"],
                                      sig["f_l"], sig["f_l"], sig["fy_ok"])):
                dve.memset(col[:, 3 + j // 4, j % 4:j % 4 + 1], 0.0).then_inc(free, 1)
            for hf in range(2):
                lo(0, 2, 0, 0, KT, hf)
            dve.wait_ge(sig["prm_in"], 16)
            for k in range(KT):
                g0 = PRM["g1"].start + k
                dve.wait_ge(sig["xgh_ok"], k + 1)
                dve.scalar_tensor_tensor(out=xg_l[:, k, :], in0=x_in[:, k, :], scalar=prm[:, g0:g0 + 1],
                                         in1=xg_h[:, k, :].bitcast(F32), op0=ALU.mult, op1=ALU.subtract)\
                    .then_inc(sig["xg_ok"], 1)
            lo(0, 2, 0, 1, KT, 0)
            dve.tensor_tensor(x_sq[:, 6:8, :], x_in[:, 6:8, :], x_in[:, 6:8, :], ALU.mult).then_inc(sig["xsq_dve"], 1)
            lo(0, 2, 0, 1, KT, 1)
            dve.wait_ge(sig["xsq_dve"], 1)
            dve.wait_ge(sig["xsq_act"], 1)
            link(dve.tensor_tensor(x_sq[:, 4:6, :], x_sq[:, 4:6, :], x_sq[:, 6:8, :], ALU.add))
            dve.wait_ge(sig["xsum_pool"], 1)
            dve.tensor_tensor(x_sq[:, 0:2, :], x_sq[:, 0:2, :], x_sq[:, 4:6, :], ALU.add).then_inc(sig["xsum_ok"], 1)
            for hf in range(2):
                lo(0, 2, 0, 2, KT, hf)
            dve.wait_ge(sig["wsh_done"], 1)
            dve.tensor_tensor(ws_l[:, :], ws_raw[:, :], ws_h[:, :].bitcast(F32), ALU.subtract).then_inc(sig["wsl_done"], 1)
            dve.wait_ge(sig["cst_in"], 16)
            token_row(0)

            def add_tap(y, x, tap, back):
                return dve.scalar_tensor_tensor(out=y[:, back:T], in0=x[:, 0:T - back], scalar=tap, in1=y[:, back:T],
                                                op0=ALU.mult, op1=ALU.add)

            def lo_qkv(u, hf):
                lo(0, 2, 0, u, KT, hf)

            def silu_of(u):
                dve.wait_ge(sig["qth_ok"], u + 1)
                dve.scalar_tensor_tensor(out=qkv[:, u, :], in0=th[u % 2][:, :], scalar=1.0, in1=cy[u % 2][:, :],
                                         op0=ALU.add, op1=ALU.mult).then_inc(sig["q_done"], 1)

            def taps_of(u, src, end):
                t0 = PRM["conv_qkv"].start + 4 * u
                dve.wait_ge(sig["qy_tap"], u + 1)
                for j in (2, 1):
                    add_tap(cy[u % 2], src, prm[:, t0 + j:t0 + j + 1], 3 - j).then_inc(sig["qc_ok"], 1)
                    dve.wait_ge(sig["qc_ok"], 2 * u + 3 - j)
                add_tap(cy[u % 2], src, prm[:, t0:t0 + 1], 3).then_inc(end, 1)

            for u in range(U_V):
                if u < U_V - 1:
                    lo_qkv(u + 3, 0)
                done(0, 2, 0, u)
                dve.tensor_tensor(yq[u % 2][:, :], qkv_bank[u][0][:, :], rms_row[:, :], ALU.mult).then_inc(qkv_bank[u][1], 1)
                dve.wait_ge(qkv_bank[u][1], freed(u) + 1)
                if u < U_V - 1:
                    lo_qkv(u + 3, 1)
                if u:
                    silu_of(u - 1)
                taps_of(u, yq[u % 2], sig["qy_ok"])
            silu_of(U_V - 1)

            def v_taps(u):
                taps_of(u, qkv_bank[u][0], qkv_bank[u][1])

            dve.wait_ge(sig["small_tr"], 1)
            link(dve.tensor_copy(lg[:, :, :], gb[0][:, 0:12 * NT].rearrange("p (t c) -> p t c", c=12)))

            def rep(name):
                return prm[:, PRM[name]].unsqueeze(1).broadcast_to([P, NT, H])

            dve.tensor_tensor(spu[:, 0, :, 0:H], lg[:, :, H:2 * H], rep("dt_bias"), ALU.add)
            link(dve.tensor_tensor(spu[:, 0, :, H:], lg[:, :, 2 * H:], rep("fox_bias"), ALU.add))
            link(dve.tensor_scalar(spu[:, 0, :, H:], spu[:, 0, :, H:], -1.0, None, ALU.mult))
            dve.tensor_scalar(spu[:, 3, :, :], spu[:, 0, :, :], 0.0, None, ALU.max).then_inc(sig["colu_ok"], 1)
            dve.wait_ge(sig["eb_done"], 2)
            link(dve.tensor_scalar(bet[:, 1, :, :], bet[:, 0, :, :], 1.0, None, ALU.add))
            link(dve.reciprocal(bet[:, 2, :, :], bet[:, 1, :, :]))
            e, z, w, q = spu[:, 2, :, :], spu[:, 5, :, :], spu[:, 6, :, :], spu[:, 7, :, :]
            link(dve.tensor_scalar(w, e, 2.0, None, ALU.add))
            link(dve.reciprocal(q, w))
            link(dve.tensor_tensor(z, e, q, ALU.mult))
            link(dve.tensor_tensor(w, z, z, ALU.mult))
            link(dve.tensor_scalar(q, w, 1.0 / 17, None, ALU.mult))
            for n in (15, 13, 11, 9, 7, 5, 3):
                link(dve.scalar_tensor_tensor(out=q, in0=q, scalar=1.0 / n, in1=w, op0=ALU.add, op1=ALU.mult))
            link(dve.scalar_tensor_tensor(out=q, in0=q, scalar=1.0, in1=z, op0=ALU.add, op1=ALU.mult))
            sp = spu[:, 4, :, :]
            link(dve.scalar_tensor_tensor(out=sp, in0=q, scalar=2.0, in1=spu[:, 3, :, :], op0=ALU.mult, op1=ALU.add))
            dve.wait_ge(sig["ea_ok"], 1)
            dve.scalar_tensor_tensor(out=g16[:, :, :], in0=sp[:, :, 0:H], scalar=-1.0,
                                     in1=ea[:, :].unsqueeze(1).broadcast_to([P, NT, H]),
                                     op0=ALU.mult, op1=ALU.mult).then_inc(sig["colx"], 1)
            dve.wait_ge(sig["colx"], 1)

            def split_columns(a, b):
                link(dve.tensor_copy(gch[:, :, a:b, :], gcols[:, :, a:b, :]))
                dve.tensor_tensor(gcl[:, :, a:b, :], gcols[:, :, a:b, :], gch[:, :, a:b, :].bitcast(F32), ALU.subtract)\
                   .then_inc(sig["gcl_ok"], 1)

            link(dve.tensor_copy(gcols[:, :, Q_G, :], g16[:, :, :]))
            split_columns(Q_G, Q_G + 1)
            v_taps(U_V)
            link(dve.tensor_copy(fcols[:, :, 0:NT], sp[:, :, H:].rearrange("p t h -> p h t")))
            link(dve.memset(fcols[:, :, NT:NT + 1], 0.0))
            for t in range(1, NT):
                link(dve.tensor_tensor(fcols[:, :, NT + t:NT + t + 1], fcols[:, :, NT + t - 1:NT + t],
                                       fcols[:, :, t - 1:t], ALU.add))
            dve.wait_ge(sig["stat_mm"], 2 * H)
            n2 = [nrm[:, j, :, :, :].rearrange("p a t h -> p (a t h)") for j in range(3)]
            link(dve.tensor_scalar(n2[0], fb[0][:, 0:32], 4.0 * EPS, None, ALU.add))
            rsqrt(n2[1], n2[0], n2[2])
            rq, rk = nrm[:, 1, 0, :, :], nrm[:, 1, 1, :, :]
            link(dve.tensor_scalar(gcols[:, :, Q_RQ, :], rq, HD ** -0.5, None, ALU.mult))
            link(dve.tensor_copy(gcols[:, :, Q_RK, :], rk))
            link(dve.tensor_tensor(gcols[:, :, Q_BRK, :], bet[:, 2, :, :], rk, ALU.mult))
            split_columns(Q_BRK, Q_RQ + 1)
            link(dve.tensor_scalar(gcols[:, :, Q_HB, :], bet[:, 2, :, :], 0.5, None, ALU.mult))
            silu_of(U_V)
            v_taps(U_V + 1)
            dve.wait_ge(lo_done, 2 * (U_V + 4))
            lo_qkv(U_V + 4, 0)
            dve.wait_ge(sig["gcc_ok"], 2)
            dve.scalar_tensor_tensor(out=gcols[:, :, Q_NBE, :], in0=gcols[:, :, Q_BRK, :], scalar=-1.0, in1=ec16[:, :, :],
                                     op0=ALU.mult, op1=ALU.mult).then_inc(sig["gcols_ok"], 1)
            silu_of(U_V + 1)
            lo_qkv(U_V + 4, 1)
            v_taps(U_V + 2)
            lo_qkv(U_V + 5, 0)
            lo_qkv(U_V + 5, 1)
            silu_of(U_V + 2)
            v_taps(U_V + 3)
            silu_of(U_V + 3)

            def hcol(ap, h):
                return ap[:, h:h + 1]

            def v_rows(i):
                dve.wait_ge(sig["rows_mm"], i + 1)
                dve.wait_ge(sig["gcs_ok"], 2 * i + 2)
                for h in range(H):
                    dve.scalar_tensor_tensor(out=dec[:, h, :], in0=gb[0][:, h * P:(h + 1) * P], scalar=gcs[:, Q_GC, h:h + 1],
                                             in1=cst[:, C_NEGT, :], op0=ALU.subtract, op1=ALU.min)
                dve.tensor_tensor(kd[:, 0, :], four(gb[0])[:, :, P - 1], gcs[:, Q_GC, :], ALU.subtract)\
                    .then_inc(sig["kd0_ok"], 1)
                dve.wait_ge(sig["stage_ok"], 3 * i + 2)
                dve.tensor_tensor(kb[:, :, :], stg[:, H:2 * H, :], four(gb[1]), ALU.mult).then_inc(sig["kb_ok"], 1)
                dve.tensor_tensor(qh[:, :, :], stg[:, 0:H, :], four(gb[2]), ALU.mult).then_inc(sig["qh_ok"], 1)
                dve.wait_ge(sig["kdx_ok"], i + 1)
                dve.tensor_tensor(kd[:, 1, :], kd[:, 1, :], gcs[:, Q_RK, :], ALU.mult).then_inc(sig["kd1_ok"], 1)

            def v_kv(i):
                dve.wait_ge(sig["kvt_mm"], i + 1)
                dve.tensor_tensor(vb[:, :, :], four(fb[1]), heads(gcs[:, Q_HB, :]), ALU.mult).then_inc(sig["vb_ok"], 1)
                dve.wait_ge(sig["kd1_ok"], i + 1)
                dve.tensor_tensor(ktok[:, :, :], four(fb[0]), heads(kd[:, 1, :]), ALU.mult).then_inc(sig["ktok_ok"], 1)

            def rk_decay(dst, b, i):
                for h in range(H):
                    mm = dve.scalar_tensor_tensor(out=dst[:, h, :], in0=gb[b][:, h * P:(h + 1) * P],
                                                  scalar=gcs[:, Q_RK, h:h + 1], in1=dec[:, h, :], op0=ALU.mult, op1=ALU.mult)
                return mm

            def v_kk(i):
                dve.wait_ge(sig["kk_mm"], i + 1)
                dve.wait_ge(sig["dec_ok"], i + 1)
                rk_decay(lt, 1, i).then_inc(sig["lt_ok"], 1)
                dve.wait_ge(sig["lt_ok"], i + 1)
                dve.tensor_tensor(xi[:, :, :], lt[:, :, :], tiles(cst[:, C_LEV, :]), ALU.mult).then_inc(sig["ot0_ok"], 1)
                dve.wait_ge(sig["ot0_ok"], i + 1)
                dve.tensor_tensor(xt[:, :, :], tiles(ident), xi[:, :, :], ALU.subtract).then_inc(sig["xt0_ok"], 1)

            def v_kq(i):
                dve.wait_ge(sig["kq_mm"], i + 1)
                rk_decay(at, 2, i).then_inc(sig["at_ok"], 1)
                dve.wait_ge(sig["erow_ok"], i + 1)
                dve.tensor_tensor(erow[:, :, :], erow[:, :, :], qh[:, :, :], ALU.mult).then_inc(sig["qe_ok"], 1)

            def v_r(i):
                dve.wait_ge(sig["ks_mm"], i + 1)
                for h in range(H):
                    hs = slice(h * P, (h + 1) * P)
                    mm = dve.scalar_tensor_tensor(out=vb[:, h, :], in0=fb[2][:, hs], scalar=gcs[:, Q_NBE, h:h + 1],
                                                  in1=vb[:, h, :], op0=ALU.mult, op1=ALU.add)
                mm.then_inc(sig["r_ok"], 1)

            def v_lev(lev):
                def go(i):
                    dve.wait_ge(sig["xz_mm"], 6 * i + lev)
                    if lev < NLEV - 1:
                        v = half(xi[:, :, :], lev, 0)
                        dve.tensor_tensor(v, v, packed(gb[1], lev), ALU.subtract).then_inc(sig["xi_ok"], 1)
                    v = half(xt[:, :, :], lev, 1)
                    dve.tensor_tensor(v, v, packed(gb[2], lev), ALU.subtract).then_inc(sig["xt_ok"], 1)
                return go

            def v_state(i):
                dve.wait_ge(sig["ds_mm"], i + 1)
                for h in range(H):
                    mm = dve.scalar_tensor_tensor(out=state[:, h, :], in0=state[:, h, :], scalar=kd[:, 2, h:h + 1],
                                                  in1=gb[0][:, h * P:(h + 1) * P], op0=ALU.mult, op1=ALU.add)
                mm.then_inc(sig["st_ok"], 1)

            def v_soft(t):
                def go(i):
                    n, d = (t + 1) * P, slice(t * P, (t + 1) * P)
                    x = pr[t % 2]
                    dve.wait_ge(sig["s_mm"], 4 * i + t + 1)
                    dve.tensor_tensor(x[:, 0:n], fb[0][:, 0:n], fcum[:, 0:t + 1, :].rearrange("p t c -> p (t c)"), ALU.add)\
                        .then_inc(sig["lgt_ok"], 1)
                    dve.wait_ge(sig["lgt_ok"], 4 * i + t + 1)
                    dve.tensor_tensor(x[:, d], x[:, d], cst[:, C_CAUSAL, :], ALU.add).then_inc(sig["msk_ok"], 1)
                    dve.wait_ge(sig["msk_ok"], 4 * i + t + 1)
                    dve.reduce_max(fst[:, 0, t:t + 1], x[:, 0:n], AX_X).then_inc(sig["mx_ok"], 1)
                    dve.wait_ge(sig["mx_ok"], 4 * i + t + 1)
                    dve.tensor_scalar(fst[:, 1, t:t + 1], fst[:, 0, t:t + 1], -1.0, None, ALU.mult)\
                        .then_inc(sig["nmx_ok"], 1)
                return go

            def v_pn(t):
                def go(i):
                    n = (t + 1) * P
                    dve.wait_ge(sig["exp_ok"], 4 * i + t + 1)
                    dve.reciprocal(fst[:, 3, t:t + 1], fst[:, 2, t:t + 1]).then_inc(sig["ri_ok"], 1)
                    dve.wait_ge(sig["ri_ok"], 4 * i + t + 1)
                    dve.tensor_scalar(pr[t % 2][:, 0:n], pr[t % 2][:, 0:n], fst[:, 3, t:t + 1], None, ALU.mult)\
                        .then_inc(sig["pn_ok"], 1)
                return go

            def v_fx(i):
                dve.wait_ge(sig["fxh_ok"], i + 1)
                dve.tensor_tensor(fx_l[:, i, :], fb[2][:, :], fx_h[:, i, :].bitcast(F32), ALU.subtract)\
                    .then_inc(sig["fxl_ok"], 1)

            mixer = {0: [v_rows], 1: [v_kv], 3: [v_kk], 4: [v_r], 5: [v_kq],
                     10: [v_soft(0)], 12: [v_soft(1)], 11: [v_pn(0)], 14: [v_pn(1)],
                     15: [v_soft(2)], 17: [v_pn(2), v_soft(3)], 19: [v_pn(3)], 20: [v_state]}
            for lev in range(1, NLEV):
                mixer.setdefault(5 + 2 * lev, []).insert(0, v_lev(lev))

            def v_conv(i):
                done(U_MIX, 6, i, 4)
                evacuated(dve, U_MIX, 6, i, 3)
                dve.tensor_tensor(us[:, :], cs[:, :], acc[0][:, :], ALU.mult).then_inc(acc_free[0], 1)
                t0 = PRM["conv_sc"].start
                dve.tensor_copy(tap3[:, :], prm[:, bass.ds(t0 + 3 * i, 3)]).then_inc(sig["sct_ok"], 1)
                dve.wait_ge(sig["sct_ok"], i + 1)
                evacuated(dve, U_MIX, 6, i, 4)
                dve.tensor_scalar(cs[:, :], us[:, :], tap3[:, 2:3], None, ALU.mult).then_inc(sig["scc_ok"], 1)
                for j in (1, 0):
                    dve.wait_ge(sig["scc_ok"], 3 * i + 2 - j)
                    add_tap(cs, us, tap3[:, j:j + 1], 2 - j).then_inc(sig["scc_ok"], 1)

            with dve.Fori(0, H) as i:
                for g in range(24):
                    for step in mixer.get(g, ()):
                        step(i)
                    if g % 4 == 3:
                        lo(U_MIX + 2, 6, i, g // 4, KT, 0)
                    if g % 4 == 0 and g:
                        lo(U_MIX + 2, 6, i, g // 4 - 1, KT, 1)
                    if g == 21:
                        v_conv(i)
                v_fx(i)
                done(U_MIX, 6, i, 5)
                dve.wait_ge(sig["scc_ok"], 3 * i + 3)
                dve.tensor_tensor(us[:, :], cs[:, :], acc[1][:, :], ALU.mult).then_inc(acc_free[1], 1)
                lo(U_MIX + 2, 6, i, 5, KT, 1)
                dve.wait_ge(sig["sch_ok"], i + 1)
                dve.tensor_tensor(sc_l[:, i, :], us[:, :], sc_h[:, i, :].bitcast(F32), ALU.subtract)\
                    .then_inc(sig["scl_ok"], 1)

            def v_z(p):
                lo(U_Z + 2, 4, 0, p, H if p == 3 else KT, 0)
                lo(U_Z + 2, 4, 0, p, H if p == 3 else KT, 1)
                dve.wait_ge(sig["zth_ok"], p + 1)
                dve.scalar_tensor_tensor(out=zg[:, p, :], in0=zt[p % 2][:, :], scalar=1.0, in1=acc[p % 2][:, :],
                                         op0=ALU.add, op1=ALU.mult).then_inc(acc_free[p % 2], 1)

            def v_odiag(h):
                dve.tensor_tensor(osq[:, h, :].rearrange("p (t c) -> p t c", t=NT), tiles(ident), heads(onrm[:, 1, h, :]),
                                  ALU.mult).then_inc(sig["odiag_ok"], 1)

            def v_oa(h):
                dve.wait_ge(sig["orow_mm"], h + 1)
                dve.scalar_tensor_tensor(out=ogd[:, h, :], in0=ogd[:, h, :], scalar=gn_half[:, 0:1], in1=obank[h][:, :],
                                         op0=ALU.mult, op1=ALU.mult).then_inc(sig["oa1_ok"], 1)
                dve.wait_ge(sig["oa1_ok"], h + 1)
                evacuated(dve, U_Z, 4, 0, h)
                dve.tensor_tensor(ogd[:, h, :], ogd[:, h, :], zg[:, h, :], ALU.mult).then_inc(sig["oa2_ok"], 1)

            def v_oal(h):
                dve.wait_ge(sig["oah_ok"], h + 1)
                dve.tensor_tensor(oa_l[:, h, :], ogd[:, h, :], oa_h[:, h, :].bitcast(F32), ALU.subtract)\
                    .then_inc(sig["oal_ok"], 1)

            link(dve.tensor_scalar(gn_half[:, :], prm[:, PRM["gdn_norm"]], 0.5, None, ALU.mult))
            v_z(0)
            dve.wait_ge(sig["ostat_mm"], H)
            o2 = [onrm[:, j, :, :].rearrange("p h t -> p (h t)") for j in range(3)]
            link(dve.tensor_scalar(o2[0], fb[0][:, 0:16], 1.0 / HD, EPS, ALU.mult, ALU.add))
            rsqrt(o2[1], o2[0], o2[2])
            for h in range(H):
                v_odiag(h)
            v_z(1)
            v_z(2)
            v_oa(0)
            v_oa(1)
            v_oal(0)
            v_oa(2)
            v_oal(1)
            v_z(3)
            v_oa(3)
            v_oal(2)
            v_oal(3)

            def v_merge(i, last):
                for p in range(6):
                    lo(U_BR + 2, 6, i, p, KT if p % 2 == 0 or (last and p == 5) else H, 0)
                    if p % 2:
                        done(U_BR, 6, i, p)
                        evacuated(dve, U_BR, 6, i, p - 1)
                        if p == 1:
                            dve.wait_ge(sig["mgl_ok"], i + 1)
                        dst = mg if p == 1 else mg2
                        dve.scalar_tensor_tensor(out=dst[:, :], in0=tg[:, :], scalar=1.0, in1=acc[1][:, :],
                                                 op0=ALU.add, op1=ALU.mult).then_inc(acc_free[1], 1)
                        if p > 1:
                            evacuated(dve, U_BR, 6, i, p)
                            dve.tensor_tensor(mg[:, :], mg[:, :], mg2[:, :], ALU.add).then_inc(sig["m2_ok"], 1)
                            if p == 3:
                                dve.wait_ge(sig["m2_ok"], 2 * i + 1)
                    lo(U_BR + 2, 6, i, p, KT if p % 2 == 0 or (last and p == 5) else H, 1)
                dve.wait_ge(sig["mgh_ok"], i + 1)
                dve.scalar_tensor_tensor(out=mg_l[:, i, :], in0=mg[:, :], scalar=0.5, in1=mg_h[:, i, :].bitcast(F32),
                                         op0=ALU.mult, op1=ALU.subtract).then_inc(sig["mgl_ok"], 1)

            with dve.Fori(0, KT - 1) as i:
                v_merge(i, False)
            v_merge(KT - 1, True)

            dve.memset(sqsum[:, :], 0.0).then_inc(sig["rss_ok"], 1)
            dve.wait_ge(sig["xres_in"], 16)
            with dve.Fori(0, KT // 2) as i:
                for p in range(2):
                    lo(U_O + 2, 2, i, p, KT, 0)
                    lo(U_O + 2, 2, i, p, KT, 1)
                    done(U_O, 2, i, p)
                    dve.tensor_tensor(res[:, 2 * i + p, :], x_res[:, 2 * i + p, :], acc[p][:, :], ALU.add)\
                        .then_inc(acc_free[p], 1)
                    evacuated(dve, U_O, 2, i, p)
                    g0 = PRM["g2"].start + p
                    dve.tensor_tensor(rsg[p][:, :], res[:, 2 * i + p, :],
                                      prm[:, bass.ds(2 * i + g0, 1)].broadcast_to([P, T]), ALU.mult)\
                        .then_inc(sig["rsg_ok"], 1)
                    dve.wait_ge(sig["rsq_ok"], 2 * i + p + 1)
                    dve.tensor_tensor(sqsum[:, :], sqsum[:, :], sq2[:, :], ALU.add).then_inc(sig["rss_ok"], 1)
                    dve.wait_ge(sig["nh_done"], 2 * i + (KT + p + 1))
                    dve.tensor_tensor(xn_l[:, 2 * i + p, :], rsg[p][:, :], xn_h[:, 2 * i + p, :].bitcast(F32), ALU.subtract)\
                        .then_inc(sig["nl_done"], 1)
            token_row(1)

            def f_low(n, q):
                dve.wait_ge(sig["f_h"], n + 1)
                dve.scalar_tensor_tensor(out=ff_l[:, n, :], in0=hv[q][:, :], scalar=0.5, in1=ff_h[:, n, :].bitcast(F32),
                                         op0=ALU.mult, op1=ALU.subtract).then_inc(sig["f_l"], 1)

            def hidden(n, q):
                dve.wait_ge(sig["f_sg"], n + 1)
                dve.wait_ge(sig["fy_ok"], 2 * n + 3)
                dve.wait_ge(sig["f_l"], n + 1)
                dve.tensor_tensor(hv[q][:, :], yc[2 * q][:, :], yc[2 * q + 1][:, :], ALU.mult).then_inc(sig["f_hv"], 1)

            def v_up(i, first):
                for p in range(4):
                    b, q, u = p % 2, p // 2, 4 * i + p
                    after_pair = b == 0 and (p or not first)
                    lo(U_UP + 2, 4, i, p, KT, 0)
                    if after_pair:
                        hidden(2 * i + (q - 1), 1 - q)
                    done(U_UP, 4, i, p)
                    dve.tensor_tensor(yr[b][:, :], acc[b][:, :], rms_row[:, :], ALU.mult).then_inc(acc_free[b], 1)
                    evacuated(dve, U_UP, 4, i, p)
                    lo(U_UP + 2, 4, i, p, KT, 1)
                    if after_pair:
                        f_low(2 * i + (q - 1), 1 - q)
                    if b:
                        dve.wait_ge(sig["fth_ok"], 2 * i + q + 1)
                        dve.scalar_tensor_tensor(out=yc[p - 1][:, :], in0=yt[q][:, :], scalar=1.0, in1=yc[p - 1][:, :],
                                                 op0=ALU.add, op1=ALU.mult).then_inc(sig["f_sg"], 1)
                    dve.wait_ge(sig["fy_tap"], u + 1)
                    add_tap(yc[p], yr[b], tapf[:, p, 1:2], 1).then_inc(sig["fc1_ok"], 1)
                    dve.wait_ge(sig["fc1_ok"], u + 1)
                    add_tap(yc[p], yr[b], tapf[:, p, 0:1], 2).then_inc(sig["fy_ok"], 1)

            v_up(0, True)
            with dve.Fori(1, KF // 2) as i:
                v_up(i, False)
            hidden(KF - 1, 1)
            f_low(KF - 1, 1)

            dve.memset(sqsum[:, :], 0.0).then_inc(sig["rss_ok"], 1)

            def v_down(i, last):
                for p in range(6):
                    if not (last and p >= 4):
                        lo(U_DN + 2, 6, i, p, KDN[(p + 2) % 3], 0)
                        lo(U_DN + 2, 6, i, p, KDN[(p + 2) % 3], 1)
                    if p % 3 == 2:
                        m, b = 2 * i + p // 3, p // 3
                        done(U_DN, 6, i, p)
                        dve.tensor_tensor(res[:, m, :], res[:, m, :], acc[b][:, :], ALU.add).then_inc(acc_free[b], 1)
                        dve.wait_ge(sig["rsq_ok"], m + KT + 1)
                        dve.tensor_tensor(sqsum[:, :], sqsum[:, :], sq2[:, :], ALU.add).then_inc(sig["rss_ok"], 1)

            with dve.Fori(0, KT // 2 - 1) as i:
                v_down(i, False)
            v_down(KT // 2 - 1, True)

            dve.wait_ge(sig["rstat_mm"], 3)
            token_factors()
            dve.wait_ge(sig["rown_mm"], 3)
            for k in range(KT):
                g0 = PRM["gf"].start + k
                dve.scalar_tensor_tensor(out=res[:, k, :], in0=res[:, k, :], scalar=prm[:, g0:g0 + 1], in1=fb[1][:, :],
                                         op0=ALU.mult, op1=ALU.mult).then_inc(sig["out_ok"], 1)


def kernel(x, norm1_g, w_in, conv_qkv, a_log, dt_bias, gdn_norm, w_br_a, conv_sc, w_br_b, fox_bias, w_br_c, w_o,
           norm2_g, w_up, conv_ffn, w_down, norm_f):
    import numpy as np
    import concourse.bacc as bacc
    from concourse import mybir
    from concourse.bass_utils import run_bass_kernel_spmd

    def blocks(w, kt):
        n = w.shape[1] // P
        return w.reshape(kt, P, n, P).transpose(2, 1, 0, 3).reshape(n, P, kt * P)

    def columns(v):
        return v.reshape(-1, P).T

    def tap_columns(v, kinds):
        taps = v.shape[0]
        return v.reshape(taps, kinds, -1, P).transpose(3, 2, 1, 0).reshape(P, -1)

    w_in = w_in[0]
    W = H * HD
    at = [0]

    def take(n):
        at[0] += n
        return w_in[:, at[0] - n:at[0]]

    qkv_a, z_a, beta, alog, bch, qkv_c, flog, gates = (
        take(3 * W), take(W), take(H), take(H), take(3 * W), take(3 * W), take(H), take(3 * D))

    def part(a, j, n):
        return a[:, j * n:(j + 1) * n]

    mix = [blocks(part(qkv_c, 0, W), KT), blocks(part(qkv_c, 1, W), KT), blocks(part(qkv_c, 2, W), KT),
           blocks(part(bch, 1, W), KT), blocks(part(bch, 2, W), KT), blocks(part(bch, 0, W), KT)]
    idx = np.arange(P)
    row, colm = idx[:, None], idx[None, :]
    consts = np.zeros((P, NCONST, P), np.float32)
    consts[:, C_ID] = row == colm
    consts[:, C_ONE] = 1.0
    consts[:, C_TRI] = row <= colm
    consts[:, C_NEGT] = np.where(colm >= row, 0.0, NEG)
    consts[:, C_CAUSAL] = np.where(colm <= row, 0.0, NEG)
    for lev in range(NLEV):
        b = 1 << lev
        consts[:, C_LEV + lev] = (row // (2 * b) == colm // (2 * b)) & (row % (2 * b) < b) & (colm % (2 * b) >= b)

    def everywhere(v):
        return np.broadcast_to(v, (P, v.shape[-1]))

    params = np.concatenate([
        columns(norm1_g[0]), columns(norm2_g[0]), columns(norm_f), tap_columns(conv_qkv[0], 1),
        tap_columns(conv_sc[0], 1), tap_columns(conv_ffn[0], 2), columns(gdn_norm[0]),
        everywhere(a_log), everywhere(dt_bias), everywhere(fox_bias)], axis=1)
    w_small = np.concatenate([beta, alog, flog], axis=1).reshape(KT, P, 12).transpose(1, 0, 2).reshape(P, KT * 12)
    arrays = {
        "xT": x[0].T,
        "consts": consts.reshape(P, NCONST * P),
        "params": params,
        "w_small": w_small,
        "w_qkv": blocks(qkv_a, KT),
        "w_mix": np.stack(mix, axis=1).reshape(6 * H, P, KT * P),
        "w_z": blocks(z_a, KT),
        "w_gate": np.stack([blocks(part(gates, j, D), KT) for j in range(3)], axis=1).reshape(3 * KT, P, KT * P),
        "w_br": np.stack([blocks(w[0], H) for w in (w_br_a, w_br_b, w_br_c)], axis=1).reshape(3 * KT, P, H * P),
        "w_o": blocks(w_o[0], KT),
        "w_up": np.stack([blocks(part(w_up[0], j, FF), KT) for j in range(2)], axis=1).reshape(2 * KF, P, KT * P),
        "w_dn": blocks(w_down[0], KF),
    }
    arrays = {n: np.ascontiguousarray(a) for n, a in arrays.items()}
    nc = bacc.Bacc("TRN2", target_bir_lowering=False, num_devices=1)
    args = [nc.dram_tensor(n, a.shape, mybir.dt.from_np(a.dtype), kind="ExternalInput").ap() for n, a in arrays.items()]
    outT = nc.dram_tensor("outT", (D, T), mybir.dt.float32, kind="ExternalOutput").ap()
    build(nc, *args, outT)
    r = run_bass_kernel_spmd(nc, [arrays], core_ids=[0])
    return np.ascontiguousarray(r.results[0]["outT"].T)[None]
```
